# Optimizing a Trainium2 kernel written in Bass

```python
import math
import jax, jax.numpy as jnp
from jax import lax
import numpy as np

D_MODEL = 1024
BATCH = 1
SEQ = 512
DEPTH = 1
DEC_BATCH = 8
DEC_SEQ = 1
PAST_LEN = 4096
PAGE_SIZE = 128

D_RNN = D_MODEL
RG_BLOCKS = 8
RG_BW = D_RNN // RG_BLOCKS
CONV_W = 4
RG_C = 8.0
M_HEADS = 4
M_DK = D_MODEL // M_HEADS
M_DV = D_MODEL // M_HEADS
D_M = M_HEADS * M_DV
MLSTM_CHUNK = 128
D_FF = ((8 * D_MODEL // 3) + 255) // 256 * 256
N_MOD = 9
N_IN = D_RNN + 2 * M_HEADS * M_DK + 2 * D_M + 2 * M_HEADS + 2 * D_MODEL
EPS = 1e-6

kernel_name = 'griffin_mlstm_macaron_adaln_step'

def _rms(x, gain):
    x32 = x.astype(jnp.float32)
    return x32 * lax.rsqrt(jnp.mean(x32 * x32, axis=-1, keepdims=True) + EPS) * gain.astype(jnp.float32)

def _rms_mod(x, gain, shift, scale):
    return (_rms(x, gain) * (1.0 + scale) + shift).astype(x.dtype)

def _swiglu(x, w_in, w_out):
    g, u = jnp.split(x @ w_in, 2, axis=-1)
    return (jax.nn.silu(g) * u) @ w_out

def _lin_comb(left, right):
    a1, b1 = left
    a2, b2 = right
    return a1 * a2, a2 * b1 + b2

def _rglru(x_rg, conv_buf, h0, conv_w, conv_b, w_a, b_a, w_i, b_i, lam):
    f32 = jnp.float32
    bsz, L, _ = x_rg.shape
    xc = jnp.concatenate([conv_buf.astype(x_rg.dtype), x_rg], axis=1)
    new_buf = xc[:, L:]
    u = conv_b.astype(f32)
    for j in range(CONV_W):
        u = u + xc[:, j:j + L].astype(f32) * conv_w[j].astype(f32)
    ub = u.reshape(bsz, L, RG_BLOCKS, RG_BW)
    r = jax.nn.sigmoid(jnp.einsum('blnc,ncd->blnd', ub, w_a.astype(f32)).reshape(bsz, L, D_RNN) + b_a.astype(f32))
    i_g = jax.nn.sigmoid(jnp.einsum('blnc,ncd->blnd', ub, w_i.astype(f32)).reshape(bsz, L, D_RNN) + b_i.astype(f32))
    log_a = -RG_C * r * jax.nn.softplus(-lam.astype(f32))
    a = jnp.exp(log_a)
    b = jnp.sqrt(-jnp.expm1(2.0 * log_a)) * (i_g * u)
    b = b.at[:, 0].add(a[:, 0] * h0.astype(f32))
    _, h = lax.associative_scan(_lin_comb, (a, b), axis=1)
    return h, new_buf, h[:, -1]

def _mlstm(q, k, v, ig, lf, C0, n0, m0):
    f32 = jnp.float32
    bsz, L = q.shape[:2]
    cs = MLSTM_CHUNK if L % MLSTM_CHUNK == 0 else L
    nc = L // cs

    def to_chunks(t):
        t = t.reshape((bsz, nc, cs) + t.shape[2:])
        return t.transpose((1, 0, 3, 2) + tuple(range(4, t.ndim)))

    mask = jnp.tril(jnp.ones((cs, cs), dtype=bool))
    scale = M_DK ** -0.5

    def step(carry, inp):
        C, n, m = carry
        qc, kc, vc, ic, lfc = inp
        bcum = jnp.cumsum(lfc, axis=-1)
        log_d = jnp.where(mask, bcum[..., :, None] - bcum[..., None, :] + ic[..., None, :], -jnp.inf)
        log_past = bcum + m[..., None]
        m_t = jnp.maximum(log_past, jnp.max(log_d, axis=-1))
        d_mat = jnp.exp(log_d - m_t[..., None])
        past_w = jnp.exp(log_past - m_t)
        qs = qc * scale
        s = jnp.einsum('bhtd,bhsd->bhts', qs, kc) * d_mat
        num = past_w[..., None] * jnp.einsum('bhtd,bhde->bhte', qs, C) + jnp.einsum('bhts,bhse->bhte', s, vc)
        den = past_w * jnp.einsum('bhtd,bhd->bht', qs, n) + jnp.sum(s, axis=-1)
        h = num / jnp.maximum(jnp.abs(den), jnp.exp(-m_t))[..., None]
        m_new = m_t[..., -1]
        w_s = jnp.exp(bcum[..., -1:] - bcum + ic - m_new[..., None])
        decay = jnp.exp(bcum[..., -1] + m - m_new)
        C_new = decay[..., None, None] * C + jnp.einsum('bhs,bhsd,bhse->bhde', w_s, kc, vc)
        n_new = decay[..., None] * n + jnp.einsum('bhs,bhsd->bhd', w_s, kc)
        return (C_new, n_new, m_new), h

    carry0 = (C0.astype(f32), n0.astype(f32), m0.astype(f32))
    (C1, n1, m1), h = lax.scan(step, carry0, (to_chunks(q), to_chunks(k), to_chunks(v), to_chunks(ig), to_chunks(lf)))
    h = h.transpose(1, 0, 3, 2, 4).reshape(bsz, L, M_HEADS * M_DV)
    return h, C1, n1, m1

def _mixer(xn, conv_buf, h0, C0, n0, m0, w_in, conv_w, conv_b, w_rg_a, b_rg_a, w_rg_i, b_rg_i,
           rg_lambda, b_ig, b_fg, w_br_a, w_br_b, w_out):
    f32 = jnp.float32
    dt = xn.dtype
    bsz, L, _ = xn.shape
    sizes = [D_RNN, M_HEADS * M_DK, M_HEADS * M_DK, D_M, D_M, M_HEADS, M_HEADS, D_MODEL, D_MODEL]
    x_rg, q, k, v, o_pre, i_pre, f_pre, g_a, g_b = jnp.split(xn @ w_in, np.cumsum(sizes)[:-1].tolist(), axis=-1)
    h_a, new_buf, h_last = _rglru(x_rg, conv_buf, h0, conv_w, conv_b, w_rg_a, b_rg_a, w_rg_i, b_rg_i, rg_lambda)
    q = q.astype(f32).reshape(bsz, L, M_HEADS, M_DK)
    k = k.astype(f32).reshape(bsz, L, M_HEADS, M_DK)
    v = v.astype(f32).reshape(bsz, L, M_HEADS, M_DV)
    ig = i_pre.astype(f32) + b_ig.astype(f32)
    lf = jax.nn.log_sigmoid(f_pre.astype(f32) + b_fg.astype(f32))
    h_m, C1, n1, m1 = _mlstm(q, k, v, ig, lf, C0, n0, m0)
    h_b = jax.nn.sigmoid(o_pre.astype(f32)) * h_m
    merged = (jax.nn.sigmoid(g_a.astype(f32)) * (h_a.astype(dt) @ w_br_a)
              + jax.nn.sigmoid(g_b.astype(f32)) * (h_b.astype(dt) @ w_br_b))
    return merged.astype(dt) @ w_out, (new_buf, h_last, C1, n1, m1)

def _layer(x, c, lw, st):
    (w_ada, b_ada, g1, wf1i, wf1o, g2, w_in, conv_w, conv_b, w_rg_a, b_rg_a, w_rg_i, b_rg_i,
     rg_lambda, b_ig, b_fg, w_br_a, w_br_b, w_out, g3, wf2i, wf2o) = lw
    conv_buf, h0, C0, n0, m0 = st
    bsz = x.shape[0]
    mod = (jax.nn.silu(c.astype(jnp.float32)) @ w_ada.astype(jnp.float32) + b_ada.astype(jnp.float32))
    mod = mod.reshape(bsz, N_MOD, 1, D_MODEL)
    sh1, sc1, ga1, sh2, sc2, ga2, sh3, sc3, ga3 = [mod[:, j] for j in range(N_MOD)]
    x = x + (0.5 * ga1 * _swiglu(_rms_mod(x, g1, sh1, sc1), wf1i, wf1o)).astype(x.dtype)
    h, new_st = _mixer(_rms_mod(x, g2, sh2, sc2), conv_buf, h0, C0, n0, m0, w_in, conv_w, conv_b,
                       w_rg_a, b_rg_a, w_rg_i, b_rg_i, rg_lambda, b_ig, b_fg, w_br_a, w_br_b, w_out)
    x = x + (ga2 * h).astype(x.dtype)
    x = x + (0.5 * ga3 * _swiglu(_rms_mod(x, g3, sh3, sc3), wf2i, wf2o)).astype(x.dtype)
    return x, new_st

def setup_inputs(seed: int = 0) -> dict:
    key = jax.random.key(seed)
    ks = jax.random.split(key, 40)
    f32 = jnp.float32

    def nrm(k, shape, s):
        return jax.random.normal(k, shape, f32) * s

    a_init = jax.random.uniform(ks[20], (DEPTH, D_RNN), f32, minval=0.9, maxval=0.999)
    a_root = a_init ** (1.0 / RG_C)
    rg_lambda = jnp.log(a_root) - jnp.log1p(-a_root)
    return {
        'x_prompt': nrm(ks[0], (BATCH, SEQ, D_MODEL), 1.0),
        'x_sample': nrm(ks[1], (DEC_BATCH, DEC_SEQ, D_MODEL), 1.0),
        'state_conv': nrm(ks[2], (DEPTH, DEC_BATCH, CONV_W - 1, D_RNN), 1.0),
        'state_rg_h': nrm(ks[3], (DEPTH, DEC_BATCH, D_RNN), 0.5),
        'state_C': nrm(ks[4], (DEPTH, DEC_BATCH, M_HEADS, M_DK, M_DV), 0.1),
        'state_n': nrm(ks[5], (DEPTH, DEC_BATCH, M_HEADS, M_DK), 0.1),
        'state_m': nrm(ks[6], (DEPTH, DEC_BATCH, M_HEADS), 1.0),
        'c_prompt': nrm(ks[7], (BATCH, D_MODEL), 1.0),
        'c_sample': nrm(ks[8], (DEC_BATCH, D_MODEL), 1.0),
        'w_ada': nrm(ks[9], (DEPTH, D_MODEL, N_MOD * D_MODEL), 0.5 * D_MODEL ** -0.5),
        'b_ada': nrm(ks[10], (DEPTH, N_MOD * D_MODEL), 0.02),
        'g_norm1': 1.0 + nrm(ks[11], (DEPTH, D_MODEL), 0.05),
        'w_ff1_in': nrm(ks[12], (DEPTH, D_MODEL, 2 * D_FF), D_MODEL ** -0.5),
        'w_ff1_out': nrm(ks[13], (DEPTH, D_FF, D_MODEL), D_FF ** -0.5),
        'g_norm2': 1.0 + nrm(ks[14], (DEPTH, D_MODEL), 0.05),
        'w_in': nrm(ks[15], (DEPTH, D_MODEL, N_IN), D_MODEL ** -0.5),
        'conv_w': nrm(ks[16], (DEPTH, CONV_W, D_RNN), CONV_W ** -0.5),
        'conv_b': nrm(ks[17], (DEPTH, D_RNN), 0.02),
        'w_rg_a': nrm(ks[18], (DEPTH, RG_BLOCKS, RG_BW, RG_BW), RG_BW ** -0.5),
        'b_rg_a': nrm(ks[19], (DEPTH, D_RNN), 0.02),
        'w_rg_i': nrm(ks[21], (DEPTH, RG_BLOCKS, RG_BW, RG_BW), RG_BW ** -0.5),
        'b_rg_i': nrm(ks[22], (DEPTH, D_RNN), 0.02),
        'rg_lambda': rg_lambda,
        'b_ig': nrm(ks[23], (DEPTH, M_HEADS), 0.1),
        'b_fg': 3.0 + nrm(ks[24], (DEPTH, M_HEADS), 0.5),
        'w_br_a': nrm(ks[25], (DEPTH, D_RNN, D_MODEL), D_RNN ** -0.5),
        'w_br_b': nrm(ks[26], (DEPTH, D_M, D_MODEL), D_M ** -0.5),
        'w_out': nrm(ks[27], (DEPTH, D_MODEL, D_MODEL), D_MODEL ** -0.5),
        'g_norm3': 1.0 + nrm(ks[28], (DEPTH, D_MODEL), 0.05),
        'w_ff2_in': nrm(ks[29], (DEPTH, D_MODEL, 2 * D_FF), D_MODEL ** -0.5),
        'w_ff2_out': nrm(ks[30], (DEPTH, D_FF, D_MODEL), D_FF ** -0.5),
        'g_final': 1.0 + nrm(ks[31], (D_MODEL,), 0.05),
    }

def reference(x_prompt, x_sample, state_conv, state_rg_h, state_C, state_n, state_m, c_prompt, c_sample,
              w_ada, b_ada, g_norm1, w_ff1_in, w_ff1_out, g_norm2, w_in, conv_w, conv_b, w_rg_a, b_rg_a,
              w_rg_i, b_rg_i, rg_lambda, b_ig, b_fg, w_br_a, w_br_b, w_out, g_norm3, w_ff2_in, w_ff2_out,
              g_final):
    f32 = jnp.float32
    bp = x_prompt.shape[0]
    zero_st = (jnp.zeros((bp, CONV_W - 1, D_RNN), x_prompt.dtype), jnp.zeros((bp, D_RNN), f32),
               jnp.zeros((bp, M_HEADS, M_DK, M_DV), f32), jnp.zeros((bp, M_HEADS, M_DK), f32),
               jnp.zeros((bp, M_HEADS), f32))
    yp, ys = x_prompt, x_sample
    sts_p, sts_s = [], []
    for l in range(DEPTH):
        lw = (w_ada[l], b_ada[l], g_norm1[l], w_ff1_in[l], w_ff1_out[l], g_norm2[l], w_in[l], conv_w[l],
              conv_b[l], w_rg_a[l], b_rg_a[l], w_rg_i[l], b_rg_i[l], rg_lambda[l], b_ig[l], b_fg[l],
              w_br_a[l], w_br_b[l], w_out[l], g_norm3[l], w_ff2_in[l], w_ff2_out[l])
        yp, sp = _layer(yp, c_prompt, lw, zero_st)
        ys, ss = _layer(ys, c_sample, lw, (state_conv[l], state_rg_h[l], state_C[l], state_n[l], state_m[l]))
        sts_p.append(sp)
        sts_s.append(ss)
    conv_p, h_p, C_p, n_p, m_p = [jnp.stack([s[j] for s in sts_p]) for j in range(5)]
    conv_s, h_s, C_s, n_s, m_s = [jnp.stack([s[j] for s in sts_s]) for j in range(5)]
    yp = _rms(yp, g_final).astype(x_prompt.dtype)
    ys = _rms(ys, g_final).astype(x_sample.dtype)
    return (yp, ys, conv_p, h_p, C_p, n_p, m_p, conv_s, h_s, C_s, n_s, m_s)


_drawn_inputs = setup_inputs


def setup_inputs(seed=0):
    import zlib

    import numpy as np

    out = dict(_drawn_inputs(seed))
    spreads = {}
    factors = {'g_norm1': 4.413, 'b_rg_a': 8.0, 'b_rg_i': 6.892, 'g_norm3': 7.184}
    for name, (base, spread) in spreads.items():
        noise = np.random.default_rng([zlib.crc32(name.encode()), seed]).standard_normal(out[name].shape)
        drawn = base * np.exp(spread * noise) if base else spread * noise
        out[name] = __import__('jax').numpy.asarray(drawn.astype(out[name].dtype))
    for name, factor in factors.items():
        out[name] = (out[name] * factor).astype(out[name].dtype)
    return out
```

```python
from contextlib import ExitStack

import numpy as np

import concourse.bass as bass
from concourse import mybir
from concourse.alu_op_type import AluOpType as ALU

F32 = mybir.dt.float32
F32R = mybir.dt.float32r
ACT = mybir.ActivationFunctionType

P = 128
D = 1024
KT = D // P
NP_ = 512
NB = 8
T = NP_ + NB
HALF = T // 2
D_FF = 2816
FT = D_FF // P
HEADS = 4
DT = 2
HD = DT * P
CH = NP_ // P
CONV_W = 4
NMOD = 9
EPS = 1e-6
QSCALE = HD ** -0.5
NEG = -1e30

RING = 3
LEAD = 2
BANKS = 4

ADA_FIRST = 16
FFI_LOOPS, FFI_BODY = 7, 6
FFO_CHUNKS = ((0, 8), (8, 8), (16, 6))

(SH1, SC1, GA1, SH2, SC2, GA2, SH3, SC3, GA3) = range(NMOD)
(V_G1, V_G2, V_G3, V_GF, V_CB, V_BA, V_BI, V_LAM, NVEC) = range(9)

MIX = [("gates", 0)]
for _p, _key in enumerate([("q", 0), ("q", 1), ("k", 0), ("k", 1)]):
    MIX += [("xrg", 2 * _p), ("xrg", 2 * _p + 1), _key]
for _j in range(KT):
    MIX += [("ga", _j), ("bra", _j)]
MIX += [("v", 0), ("v", 1)]
EARLY = 4
for _h in range(HEADS):
    if _h + 1 < HEADS:
        for _w in "qkv":
            MIX += [(_w, DT * (_h + 1)), (_w, DT * (_h + 1) + 1)]
    else:
        MIX += [("gb", _j) for _j in range(EARLY)]
    MIX += [("o", DT * _h), ("o", DT * _h + 1)]
MIX.remove(("o", DT * (HEADS - 2)))
MIX.remove(("o", DT * (HEADS - 2) + 1))
_at = MIX.index(("gb", 0))
MIX[_at:_at] = [("o", DT * (HEADS - 2)), ("o", DT * (HEADS - 2) + 1)]
for _j in range(KT):
    MIX += [("gb", _j)] * (_j >= EARLY) + [("brb", _j)]
MIX += [("out", _j) for _j in range(KT)]
NMIX = len(MIX)

C_FFI1 = 0
C_FFO1 = C_FFI1 + 2 * FT
C_MIX = C_FFO1 + 3 * KT
C_FFI2 = C_MIX + NMIX
C_FFO2 = C_FFI2 + 2 * FT
C_END = C_FFO2 + 3 * KT
T_FFI1 = 0
T_FFO1 = T_FFI1 + 2 * FT
T_MIX = T_FFO1 + KT
T_FFI2 = T_MIX + NMIX
T_FFO2 = T_FFI2 + 2 * FT
T_OF = {key: T_MIX + i for i, key in enumerate(MIX)}
C_OF = {key: C_MIX + i for i, key in enumerate(MIX)}


def head_jobs(h):
    return [
        [("kT", h, 0), ("kT", h, 1), ("Bt", h, 0)],
        [("vT", h, 0), ("vT", h, 1)],
        [("sm", h, 0), ("V", h, 0), ("V", h, 1)],
        [("S", h, c) for c in range(CH)],
        [("em", h, 0), ("den", h, 0), ("num", h, 0), ("num", h, 1)],
        [("sm", h, 1), ("V", h, 2), ("V", h, 3), ("C", h, 0), ("C", h, 1)],
    ]


AFTER = {i: [] for i in range(-1, NMIX)}
RG_AT = {}
for _j in range(0, KT, 2):
    _at = MIX.index(("xrg", _j + 1)) + 1
    RG_AT[_at] = (_j, _j + 1)
    for _jj in (_j, _j + 1):
        AFTER[_at] += [("rga", _jj, 0), ("rga", _jj, 1), ("rgi", _jj, 0), ("rgi", _jj, 1)]
AFTER[MIX.index(("ga", 3))] += [("aT", 0, 0), ("srow", 0, 0)]
for _h in range(HEADS):
    _groups = head_jobs(_h)
    if _h + 1 < HEADS:
        _places = [MIX.index((w, DT * (_h + 1) + i)) for w in "qkv" for i in range(2)]
    else:
        _places = [MIX.index(("o", DT * _h - 2)), MIX.index(("o", DT * _h - 1))]
        _places += [MIX.index(("gb", j)) for j in range(EARLY)]
    for _p, _g in zip(_places, _groups):
        AFTER[_p] += _g

M_ADA0 = 0
M_NORM1 = M_ADA0 + ADA_FIRST // 2
M_ADA1 = M_NORM1 + 2
M_NORM2 = M_ADA1 + FFI_LOOPS * 4
M_MIX = M_NORM2 + 2
JOB = {}
for _i in range(-1, NMIX):
    for _key in AFTER[_i]:
        JOB[_key] = M_MIX + len(JOB)
M_NORM3 = M_MIX + len(JOB)
M_NORM4 = M_NORM3 + 2

S_XN1 = 0
S_HID1 = S_XN1 + 1 + KT
S_XN2 = S_HID1 + FT
S_HA = S_XN2 + 1 + KT
S_HB = S_HA + KT
S_MG = S_HB + KT
S_XN3 = S_MG + KT
S_HID2 = S_XN3 + 1 + KT


def sources(s):
    return s - FT * (s >= S_XN2) - FT * (s > S_HID2)


def build(nc, xT, cT, w_ada, b_ada, ff1_in, ff1_out, w_mix, ff2_in, ff2_out, vecs, conv_w, w_rg,
          gate_b, st_conv, st_h, st_C, st_n, st_m,
          yT, o_convp, o_convs, o_h, o_Cp, o_Cs, o_ns, o_m):
    ctx = ExitStack()
    with ctx:
        def sb(name, shape, dt=F32, stack=ctx):
            return stack.enter_context(nc.sbuf_tensor(name, shape, dt))

        def sem(name):
            return ctx.enter_context(nc.semaphore(name))

        x = sb("x", [P, KT, T])
        xn_h = sb("xn_h", [P, KT, T], F32R)
        xn_l = sb("xn_l", [P, KT, T], F32R)
        raw = sb("raw", [P, RING, KT * P])
        w_h = [sb(f"w_h{i}", [P, KT * P], F32R) for i in range(RING)]
        w_l = [sb(f"w_l{i}", [P, KT * P], F32R) for i in range(RING)]
        ada = sb("ada", [P, 2, KT * P])
        cs = sb("cs", [P, KT, NB + 1])
        mod = sb("mod", [P, NMOD * KT, NB + 1])
        badat = sb("badat", [P, NMOD * KT])
        gain = sb("gain", [P, KT, NB + 1])
        vec = sb("vec", [P, NVEC, KT])
        cw = sb("cw", [P, KT, CONV_W])
        gb_t = sb("gb_t", [P, 1])
        eps_t = sb("eps_t", [P, 1])
        ident = sb("ident", [P, P])
        ones = sb("ones", [P, P])
        maskneg = sb("maskneg", [P, P])
        sel = sb("sel", [HEADS, HEADS, P])
        tb = [sb(f"tb{i}", [P, T]) for i in range(4)]
        ssq = sb("ssq", [P, T])
        rstd = ssq
        ys = sb("ys", [P, KT, NB])
        tmp8 = sb("tmp8", [P, NB])
        aT = sb("aT", [P, CH, HEADS])
        rs = sb("rs", [HEADS, 3, NB])
        rsb = sb("rsb", [P, HEADS, 3, NB])
        stn = sb("stn", [P, HEADS, DT, NB])
        stm = sb("stm", [HEADS, NB])
        hid_stack = ExitStack()
        hid_h = sb("hid_h", [P, FT, T], F32R, hid_stack)
        hid_l = sb("hid_l", [P, FT, T], F32R, hid_stack)
        hid_stack.close()
        pre_stack = ExitStack()
        ada_pre = sb("ada_pre", [P, ADA_FIRST, KT * P], F32, pre_stack)
        pre_stack.close()
        mix_stack = ExitStack()
        ma = sb("ma", [P, KT, T], F32, mix_stack)
        hb_h = sb("hb_h", [P, KT, T], F32R, mix_stack)
        hb_l = sb("hb_l", [P, KT, T], F32R, mix_stack)
        row_i = sb("row_i", [HEADS, T], F32, mix_stack)
        row_f = sb("row_f", [HEADS, T], F32, mix_stack)
        row_m = sb("row_m", [HEADS, T], F32, mix_stack)
        heads_stack = ExitStack()
        q_0 = sb("q_0", [P, DT, T], F32, heads_stack)
        k_0 = sb("k_0", [P, DT, T], F32, heads_stack)
        rg_stack = ExitStack()
        rg_u = [sb(f"rg_u{i}", [P, T], F32, rg_stack) for i in range(2)]
        rg_x = [sb(f"rg_x{i}", [P, CONV_W - 1 + T], F32, rg_stack) for i in range(2)]
        rg_r, rg_i, rg_a, rg_v = ([sb(f"rg_{n}{i}", [P, T], F32, rg_stack) for i in range(2)] for n in "riav")
        wrg = sb("wrg", [P, 2, KT, P], F32, rg_stack)
        stc = sb("stc", [P, KT, CONV_W - 1, NB], F32, rg_stack)
        sth = sb("sth", [P, KT, NB], F32, rg_stack)
        c8 = sb("c8", [P, 2, KT], F32, rg_stack)
        rg_stack.close()
        mg_stack = ExitStack()
        mg_h = sb("mg_h", [P, KT, T], F32R, mg_stack)
        mg_l = sb("mg_l", [P, KT, T], F32R, mg_stack)
        mg_stack.close()
        q_t = [q_0, sb("q_1", [P, DT, T], F32, heads_stack)]
        k_t = [k_0, sb("k_1", [P, DT, T], F32, heads_stack)]
        v_t = sb("v_t", [P, DT, T], F32, heads_stack)
        ktok = sb("ktok", [P, CH, HD], F32, heads_stack)
        vtok = sb("vtok", [P, CH, HD + 1], F32, heads_stack)
        dmat = sb("dmat", [P, CH, NP_], F32, heads_stack)
        hm = sb("hm", [P, DT, T], F32, heads_stack)
        sm = sb("sm", [P, 3, DT, NB], F32, heads_stack)
        prod = sb("prod", [P, 2, DT, NB], F32, heads_stack)
        kd = sb("kd", [P, DT, NB], F32, heads_stack)
        sres = sb("sres", [P, 4, NB], F32, heads_stack)
        s8 = sb("s8", [P, 4, NB], F32, heads_stack)
        wcol = sb("wcol", [P, CH], F32, heads_stack)
        sgb = [(q_0, k_0)[j // 2][:, j % 2, :] for j in range(EARLY)]
        heads_stack.close()
        mix_stack.close()
        n_cs, n_ho = KT * (CONV_W - 1) * NB, KT * (NB + 1)
        convs = ssq[:, 0:n_cs].rearrange("p (k j b) -> p k j b", k=KT, j=CONV_W - 1)
        hout = ssq[:, n_cs:n_cs + n_ho].rearrange("p (k n) -> p k n", k=KT)
        convp = ssq[:, n_cs + n_ho:n_cs + n_ho + KT * (CONV_W - 1)].rearrange("p (k j) -> p k j", k=KT)
        sp = ssq[:, T - 4 * KT:T].rearrange("p (a k) -> p a k", a=4)
        cst = tb[1][:, 0:DT * (HD + 1)].rearrange("p (d e) -> p d e", d=DT)
        cst_c = ada[:, :, :].rearrange("p a (b d e) -> p (a b) d e", b=2, d=DT)

        big = [ctx.enter_context(nc.psum_tensor(f"big{i}", [P, 2, 512], F32)) for i in range(2)]
        bank = [ctx.enter_context(nc.psum_tensor(f"bank{i}", [P, 512], F32)) for i in range(BANKS)]

        def two(ap):
            return ap.rearrange("p (h n) -> p h n", h=2)

        def slot_view(t):
            return big[t % 2][:, :, 0:HALF]

        raw_in = [sem(f"raw_in{i}") for i in range(RING)]
        w_hi_ready = sem("w_hi_ready")
        w_lo_ready = sem("w_lo_ready")
        chunk_done = sem("chunk_done")
        evac = [sem(f"evac{i}") for i in range(2)]
        job_done = sem("job_done")
        taken = [sem(f"taken{i}") for i in range(BANKS)]
        src_ready = sem("src_ready")
        hi_ready = sem("hi_ready")
        lo_ready = sem("lo_ready")
        pre_in = [sem(f"pre_in{i}") for i in range(4)]
        ada_in = [sem(f"ada_in{i}") for i in range(2)]
        const_ready = sem("const_ready")
        sel0 = sem("sel0")
        x_in = sem("x_in")
        small_in = sem("small_in")
        cs_ready = sem("cs_ready")
        sq_ready = sem("sq_ready")
        ssq_ready = sem("ssq_ready")
        x_ready = sem("x_ready")
        std_ready = sem("std_ready")
        nrm_ready = sem("nrm_ready")
        nrm_used = sem("nrm_used")
        gain_ready = sem("gain_ready")
        rg_in = sem("rg_in")
        conv_done = sem("conv_done")
        rg_ra = sem("rg_ra")
        rg_w = sem("rg_w")
        rg_sq = sem("rg_sq")
        exp_sp = sem("exp_sp")
        sp_abs = sem("sp_abs")
        f_abs = sem("f_abs")
        f_exp = sem("f_exp")
        row_arg = sem("row_arg")
        row_exp = sem("row_exp")
        rows_ready = sem("rows_ready")
        diag_ready = sem("diag_ready")
        d_ready = sem("d_ready")
        prod_ready = sem("prod_ready")
        vw_ready = sem("vw_ready")
        hm_ready = sem("hm_ready")
        c_in = [sem(f"c_in{i}") for i in range(4)]
        c_scaled = sem("c_scaled")
        c_out = [sem(f"c_out{i}") for i in range(4)]
        cp_out = sem("cp_out")
        state_out = sem("state_out")
        states_ready = sem("states_ready")
        y_ready = sem("y_ready")
        y_out = [sem(f"y_out{i}") for i in range(2)]
        dch = sem("dch")
        ach = sem("ach")

        block = ctx.enter_context(nc.Block())

        def wait_evac(eng, t):
            eng.wait_ge(evac[t % 2], t // 2 + 1)

        def wait_taken(eng, m):
            eng.wait_ge(taken[m % BANKS], m // BANKS + 1)

        @block.sync
        def _(sp_):
            sp_.dma_start(x[:, 0:KT // 2, :], xT[:, 0:KT // 2, :]).then_inc(x_in, 16)
            sp_.dma_start(x[:, KT // 2:, :], xT[:, KT // 2:, :]).then_inc(x_in, 16)
            for n in range(4):
                tiles = slice(n * ADA_FIRST // 4, (n + 1) * ADA_FIRST // 4)
                sp_.dma_start(ada_pre[:, tiles, :], w_ada[tiles].rearrange("t p f -> p t f")).then_inc(pre_in[n], 16)

            def load(c_static, c_expr, src, width=KT * P):
                if not isinstance(c_expr, int) or c_expr >= RING:
                    sp_.wait_ge(w_lo_ready, c_expr - (RING - 1))
                sp_.dma_start(raw[:, c_static % RING, 0:width], src).then_inc(raw_in[c_static % RING], 16)

            def load_ffn(base, w_i, w_o):
                for k in range(FFI_BODY):
                    load(base + k, base + k, w_i[k])
                with sp_.Fori(1, FFI_LOOPS) as i:
                    for k in range(FFI_BODY):
                        load(base + k, i * FFI_BODY + (base + k), w_i[i * FFI_BODY + k])
                for k in range(FFI_LOOPS * FFI_BODY, 2 * FT):
                    load(base + k, base + k, w_i[k])
                base += 2 * FT
                with sp_.Fori(0, KT) as i:
                    for k, (k0, n) in enumerate(FFO_CHUNKS):
                        load(base + k, i * 3 + (base + k), w_o[i, :, k0 * P:(k0 + n) * P], n * P)

            load_ffn(C_FFI1, ff1_in, ff1_out)
            with sp_.Fori(0, NMIX // RING) as i:
                for k in range(RING):
                    load(C_MIX + k, i * RING + (C_MIX + k), w_mix[i * RING + k])
            for k in range(NMIX // RING * RING, NMIX):
                load(C_MIX + k, C_MIX + k, w_mix[k])
            load_ffn(C_FFI2, ff2_in, ff2_out)

        @block.gpsimd
        def _(pool):
            pool.dma_start(cs[:, :, :], cT).then_inc(small_in, 16)
            pool.dma_start(badat[:, :], b_ada).then_inc(small_in, 16)
            pool.dma_start(vec[:, :, :], vecs).then_inc(small_in, 16)
            for t in range(2):
                pool.dma_start(ada[:, t, :], w_ada[ADA_FIRST + t]).then_inc(ada_in[t], 16)
            nc.gpsimd.memset(ident[:, :], 0.0).then_inc(sel0, 1)
            nc.gpsimd.memset(maskneg[:, :], 0.0).then_inc(sel0, 1)
            nc.gpsimd.memset(sel[:, :, :], 0.0).then_inc(sel0, 1)
            pool.wait_ge(sel0, 3)
            nc.gpsimd.affine_select(out=ident[:, :], in_=ident[:, :], compare_op=ALU.not_equal, fill=1.0,
                                    base=0, pattern=[[-1, P]], channel_multiplier=1).then_inc(const_ready, 1)
            nc.gpsimd.affine_select(out=maskneg[:, :], in_=maskneg[:, :], compare_op=ALU.is_ge, fill=NEG,
                                    base=0, pattern=[[1, P]], channel_multiplier=-1).then_inc(const_ready, 1)
            nc.gpsimd.affine_select(out=sel[:, :, :], in_=sel[:, :, :], compare_op=ALU.not_equal, fill=1.0,
                                    base=0, pattern=[[-1, HEADS], [0, P]], channel_multiplier=1
                                    ).then_inc(const_ready, 1)
            nc.gpsimd.memset(ones[:, :], 1.0).then_inc(const_ready, 1)
            nc.gpsimd.memset(eps_t[:, :], EPS).then_inc(const_ready, 1)

            with pool.Fori(1, FFI_LOOPS * 4) as q:
                pool.wait_ge(job_done, q + M_ADA1)
                for t in range(2):
                    pool.dma_start(ada[:, t, :], w_ada[q * 2 + (ADA_FIRST + t)]).then_inc(ada_in[t], 16)

            pool.dma_start(cw[:, :, :], conv_w).then_inc(rg_in, 16)
            pool.dma_start(gb_t[:, :], gate_b).then_inc(rg_in, 16)
            pool.dma_start(stn[:, :, :, :], st_n).then_inc(rg_in, 16)
            pool.dma_start(stm[:, :], st_m).then_inc(rg_in, 16)
            pool.wait_ge(chunk_done, C_MIX)
            pool.dma_start(wrg[:, :, :, :], w_rg).then_inc(rg_in, 16)
            pool.dma_start(stc[:, :, :, :], st_conv).then_inc(rg_in, 16)
            pool.dma_start(sth[:, :, :], st_h).then_inc(rg_in, 16)

            def load_state(n):
                if n >= 4:
                    pool.wait_ge(c_out[n % 4], 16 * (n // 4))
                pool.dma_start(cst_c[:, n % 4, :, :], st_C[n].rearrange("p (d e) -> p d e", d=DT)
                               ).then_inc(c_in[n % 4], 16)

            def store_state(n):
                wait_taken(pool, JOB["V", n // NB, n % NB // 2])
                pool.dma_start(o_Cs[n].rearrange("p (d e) -> p d e", d=DT), cst_c[:, n % 4, :, :]
                               ).then_inc(c_out[n % 4], 16)

            for n in range(4):
                load_state(n)
            pool.wait_ge(lo_ready, S_HA + KT)
            pool.dma_start(o_convp, convp[:, :, :]).then_inc(state_out, 16)
            pool.dma_start(o_convs, convs[:, :, :, :]).then_inc(state_out, 16)
            pool.dma_start(o_h, hout[:, :, :]).then_inc(state_out, 16)
            for h in range(HEADS):
                for b in range(NB):
                    n = h * NB + b
                    store_state(n)
                    if n + 4 < HEADS * NB:
                        load_state(n + 4)
                for dt in range(DT):
                    wait_taken(pool, JOB["C", h, dt])
                    pool.dma_start(o_Cp[h, dt], cst[:, dt, :]).then_inc(cp_out, 16)
            pool.wait_ge(states_ready, HEADS)
            pool.dma_start(o_ns, stn[:, :, :, :]).then_inc(state_out, 16)
            pool.dma_start(o_m, row_m[:, NP_ - 1:T]).then_inc(state_out, 16)
            for kt in range(KT):
                pool.wait_ge(y_ready, kt + 1)
                pool.dma_start(yT[:, kt, :], tb[2 + kt % 2][:, :]).then_inc(y_out[kt % 2], 16)
            for i in range(2):
                pool.wait_ge(y_out[i], 16 * (KT // 2))
            pool.wait_ge(state_out, 16 * 5)
            pool.wait_ge(cp_out, 16 * HEADS * DT)
            for i in range(4):
                pool.wait_ge(c_out[i], 16 * (HEADS * NB // 4))

        @block.tensor
        def _(pe):
            def product(c, c_expr, t, t_half, xh, xl, k0, n, first=True, last=True, ready=None):
                pe.wait_ge(w_lo_ready, c_expr + 1)
                if first and not (isinstance(t_half, int) and t_half == 0):
                    pe.wait_ge(evac[t % 2], t_half)
                out = big[t % 2]
                wh, wl = w_h[c % RING], w_l[c % RING]
                for i in range(n):
                    if ready is not None:
                        pe.wait_ge(lo_ready, ready(k0 + i))
                    w = slice(i * P, (i + 1) * P)
                    for s, (a, b) in enumerate(((wh, xh), (wh, xl), (wl, xh))):
                        for hf in range(2):
                            ins = nc.tensor.matmul(out[:, hf, 0:HALF], a[:, w],
                                                   b[:, k0 + i, hf * HALF:(hf + 1) * HALF],
                                                   start=first and i == 0 and s == 0,
                                                   stop=last and i == n - 1 and s == 2)
                ins.then_inc(chunk_done, 1)

            def job(m):
                if m >= BANKS:
                    pe.wait_ge(taken[m % BANKS], m // BANKS)
                return bank[m % BANKS]

            def modulation(out, weights, q16=None):
                for t in range(2):
                    if q16 is not None:
                        pe.wait_ge(ada_in[t], q16)
                    for kt in range(KT):
                        ins = nc.tensor.matmul(out[:, t * (NB + 1):(t + 1) * (NB + 1)],
                                               weights[:, t, kt * P:(kt + 1) * P], cs[:, kt, :],
                                               start=kt == 0, stop=kt == KT - 1)
                ins.then_inc(job_done, 1)

            def norm_sums(m, ssq_count):
                pe.wait_ge(ssq_ready, ssq_count)
                for hf in range(2):
                    b = job(m + hf)
                    nc.tensor.matmul(b[:, 0:HALF], ones[:, :], ssq[:, hf * HALF:(hf + 1) * HALF],
                                     start=True, stop=True).then_inc(job_done, 1)

            def ffn(cb, tbase, s_xn, s_hid, with_ada):
                def xn_split(kt):
                    return s_xn + 2 + kt

                def turn(i):
                    for k in range(FFI_BODY):
                        product(cb + k, i * FFI_BODY + (cb + k), tbase + k,
                                i * (FFI_BODY // 2) + (tbase + k) // 2, xn_h, xn_l, 0, KT,
                                ready=xn_split if k == 0 else None)
                        if with_ada and k in (0, 1, 3, 4):
                            n = (0, 1, 3, 4).index(k)
                            m = M_ADA1 + n
                            pe.wait_ge(taken[m % BANKS], i + m // BANKS)
                            modulation(bank[m % BANKS], ada, i * (4 * 16) + 16 * (n + 1))

                first = 1 if cb == 0 else 0
                if first:
                    turn(0)
                with pe.Fori(first, FFI_LOOPS) as i:
                    turn(i)
                for k in range(FFI_LOOPS * FFI_BODY, 2 * FT):
                    product(cb + k, cb + k, tbase + k, (tbase + k) // 2, xn_h, xn_l, 0, KT)
                cb += 2 * FT
                tbase += 2 * FT
                pe.wait_ge(lo_ready, s_hid + FT - 1)
                with pe.Fori(0, KT // 2) as i:
                    for jj in range(2):
                        for k, (k0, n) in enumerate(FFO_CHUNKS):
                            product(cb + 3 * jj + k, i * 6 + (cb + 3 * jj + k), tbase + jj,
                                    i + (tbase + jj) // 2, hid_h, hid_l, k0, n, first=k == 0, last=k == 2,
                                    ready=(lambda kt: s_hid + FT) if k == 2 and jj == 0 else None)

            pe.wait_ge(const_ready, 5)
            pe.wait_ge(cs_ready, 1)
            for q in range(ADA_FIRST // 2):
                pe.wait_ge(pre_in[q // 2], 16)
                modulation(job(M_ADA0 + q), ada_pre[:, 2 * q:2 * q + 2, :])
            norm_sums(M_NORM1, KT)
            ffn(C_FFI1, T_FFI1, S_XN1, S_HID1, True)
            norm_sums(M_NORM2, 2 * KT)

            def small_job(key):
                kind, a, b = key
                m = JOB[key]
                out = job(m)
                h = a
                if kind in ("rga", "rgi"):
                    pe.wait_ge(rg_in, 16 * 7)
                    pe.wait_ge(conv_done, a + 1)
                    ins = nc.tensor.matmul(out[:, 0:HALF], wrg[:, 0 if kind == "rga" else 1, a, :],
                                           rg_u[a % 2][:, b * HALF:(b + 1) * HALF], start=True, stop=True)
                elif kind == "aT":
                    pe.wait_ge(rows_ready, 1)
                    for c in range(CH):
                        ins = nc.tensor.transpose(out[:, c * HEADS:(c + 1) * HEADS],
                                                  row_i[0:HEADS, c * P:(c + 1) * P], ident[0:HEADS, 0:HEADS])
                elif kind == "srow":
                    pe.wait_ge(row_exp, 1)
                    for hh in range(HEADS):
                        ins = nc.tensor.matmul(out[:, hh * 3 * NB:(hh + 1) * 3 * NB], sel[:, hh, :],
                                               rs[:, :, :].rearrange("h a b -> h (a b)"), start=True, stop=True)
                elif kind in ("kT", "vT"):
                    src = k_t[h % 2] if kind == "kT" else v_t
                    wait_evac(pe, T_OF[kind[0], DT * h + b])
                    for c in range(CH):
                        ins = nc.tensor.transpose(out[:, c * P:(c + 1) * P], src[:, b, c * P:(c + 1) * P],
                                                  ident[:, :])
                elif kind == "Bt":
                    ins = nc.tensor.matmul(out[:, 0:NP_], sel[:, h, :], row_f[:, 0:NP_], start=True, stop=True)
                elif kind == "em":
                    ins = nc.tensor.matmul(out[:, 0:NP_], sel[:, h, :], row_m[:, 0:NP_], start=True, stop=True)
                elif kind == "S":
                    for dt in range(DT):
                        ins = nc.tensor.matmul(out[:, b * P:NP_], k_t[h % 2][:, dt, b * P:(b + 1) * P],
                                               q_t[h % 2][:, dt, b * P:NP_], start=dt == 0, stop=dt == DT - 1)
                elif kind in ("den", "num"):
                    for c in range(CH):
                        wait_taken(pe, JOB["S", h, c])
                        if kind == "num":
                            wait_taken(pe, JOB["vT", h, b])
                        lhs = ones[:, :] if kind == "den" else vtok[:, c, b * P:(b + 1) * P]
                        ins = nc.tensor.matmul(out[:, c * P:NP_], lhs, dmat[:, c, c * P:NP_],
                                               start=c == 0, stop=c == CH - 1)
                elif kind == "C":
                    pe.wait_ge(vw_ready, 5 * (h + 1))
                    for c in range(CH):
                        ins = nc.tensor.matmul(out[:, 0:HD + 1], ktok[:, c, b * P:(b + 1) * P], vtok[:, c, :],
                                               start=c == 0, stop=c == CH - 1)
                elif kind == "sm":
                    if b == 0:
                        pe.wait_ge(prod_ready, 2 * (h + 1))
                        for g in range(2):
                            for dt in range(DT):
                                nc.tensor.matmul(out[:, g * NB:(g + 1) * NB], ones[:, :], prod[:, g, dt, :],
                                                 start=dt == 0, stop=dt == DT - 1)
                    for bb in range(4):
                        n = h * NB + 4 * b + bb
                        pe.wait_ge(c_in[n % 4], 16 * (n // 4 + 1))
                        for et in range(DT):
                            col = 2 * NB + et * 4 + bb
                            for dt in range(DT):
                                ins = nc.tensor.matmul(out[:, col:col + 1],
                                                       cst_c[:, n % 4, dt, et * P:(et + 1) * P],
                                                       sm[:, 0, dt, 4 * b + bb:4 * b + bb + 1],
                                                       start=dt == 0, stop=dt == DT - 1)
                elif kind == "V":
                    pe.wait_ge(prod_ready, 2 * (h + 1))
                    for bb in range(2):
                        for et in range(DT):
                            v_col = sm[:, 2, et, 2 * b + bb:2 * b + bb + 1]
                            ins = nc.tensor.matmul(out[:, bb * HD + et * P:bb * HD + (et + 1) * P],
                                                   v_col.broadcast_to([P, P]), ident[:, :],
                                                   start=True, stop=True)
                ins.then_inc(job_done, 1)

            for i, (what, j) in enumerate(MIX):
                if what == "bra":
                    xh, xl, base = hb_h, hb_l, S_HA
                elif what == "brb":
                    xh, xl, base = hb_h, hb_l, S_HB
                elif what == "out":
                    xh, xl, base = mg_h, mg_l, S_MG
                else:
                    xh, xl, base = xn_h, xn_l, S_XN2 + 1
                t = T_MIX + i
                product(C_MIX + i, C_MIX + i, t, t // 2, xh, xl, 0, KT,
                        ready=(lambda kt: base + kt + 1) if i == 0 or (j == 0 and what in ("bra", "brb", "out"))
                        else None)
                for key in AFTER[i]:
                    small_job(key)
            norm_sums(M_NORM3, 3 * KT)
            ffn(C_FFI2, T_FFI2, S_XN3, S_HID2, False)
            norm_sums(M_NORM4, 4 * KT)

        @block.scalar
        def _(act):
            A = nc.scalar.activation
            own = [0]

            def link(ins):
                own[0] += 1
                ins.then_inc(ach, 1)
                act.wait_ge(ach, own[0])

            def split(c, c_expr, need, width=KT * P):
                act.wait_ge(raw_in[c % RING], need)
                if not isinstance(c_expr, int) or c_expr >= RING:
                    act.wait_ge(chunk_done, c_expr - (RING - 1))
                A(w_h[c % RING][:, 0:width], raw[:, c % RING, 0:width], ACT.Copy).then_inc(w_hi_ready, 1)

            def arrivals(c):
                return 16 * (c // RING + 1)

            def high(s, out, src):
                act.wait_ge(src_ready, sources(s) + 1)
                A(out, src, ACT.Copy).then_inc(hi_ready, 1)

            def squares(n, kt):
                if not isinstance(n, int) or n >= 1:
                    act.wait_ge(ssq_ready, n)
                A(tb[2][:, :], x[:, kt, :], ACT.Square).then_inc(sq_ready, 1)

            def root(m):
                for hf in range(2):
                    act.wait_ge(job_done, m + hf + 1)
                    A(rstd[:, hf * HALF:(hf + 1) * HALF], bank[(m + hf) % BANKS][:, 0:HALF], ACT.Sqrt,
                      bias=eps_t[:, :], scale=1.0 / D).then_inc(taken[(m + hf) % BANKS], 1)

            def norm(index, m, shift, s_base):
                root(m)
                high(s_base, xn_h[:, :, NP_:T], ys[:, :, :])
                act.wait_ge(gain_ready, index + 1)
                for kt in range(KT):
                    act.wait_ge(nrm_ready, index * KT + kt + 1)
                    if kt >= 2:
                        act.wait_ge(lo_ready, s_base + kt)
                    A(tb[2 + kt % 2][:, 0:NP_], tb[kt % 2][:, 0:NP_], ACT.Identity,
                      bias=mod[:, shift * KT + kt, 0:1], scale=gain[:, kt, 0:1]).then_inc(src_ready, 1)
                    high(s_base + 1 + kt, xn_h[:, kt, 0:NP_], tb[2 + kt % 2][:, 0:NP_])

            def ffn(cb, tbase, s_hid, sq_base, x_base):
                def step(k, i, peeled):
                    off = 0 if peeled else i * FFI_BODY
                    third = 0 if peeled else i * (FFI_BODY // 2)
                    c = cb + k + LEAD
                    split(c, off + c, arrivals(c) + (0 if peeled else i * (16 * FFI_BODY // RING)))
                    t = tbase + k
                    if k % 2 == 0:
                        act.wait_ge(chunk_done, off + (cb + k + 1))
                        A(two(tb[0][:, :]), slot_view(t), ACT.Silu).then_inc(evac[t % 2], 1)
                    else:
                        act.wait_ge(evac[t % 2], third + (t // 2 + 1))
                        A(hid_h[:, third + k // 2, :], tb[1][:, :], ACT.Copy).then_inc(hi_ready, 1)

                first = 1 if cb == 0 else 0
                for k in range(FFI_BODY * first):
                    step(k, 0, True)
                with act.Fori(first, FFI_LOOPS) as i:
                    for k in range(FFI_BODY):
                        step(k, i, False)
                for k in range(FFI_LOOPS * FFI_BODY, 2 * FT):
                    step(k, 0, True)
                co = cb + 2 * FT

                def turn(i):
                    for jj in range(2):
                        for k in range(3):
                            c = co + 3 * jj + k + LEAD
                            if isinstance(i, int) and i * 6 + c >= C_END:
                                continue
                            split(c, i * 6 + c, i * (16 * 6 // RING) + arrivals(c), FFO_CHUNKS[(k + LEAD) % 3][1] * P)
                        act.wait_ge(x_ready, i * 2 + (x_base + jj + 1))
                        squares(i * 2 + (sq_base + jj), i * 2 + jj)

                with act.Fori(0, KT // 2 - 1) as i:
                    turn(i)
                turn(KT // 2 - 1)

            act.wait_ge(small_in, 16 * 3)
            A(cs[:, :, :], cs[:, :, :], ACT.Silu).then_inc(cs_ready, 1)
            act.wait_ge(x_in, 32)
            for kt in range(KT):
                squares(kt, kt)
            for c in range(LEAD):
                split(c, c, arrivals(c))
            act.wait_ge(const_ready, 5)
            norm(0, M_NORM1, SH1, S_XN1)
            ffn(C_FFI1, T_FFI1, S_HID1, KT, 0)
            norm(1, M_NORM2, SH2, S_XN2)

            act.wait_ge(sp_abs, 1)
            A(sp[:, 1, :], sp[:, 0, :], ACT.Exp, scale=-1.0).then_inc(exp_sp, 1)

            def take(key, out, in_, func, **kw):
                m = JOB[key]
                act.wait_ge(job_done, m + 1)
                return A(out, in_, func, **kw).then_inc(taken[m % BANKS], 1)

            def rg_gates(pair):
                act.wait_ge(lo_ready, S_HA + pair[0])
                for j in pair:
                    p = j % 2
                    for dst, kind, bias in ((rg_r, "rga", V_BA), (rg_i, "rgi", V_BI)):
                        for hf in range(2):
                            key = (kind, j, hf)
                            take(key, dst[p][:, hf * HALF:(hf + 1) * HALF], bank[JOB[key] % BANKS][:, 0:HALF],
                                 ACT.Sigmoid, bias=vec[:, bias, j:j + 1])
                for j in pair:
                    p = j % 2
                    wait_taken(act, JOB["rga", j, 0])
                    wait_taken(act, JOB["rga", j, 1])
                    A(rg_a[p][:, :], rg_r[p][:, :], ACT.Exp, scale=c8[:, 0, j:j + 1]).then_inc(rg_ra, 1)
                    act.wait_ge(rg_ra, 2 * j + 1)
                    A(rg_r[p][:, :], rg_r[p][:, :], ACT.Tanh, scale=c8[:, 1, j:j + 1]).then_inc(rg_ra, 1)
                for j in pair:
                    act.wait_ge(rg_w, j + 1)
                    A(rg_v[j % 2][:, :], rg_v[j % 2][:, :], ACT.Sqrt).then_inc(rg_sq, 1)

            def small_job(key):
                kind, h, b = key
                m = JOB[key]
                src = bank[m % BANKS]
                if kind in ("rga", "rgi"):
                    if (kind, h % 2, b) == ("rgi", 1, 1):
                        rg_gates((h - 1, h))
                elif kind == "kT":
                    take(key, ktok[:, :, b * P:(b + 1) * P], src[:, :].rearrange("p (c f) -> p c f", c=CH), ACT.Copy)
                elif kind == "vT":
                    take(key, vtok[:, :, b * P:(b + 1) * P], src[:, :].rearrange("p (c f) -> p c f", c=CH), ACT.Copy)
                    if b == 1:
                        wait_taken(act, JOB["Bt", h, 0])
                        for c in range(CH - 1):
                            A(dmat[:, c, (c + 1) * P:NP_], tb[0][:, (c + 1) * P:NP_], ACT.Exp,
                              bias=aT[:, c, h:h + 1]).then_inc(d_ready, 1)
                        act.wait_ge(diag_ready, CH * (h + 1))
                        for c in range(CH):
                            A(dmat[:, c, c * P:(c + 1) * P], tb[3][:, c * P:(c + 1) * P], ACT.Exp).then_inc(d_ready, 1)
                elif kind == "em":
                    if h:
                        act.wait_ge(cp_out, 16 * DT * h)
                    take(key, tb[1][:, 0:NP_], src[:, 0:NP_], ACT.Exp, scale=-1.0)
                elif kind == "C":
                    take(key, cst[:, b, :], src[:, 0:HD + 1], ACT.Copy)
                elif kind == "sm":
                    act.wait_ge(job_done, m + 1)
                    for bb in range(4):
                        n = h * NB + 4 * b + bb
                        A(cst_c[:, n % 4, :, :], cst_c[:, n % 4, :, :], ACT.Identity,
                          scale=rsb[:, h, 1, 4 * b + bb:4 * b + bb + 1]).then_inc(c_scaled, 1)

            for i, (what, j) in enumerate(MIX):
                c = C_MIX + i + LEAD
                split(c, c, arrivals(c))
                t = T_MIX + i
                act.wait_ge(chunk_done, C_MIX + i + 1)
                src = slot_view(t)
                e = evac[t % 2]
                if what == "gates":
                    act.wait_ge(rg_in, 16 * 7)
                    A(two(row_i[:, :]), big[t % 2][0:HEADS, :, 0:HALF], ACT.Identity,
                      bias=gb_t[0:HEADS, :]).then_inc(ach, 1)
                    own[0] += 1
                    act.wait_ge(ach, own[0])
                    A(two(row_f[:, :]), big[t % 2][32:32 + HEADS, :, 0:HALF], ACT.Identity,
                      bias=gb_t[32:32 + HEADS, :]).then_inc(e, 1)
                elif what == "xrg":
                    if j >= 2:
                        act.wait_ge(conv_done, j - 1)
                    A(two(rg_x[j % 2][:, CONV_W - 1:]), src, ACT.Copy).then_inc(e, 1)
                elif what in "qkv":
                    h, dt = divmod(j, DT)
                    if what == "v":
                        dst = v_t
                        if h == 0:
                            act.wait_ge(lo_ready, S_HA + KT)
                            act.wait_ge(state_out, 16 * 3)
                    else:
                        dst = (q_t if what == "q" else k_t)[h % 2]
                    A(two(dst[:, dt, :]), src, ACT.Copy).then_inc(e, 1)
                elif what == "gb" and j < EARLY:
                    A(two(sgb[j]), src, ACT.Sigmoid).then_inc(e, 1)
                elif what in ("ga", "gb", "o"):
                    if what == "o":
                        act.wait_ge(src_ready, sources(S_HB) + j)
                    elif what == "ga":
                        if j:
                            wait_evac(act, T_OF["bra", j - 1])
                    else:
                        wait_evac(act, T_OF["brb", j - 1])
                    A(two(tb[0 if what != "o" else 2][:, :]), src, ACT.Sigmoid).then_inc(e, 1)
                for jj in RG_SCAN.get(i, ()):
                    high(S_HA + jj, hb_h[:, jj, :], rg_u[jj % 2][:, :])
                if what == "o":
                    high(S_HB + j, hb_h[:, j, :], hm[:, j % DT, :])
                elif what == "brb":
                    high(S_MG + j, mg_h[:, j, :], tb[1][:, :])
                elif what == "out":
                    act.wait_ge(x_ready, KT + j + 1)
                    squares(2 * KT + j, j)
                if (what, j) == ("ga", 1):
                    act.wait_ge(f_abs, 1)
                    A(tb[3][0:HEADS, :], tb[3][0:HEADS, :], ACT.Exp, scale=-1.0).then_inc(f_exp, 1)
                elif (what, j) == ("ga", 2):
                    act.wait_ge(row_arg, 1)
                    A(rs[:, :, :], rs[:, :, :], ACT.Exp).then_inc(row_exp, 1)
                for key in AFTER[i]:
                    small_job(key)

            norm(2, M_NORM3, SH3, S_XN3)
            act.wait_ge(state_out, 16 * 5)
            ffn(C_FFI2, T_FFI2, S_HID2, 3 * KT, 2 * KT)
            root(M_NORM4)

        @block.vector
        def _(dve):
            V = nc.vector
            own = [0]

            def link(ins):
                own[0] += 1
                ins.then_inc(dch, 1)
                dve.wait_ge(dch, own[0])

            def split(c, c_expr, width=KT * P):
                dve.wait_ge(w_hi_ready, c_expr + 1)
                V.tensor_tensor(w_l[c % RING][:, 0:width], raw[:, c % RING, 0:width],
                                w_h[c % RING][:, 0:width], ALU.subtract).then_inc(w_lo_ready, 1)

            def low(s, out, src, hi):
                dve.wait_ge(hi_ready, s + 1)
                V.tensor_tensor(out, src, hi, ALU.subtract).then_inc(lo_ready, 1)

            def add_squares(n, first):
                dve.wait_ge(sq_ready, n + 1)
                if first:
                    V.tensor_copy(ssq[:, :], tb[2][:, :]).then_inc(ssq_ready, 1)
                else:
                    dve.wait_ge(ssq_ready, n)
                    V.tensor_tensor(ssq[:, :], ssq[:, :], tb[2][:, :], ALU.add).then_inc(ssq_ready, 1)

            def mod_tiles(m_static, m_expr, tile):
                dve.wait_ge(job_done, m_expr + 1)
                V.tensor_tensor(mod[:, bass.ds(tile, 2), :],
                                bank[m_static % BANKS][:, 0:2 * (NB + 1)].rearrange("p (t n) -> p t n", t=2),
                                badat[:, bass.ds(tile, 2)].unsqueeze(2).broadcast_to([P, 2, NB + 1]),
                                ALU.add).then_inc(taken[m_static % BANKS], 1)

            def set_gain(index, scale, g, last_job):
                if last_job is not None:
                    for m in range(last_job - BANKS, last_job):
                        wait_taken(dve, m)
                V.scalar_tensor_tensor(gain[:, :, :], mod[:, scale * KT:(scale + 1) * KT, :], 1.0,
                                       vec[:, g, :].unsqueeze(2).broadcast_to([P, KT, NB + 1]),
                                       ALU.add, ALU.mult).then_inc(gain_ready, 1)
                dve.wait_ge(gain_ready, index + 1)

            def inverse_root(m):
                for hf in range(2):
                    wait_taken(dve, m + hf)
                    s = slice(hf * HALF, (hf + 1) * HALF)
                    link(V.reciprocal(rstd[:, s], rstd[:, s]))

            def norm(index, m, shift, s_base):
                inverse_root(m)
                link(V.tensor_tensor(ys[:, :, :], x[:, :, NP_:T],
                                     rstd[:, NP_:T].unsqueeze(1).broadcast_to([P, KT, NB]), ALU.mult))
                link(V.tensor_tensor(ys[:, :, :], ys[:, :, :], gain[:, :, 1:], ALU.mult))
                V.tensor_tensor(ys[:, :, :], ys[:, :, :], mod[:, shift * KT:(shift + 1) * KT, 1:],
                                ALU.add).then_inc(src_ready, 1)
                def prompt(kt):
                    if kt >= 2:
                        dve.wait_ge(src_ready, sources(s_base) + kt)
                    V.tensor_tensor(tb[kt % 2][:, 0:NP_], x[:, kt, 0:NP_], rstd[:, 0:NP_],
                                    ALU.mult).then_inc(nrm_ready, 1)
                prompt(0)
                prompt(1)
                low(s_base, xn_l[:, :, NP_:T], ys[:, :, :], xn_h[:, :, NP_:T])
                for kt in range(KT):
                    low(s_base + 1 + kt, xn_l[:, kt, 0:NP_], tb[2 + kt % 2][:, 0:NP_], xn_h[:, kt, 0:NP_])
                    if kt + 2 < KT:
                        prompt(kt + 2)

            def add_gated(t, kt, gate, ready_count):
                big_t = big[t % 2]
                V.scalar_tensor_tensor(x[:, kt, 0:HALF], big_t[:, 0, 0:HALF], mod[:, gate, 0:1],
                                       x[:, kt, 0:HALF], ALU.mult, ALU.add)
                V.scalar_tensor_tensor(x[:, kt, HALF:NP_], big_t[:, 1, 0:NP_ - HALF], mod[:, gate, 0:1],
                                       x[:, kt, HALF:NP_], ALU.mult, ALU.add)
                V.tensor_tensor(tmp8[:, :], big_t[:, 1, NP_ - HALF:HALF], mod[:, gate, 1:],
                                ALU.mult).then_inc(evac[t % 2], 1)
                dve.wait_ge(evac[t % 2], ready_count)
                V.tensor_tensor(x[:, kt, NP_:T], x[:, kt, NP_:T], tmp8[:, :], ALU.add).then_inc(x_ready, 1)

            def ffn(cb, tbase, s_hid, gate, sq_base, with_ada):
                def step(k, i, peeled):
                    off = 0 if peeled else i * FFI_BODY
                    third = 0 if peeled else i * (FFI_BODY // 2)
                    c = cb + k + LEAD
                    split(c, off + c)
                    if k % 2:
                        j = k // 2
                        t = tbase + k
                        dve.wait_ge(chunk_done, off + (cb + k + 1))
                        dve.wait_ge(evac[(t - 1) % 2], third + ((t - 1) // 2 + 1))
                        dve.wait_ge(lo_ready, third + (s_hid + j))
                        V.tensor_tensor(two(tb[1][:, :]), two(tb[0][:, :]), slot_view(t),
                                        ALU.mult).then_inc(evac[t % 2], 1)
                        low(third + (s_hid + j), hid_l[:, third + j, :], tb[1][:, :], hid_h[:, third + j, :])
                    if with_ada and not peeled and k in (0, 1, 3, 4):
                        n = (0, 1, 3, 4).index(k)
                        mod_tiles(M_ADA1 + n, i * 4 + (M_ADA1 + n), i * 8 + (ADA_FIRST + 2 * n))

                with dve.Fori(0, FFI_LOOPS) as i:
                    for k in range(FFI_BODY):
                        step(k, i, False)
                for k in range(FFI_LOOPS * FFI_BODY, 2 * FT):
                    step(k, 0, True)
                co = cb + 2 * FT
                to = tbase + 2 * FT
                if with_ada:
                    for m in range(M_NORM2 - BANKS, M_NORM2):
                        wait_taken(dve, m)
                link(V.tensor_scalar(mod[:, gate:gate + KT, :], mod[:, gate:gate + KT, :], 0.5, None, ALU.mult))
                link(V.memset(ssq[:, :], 0.0))

                def turn(i):
                    for jj in range(2):
                        for k in range(3):
                            c = co + 3 * jj + k + LEAD
                            if isinstance(i, int) and i * 6 + c >= C_END:
                                continue
                            split(c, i * 6 + c, FFO_CHUNKS[(k + LEAD) % 3][1] * P)
                        dve.wait_ge(chunk_done, i * 6 + (co + 3 * jj + 3))
                        add_gated(to + jj, i * 2 + jj, i * 2 + (jj + gate), i + ((to + jj) // 2 + 1))
                        add_squares(i * 2 + (sq_base + jj), False)

                with dve.Fori(0, KT // 2 - 1) as i:
                    turn(i)
                turn(KT // 2 - 1)

            def log1p_times2z(z, z2, p):
                link(V.tensor_tensor(z2, z, z, ALU.mult))
                link(V.tensor_scalar(p, z2, 1.0 / 19, None, ALU.mult))
                for n in range(17, 1, -2):
                    link(V.scalar_tensor_tensor(p, p, 1.0 / n, z2, ALU.add, ALU.mult))
                link(V.scalar_tensor_tensor(p, p, 1.0, z, ALU.add, ALU.mult))
                link(V.tensor_scalar(p, p, 2.0, None, ALU.mult))

            for kt in range(KT):
                add_squares(kt, kt == 0)
            dve.wait_ge(small_in, 16 * 3)
            for q in range(ADA_FIRST // 2):
                mod_tiles(M_ADA0 + q, M_ADA0 + q, 2 * q)
            for c in range(LEAD):
                split(c, c)
            set_gain(0, SC1, V_G1, M_NORM1)
            norm(0, M_NORM1, SH1, S_XN1)
            ffn(C_FFI1, T_FFI1, S_HID1, GA1 * KT, KT, True)
            set_gain(1, SC2, V_G2, None)
            norm(1, M_NORM2, SH2, S_XN2)

            lam = vec[:, V_LAM, :]
            V.scalar_tensor_tensor(sp[:, 0, :], lam, -1.0, lam, ALU.mult, ALU.max).then_inc(sp_abs, 1)
            for p in range(2):
                V.memset(rg_x[p][:, 0:CONV_W - 1], 0.0)
            dve.wait_ge(exp_sp, 1)
            link(V.tensor_scalar(sp[:, 2, :], sp[:, 1, :], 2.0, None, ALU.add))
            link(V.reciprocal(sp[:, 2, :], sp[:, 2, :]))
            link(V.tensor_tensor(sp[:, 2, :], sp[:, 2, :], sp[:, 1, :], ALU.mult))
            log1p_times2z(sp[:, 2, :], sp[:, 3, :], sp[:, 1, :])
            link(V.tensor_scalar(sp[:, 0, :], lam, -1.0, 0.0, ALU.mult, ALU.max))
            link(V.tensor_tensor(sp[:, 0, :], sp[:, 0, :], sp[:, 1, :], ALU.add))
            link(V.tensor_scalar(c8[:, 0, :], sp[:, 0, :], -8.0, None, ALU.mult))
            link(V.tensor_scalar(c8[:, 1, :], sp[:, 0, :], 8.0, None, ALU.mult))

            def conv(j):
                p = j % 2
                xr, u = rg_x[p], rg_u[p]
                wait_evac(dve, T_OF["xrg", j])
                if j == 0:
                    dve.wait_ge(rg_in, 16 * 7)
                if j >= 2:
                    dve.wait_ge(lo_ready, S_HA + j - 1)
                NC = CONV_W - 1
                for w in range(CONV_W):
                    tap = cw[:, j, w:w + 1]
                    new = xr[:, NC + NP_:NC + T] if w == NC else stc[:, j, w, :]
                    if w == 0:
                        V.tensor_scalar(u[:, 0:NP_], xr[:, 0:NP_], tap, vec[:, V_CB, j:j + 1], ALU.mult, ALU.add)
                        link(V.tensor_scalar(u[:, NP_:T], new, tap, vec[:, V_CB, j:j + 1], ALU.mult, ALU.add))
                    else:
                        V.scalar_tensor_tensor(u[:, 0:NP_], xr[:, w:w + NP_], tap, u[:, 0:NP_], ALU.mult, ALU.add)
                        link(V.scalar_tensor_tensor(u[:, NP_:T], new, tap, u[:, NP_:T], ALU.mult, ALU.add))
                V.tensor_copy(convp[:, j, :], xr[:, NP_:NP_ + NC])
                V.tensor_copy(convs[:, j, 0:NC - 1, :], stc[:, j, 1:NC, :])
                V.tensor_copy(convs[:, j, NC - 1, :], xr[:, NC + NP_:NC + T]).then_inc(conv_done, 1)

            def rg_weight(j):
                p = j % 2
                a, v, th = rg_a[p], rg_v[p], rg_r[p]
                dve.wait_ge(rg_ra, 2 * j + 2)
                link(V.tensor_tensor(v[:, :], a[:, :], a[:, :], ALU.mult))
                V.scalar_tensor_tensor(v[:, :], v[:, :], 1.0, th[:, :], ALU.add, ALU.mult).then_inc(rg_w, 1)

            def rg_scan(j):
                p = j % 2
                a, v, u, ig = rg_a[p], rg_v[p], rg_u[p], rg_i[p]
                for hf in range(2):
                    wait_taken(dve, JOB["rgi", j, hf])
                link(V.tensor_tensor(ig[:, :], ig[:, :], u[:, :], ALU.mult))
                dve.wait_ge(rg_sq, j + 1)
                link(V.tensor_tensor(ig[:, :], ig[:, :], v[:, :], ALU.mult))
                V.tensor_tensor_scan(u[:, 0:NP_], a[:, 0:NP_], ig[:, 0:NP_], 0.0, ALU.mult, ALU.add)
                link(V.tensor_tensor(u[:, NP_:T], a[:, NP_:T], sth[:, j, :], ALU.mult))
                link(V.tensor_tensor(u[:, NP_:T], u[:, NP_:T], ig[:, NP_:T], ALU.add))
                V.tensor_copy(hout[:, j, :], u[:, NP_ - 1:T]).then_inc(src_ready, 1)

            def rg_low(j):
                p = j % 2
                low(S_HA + j, hb_l[:, j, :], rg_u[p][:, :], hb_h[:, j, :])

            def gate_rows():
                f, ig, m = row_f[:, :], row_i[:, :], row_m[:, :]
                t0, t1, t2, t3 = (t[0:HEADS, :] for t in tb)
                wait_evac(dve, T_OF["gates", 0])
                V.scalar_tensor_tensor(t3, f, -1.0, f, ALU.mult, ALU.max).then_inc(f_abs, 1)
                dve.wait_ge(f_exp, 1)
                link(V.tensor_scalar(t1, t3, 2.0, None, ALU.add))
                link(V.reciprocal(t1, t1))
                link(V.tensor_tensor(t1, t1, t3, ALU.mult))
                log1p_times2z(t1, t2, t3)
                link(V.scalar_tensor_tensor(f, f, 0.0, t3, ALU.min, ALU.subtract))
                link(V.tensor_tensor_scan(m[:, 0:NP_], f[:, 0:NP_], ig[:, 0:NP_], 0.0, ALU.add, ALU.max))
                link(V.memset(t2[:, 0:NP_], 0.0))
                link(V.tensor_tensor_scan(t1[:, 0:NP_], f[:, 0:NP_], t2[:, 0:NP_], 0.0, ALU.add, ALU.add))
                s = slice(NP_, T)
                link(V.tensor_tensor(t1[:, s], f[:, s], stm[:, :], ALU.add))
                link(V.tensor_tensor(m[:, s], t1[:, s], ig[:, s], ALU.max))
                link(V.tensor_tensor(rs[:, 0, :], ig[:, s], m[:, s], ALU.subtract))
                link(V.tensor_tensor(rs[:, 1, :], t1[:, s], m[:, s], ALU.subtract))
                V.tensor_scalar(rs[:, 2, :], m[:, s], -1.0, None, ALU.mult).then_inc(row_arg, 1)
                link(V.tensor_tensor(f[:, 0:NP_], t1[:, 0:NP_], m[:, 0:NP_], ALU.subtract))
                V.tensor_tensor(ig[:, 0:NP_], ig[:, 0:NP_], t1[:, 0:NP_], ALU.subtract).then_inc(rows_ready, 1)

            def sample_products(h):
                p = h % 2
                if h:
                    wait_taken(dve, JOB["V", h - 1, 3])
                for n, src, w in ((0, q_t[p], "q"), (1, k_t[p], "k"), (2, v_t, "v")):
                    for dt in range(DT):
                        wait_evac(dve, T_OF[w, DT * h + dt])
                    link(V.tensor_copy(sm[:, n, :, :], src[:, :, NP_:T]))
                V.tensor_tensor(prod[:, 0, :, :], sm[:, 0, :, :], sm[:, 1, :, :], ALU.mult).then_inc(prod_ready, 1)
                V.tensor_tensor(prod[:, 1, :, :], sm[:, 0, :, :], stn[:, h, :, :], ALU.mult).then_inc(prod_ready, 1)
                dve.wait_ge(prod_ready, 2 * (h + 1))
                link(V.tensor_tensor(kd[:, :, :], sm[:, 1, :, :],
                                     rsb[:, h, 0, :].unsqueeze(1).broadcast_to([P, DT, NB]), ALU.mult))
                link(V.tensor_tensor(stn[:, h, :, :], stn[:, h, :, :],
                                     rsb[:, h, 1, :].unsqueeze(1).broadcast_to([P, DT, NB]), ALU.mult))
                V.tensor_tensor(stn[:, h, :, :], stn[:, h, :, :], kd[:, :, :], ALU.add).then_inc(states_ready, 1)

            def sample_outputs(h):
                wi, wp, em = (rsb[:, h, n, :] for n in range(3))
                s, den = s8[:, 0, :], s8[:, 1, :]
                link(V.scalar_tensor_tensor(s, sres[:, 0, :], QSCALE, wi, ALU.mult, ALU.mult))
                link(V.scalar_tensor_tensor(den, sres[:, 1, :], QSCALE, wp, ALU.mult, ALU.mult))
                link(V.tensor_tensor(den, den, s, ALU.add))
                link(V.scalar_tensor_tensor(s8[:, 2, :], den, -1.0, em, ALU.mult, ALU.max))
                link(V.tensor_tensor(den, den, s8[:, 2, :], ALU.max))
                link(V.reciprocal(den, den))
                for et in range(DT):
                    num, sv = sres[:, 2 + et, :], s8[:, 2 + et, :]
                    link(V.scalar_tensor_tensor(num, num, QSCALE, wp, ALU.mult, ALU.mult))
                    link(V.tensor_tensor(sv, s, sm[:, 2, et, :], ALU.mult))
                    link(V.tensor_tensor(num, num, sv, ALU.add))
                    link(V.tensor_tensor(hm[:, et, NP_:T], num, den, ALU.mult))

            def small_job(key):
                kind, h, b = key
                m = JOB[key]
                src = bank[m % BANKS]

                def done():
                    dve.wait_ge(job_done, m + 1)

                free = taken[m % BANKS]
                if kind == "aT":
                    done()
                    V.tensor_copy(aT[:, :, :], src[:, 0:CH * HEADS].rearrange("p (c h) -> p c h", c=CH)
                                  ).then_inc(free, 1)
                elif kind == "srow":
                    done()
                    V.tensor_copy(rsb[:, :, :, :], src[:, 0:HEADS * 3 * NB].rearrange("p (h a b) -> p h a b", h=HEADS, a=3)
                                  ).then_inc(free, 1)
                elif kind == "Bt":
                    if h:
                        dve.wait_ge(d_ready, (2 * CH - 1) * h)
                        wait_taken(dve, JOB["num", h - 1, 1])
                    else:
                        wait_evac(dve, T_OF["bra", KT - 1])
                    done()
                    V.tensor_copy(tb[0][:, 0:NP_], src[:, 0:NP_]).then_inc(free, 1)
                    wait_taken(dve, m)
                    for c in range(CH):
                        cc = slice(c * P, (c + 1) * P)
                        V.scalar_tensor_tensor(tb[3][:, cc], tb[0][:, cc], aT[:, c, h:h + 1], maskneg[:, :],
                                               ALU.add, ALU.add).then_inc(diag_ready, 1)
                elif kind == "vT" and b == 1:
                    sample_products(h)
                elif kind == "S":
                    if b == 0:
                        dve.wait_ge(d_ready, (2 * CH - 1) * (h + 1))
                        if h:
                            dve.wait_ge(vw_ready, 5 * h)
                        link(V.tensor_copy(wcol[:, :], dmat[:, :, NP_ - 1]))
                    done()
                    V.scalar_tensor_tensor(dmat[:, b, b * P:NP_], src[:, b * P:NP_], QSCALE, dmat[:, b, b * P:NP_],
                                           ALU.mult, ALU.mult).then_inc(free, 1)
                elif kind == "den":
                    done()
                    wait_taken(dve, JOB["em", h, 0])
                    link(V.scalar_tensor_tensor(tb[3][:, 0:NP_], src[:, 0:NP_], -1.0, tb[1][:, 0:NP_], ALU.mult, ALU.max))
                    V.tensor_tensor(tb[3][:, 0:NP_], src[:, 0:NP_], tb[3][:, 0:NP_], ALU.max).then_inc(free, 1)
                    wait_taken(dve, m)
                    link(V.reciprocal(tb[3][:, 0:NP_], tb[3][:, 0:NP_]))
                elif kind == "num":
                    if h:
                        dve.wait_ge(lo_ready, S_HB + DT * h)
                    done()
                    V.tensor_tensor(hm[:, b, 0:NP_], src[:, 0:NP_], tb[3][:, 0:NP_], ALU.mult).then_inc(free, 1)
                    wait_taken(dve, m)
                    if b == 1:
                        for c in range(CH):
                            V.tensor_scalar(vtok[:, c, 0:HD], vtok[:, c, 0:HD], wcol[:, c:c + 1], None,
                                            ALU.mult).then_inc(vw_ready, 1)
                        V.tensor_copy(vtok[:, :, HD], wcol[:, :]).then_inc(vw_ready, 1)
                elif kind == "sm":
                    done()
                    if b == 0:
                        V.tensor_copy(sres[:, 0:2, :], src[:, 0:2 * NB].rearrange("p (g b) -> p g b", g=2))
                    V.tensor_copy(sres[:, 2:4, 4 * b:4 * b + 4],
                                  src[:, 2 * NB:2 * NB + 2 * 4].rearrange("p (e b) -> p e b", e=DT)).then_inc(free, 1)
                    wait_taken(dve, m)
                    if b == 1:
                        sample_outputs(h)
                elif kind == "V":
                    done()
                    for bb in range(2):
                        n = h * NB + 2 * b + bb
                        dve.wait_ge(c_scaled, n + 1)
                        for dt in range(DT):
                            ins = V.scalar_tensor_tensor(cst_c[:, n % 4, dt, :], src[:, bb * HD:(bb + 1) * HD],
                                                         kd[:, dt, 2 * b + bb:2 * b + bb + 1],
                                                         cst_c[:, n % 4, dt, :], ALU.mult, ALU.add)
                    ins.then_inc(free, 1)

            for i, (what, j) in enumerate(MIX):
                c = C_MIX + i + LEAD
                split(c, c)
                t = T_MIX + i
                for jj in RG_SCAN.get(i, ()):
                    rg_scan(jj)
                    rg_low(jj)
                if what == "xrg":
                    conv(j)
                elif what == "bra":
                    dve.wait_ge(chunk_done, C_MIX + i + 1)
                    wait_evac(dve, t - 1)
                    V.tensor_tensor(two(ma[:, j, :]), two(tb[0][:, :]), slot_view(t), ALU.mult).then_inc(evac[t % 2], 1)
                elif what == "brb":
                    dve.wait_ge(chunk_done, C_MIX + i + 1)
                    wait_evac(dve, T_OF["gb", j])
                    if j:
                        dve.wait_ge(lo_ready, S_MG + j)
                    else:
                        dve.wait_ge(cp_out, 16 * DT * HEADS)
                    gate = sgb[j] if j < EARLY else tb[0][:, :]
                    V.tensor_tensor(two(tb[1][:, :]), two(gate), slot_view(t), ALU.mult).then_inc(evac[t % 2], 1)
                    wait_evac(dve, t)
                    V.tensor_tensor(tb[1][:, :], tb[1][:, :], ma[:, j, :], ALU.add).then_inc(src_ready, 1)
                    low(S_MG + j, mg_l[:, j, :], tb[1][:, :], mg_h[:, j, :])
                elif what == "o":
                    wait_evac(dve, t)
                    V.tensor_tensor(hm[:, j % DT, :], hm[:, j % DT, :], tb[2][:, :], ALU.mult).then_inc(src_ready, 1)
                    low(S_HB + j, hb_l[:, j, :], hm[:, j % DT, :], hb_h[:, j, :])
                elif what == "out":
                    dve.wait_ge(chunk_done, C_MIX + i + 1)
                    add_gated(t, j, GA2 * KT + j, t // 2 + 1)
                    add_squares(2 * KT + j, j == 0)
                if (what, j) == ("ga", 1):
                    gate_rows()
                for key in AFTER[i]:
                    small_job(key)
                for jj in RG_AT.get(i, ()):
                    rg_weight(jj)

            set_gain(2, SC3, V_G3, None)
            norm(2, M_NORM3, SH3, S_XN3)
            dve.wait_ge(state_out, 16 * 5)
            ffn(C_FFI2, T_FFI2, S_HID2, GA3 * KT, 3 * KT, False)
            inverse_root(M_NORM4)
            for kt in range(KT):
                if kt >= 2:
                    dve.wait_ge(y_out[kt % 2], 16 * (kt // 2))
                V.scalar_tensor_tensor(tb[2 + kt % 2][:, :], x[:, kt, :], vec[:, V_GF, kt:kt + 1], rstd[:, :],
                                       ALU.mult, ALU.mult).then_inc(y_ready, 1)


RG_SCAN = {at + 1 + n: (pair[n],) for at, pair in RG_AT.items() for n in range(2) if pair[1] < KT - 1}
RG_SCAN[MIX.index(("ga", 0))] = (KT - 2, KT - 1)


def _tiles(w):
    w = np.asarray(w)
    k, n = w.shape
    return np.ascontiguousarray(w.reshape(k // P, P, n // P, P).transpose(2, 1, 0, 3)).reshape(n // P, P, k)


def _features(a):
    a = np.asarray(a)
    lead = a.shape[:-1]
    a = a.reshape(lead + (KT, P))
    return np.ascontiguousarray(np.moveaxis(np.moveaxis(a, -1, 0), -1, 1))


def kernel(**inputs):
    import concourse.bacc as bacc
    from concourse.bass_utils import run_bass_kernel_spmd

    g = {k: np.asarray(v) for k, v in inputs.items()}
    f32 = np.float32
    x_all = np.concatenate([g["x_prompt"][0], g["x_sample"][:, 0]], 0)
    c_all = np.concatenate([g["c_prompt"], g["c_sample"]], 0)
    w_in = g["w_in"][0]
    q0, k0, v0, o0 = (D * n for n in (1, 2, 3, 4))
    i0 = 5 * D
    f0 = i0 + HEADS
    a0 = f0 + HEADS
    b0 = a0 + D
    gates = np.zeros((D, P), f32)
    gates[:, 0:HEADS] = w_in[:, i0:i0 + HEADS]
    gates[:, 32:32 + HEADS] = w_in[:, f0:f0 + HEADS]
    sources = {
        "gates": gates, "xrg": w_in[:, 0:D], "q": w_in[:, q0:q0 + D], "k": w_in[:, k0:k0 + D],
        "v": w_in[:, v0:v0 + D], "o": w_in[:, o0:o0 + D], "ga": w_in[:, a0:a0 + D], "gb": w_in[:, b0:b0 + D],
        "bra": g["w_br_a"][0], "brb": g["w_br_b"][0], "out": g["w_out"][0],
    }
    tiled = {k: _tiles(w) for k, w in sources.items()}
    w_mix = np.stack([tiled[what][j] for what, j in MIX])

    def up(w):
        t = _tiles(w)
        return np.ascontiguousarray(np.stack([t[:FT], t[FT:]], 1)).reshape(2 * FT, P, D)

    gate_b = np.zeros((P, 1), f32)
    gate_b[0:HEADS, 0] = g["b_ig"][0]
    gate_b[32:32 + HEADS, 0] = g["b_fg"][0]
    vecs = np.stack([g["g_norm1"][0], g["g_norm2"][0], g["g_norm3"][0], g["g_final"], g["conv_b"][0],
                     g["b_rg_a"][0], g["b_rg_i"][0], g["rg_lambda"][0]])
    arrays = {
        "xT": _features(x_all),
        "cT": _features(c_all),
        "w_ada": _tiles(g["w_ada"][0]),
        "b_ada": np.ascontiguousarray(g["b_ada"][0].reshape(NMOD * KT, P).T),
        "ff1_in": up(g["w_ff1_in"][0]),
        "ff1_out": _tiles(g["w_ff1_out"][0]),
        "w_mix": w_mix,
        "ff2_in": up(g["w_ff2_in"][0]),
        "ff2_out": _tiles(g["w_ff2_out"][0]),
        "vecs": np.ascontiguousarray(_features(vecs).transpose(0, 2, 1)),
        "conv_w": _features(g["conv_w"][0]),
        "w_rg": np.ascontiguousarray(np.stack([g["w_rg_a"][0], g["w_rg_i"][0]]).transpose(2, 0, 1, 3)),
        "gate_b": gate_b,
        "st_conv": np.ascontiguousarray(_features(g["state_conv"][0]).transpose(0, 1, 3, 2)),
        "st_h": _features(g["state_rg_h"][0]),
        "st_C": np.ascontiguousarray(
            g["state_C"][0].reshape(NB, HEADS, DT, P, HD).transpose(1, 0, 3, 2, 4)).reshape(HEADS * NB, P, DT * HD),
        "st_n": np.ascontiguousarray(g["state_n"][0].reshape(NB, HEADS, DT, P).transpose(3, 1, 2, 0)),
        "st_m": np.ascontiguousarray(g["state_m"][0].T),
    }
    outs = {
        "yT": (P, KT, T), "o_convp": (P, KT, CONV_W - 1), "o_convs": (P, KT, CONV_W - 1, NB),
        "o_h": (P, KT, NB + 1), "o_Cp": (HEADS, DT, P, HD + 1), "o_Cs": (HEADS * NB, P, DT * HD),
        "o_ns": (P, HEADS, DT, NB), "o_m": (HEADS, NB + 1),
    }
    nc = bacc.Bacc("TRN2", target_bir_lowering=False, num_devices=1)
    args = [nc.dram_tensor(n, a.shape, F32, kind="ExternalInput").ap() for n, a in arrays.items()]
    args += [nc.dram_tensor(n, s, F32, kind="ExternalOutput").ap() for n, s in outs.items()]
    build(nc, *args)
    r = run_bass_kernel_spmd(nc, [arrays], core_ids=[0]).results[0]

    def tokens(a):
        return np.ascontiguousarray(a.transpose(2, 1, 0)).reshape(a.shape[2], D)

    y = tokens(r["yT"])
    y_p, y_s = y[None, :NP_], y[NP_:, None]
    conv_p = tokens(r["o_convp"])[None, None]
    conv_s = np.ascontiguousarray(r["o_convs"].transpose(3, 2, 1, 0)).reshape(1, NB, CONV_W - 1, D)
    hh = tokens(r["o_h"])
    h_p, h_s = hh[None, 0:1], hh[None, 1:]
    cp = r["o_Cp"].reshape(HEADS, HD, HD + 1)
    C_p = np.ascontiguousarray(cp[None, None, :, :, :HD])
    n_p = np.ascontiguousarray(cp[None, None, :, :, HD])
    C_s = np.ascontiguousarray(
        r["o_Cs"].reshape(HEADS, NB, P, DT, HD).transpose(1, 0, 3, 2, 4)).reshape(1, NB, HEADS, HD, HD)
    n_s = np.ascontiguousarray(r["o_ns"].transpose(3, 1, 2, 0)).reshape(1, NB, HEADS, HD)
    m_p = np.ascontiguousarray(r["o_m"][:, 0])[None, None]
    m_s = np.ascontiguousarray(r["o_m"][:, 1:].T)[None]
    return tuple(np.ascontiguousarray(a) for a in
                 (y_p, y_s, conv_p, h_p, C_p, n_p, m_p, conv_s, h_s, C_s, n_s, m_s))
```

```python
from contextlib import ExitStack

import numpy as np

import concourse.bass as bass
from concourse import mybir
from concourse.alu_op_type import AluOpType as ALU

F32 = mybir.dt.float32
F32R = mybir.dt.float32r
ACT = mybir.ActivationFunctionType

P = 128
D = 1024
KT = D // P
NP_ = 512
NB = 8
T = NP_ + NB
HALF = T // 2
D_FF = 2816
FT = D_FF // P
HEADS = 4
DT = 2
HD = DT * P
CH = NP_ // P
CONV_W = 4
NMOD = 9
EPS = 1e-6
QSCALE = HD ** -0.5
NEG = -1e30

RING = 3
LEAD = 2
BANKS = 4

ADA_FIRST = 2 * KT + 1
UP1 = "PMPMPMPMM"
UP2 = "PPPPPP"
UP1_LOOPS, UP2_LOOPS = 2 * FT // 4, 2 * FT // 6
SQ_FROM = 6
MOD_JOBS = (0, 0, 1, 2, 3)
FFO_CHUNKS = ((0, 8), (8, 8), (16, 6))

(SH1, SC1, GA1, SH2, SC2, GA2, SH3, SC3, GA3) = range(NMOD)
(V_G1, V_G2, V_G3, V_GF, V_CB, V_BA, V_BI, V_LAM, NVEC) = range(9)

RG_BUFS = 4
MIX = [("gates", 0)]
for _p, _keys in enumerate([[("q", 0)], [("q", 1), ("ga", 5)], [("k", 0), ("ga", 6)], [("k", 1), ("ga", 7)]]):
    MIX += [("xrg", 2 * _p), ("xrg", 2 * _p + 1)] + _keys
MIX += [("ga", 2), ("ga", 3), ("ga", 4)] + [("bra", _j) for _j in (5, 6, 7, 2, 3, 4)]
MIX += [("ga", 0), ("bra", 0), ("ga", 1), ("bra", 1)]
MIX += [("v", 0), ("v", 1)]
EARLY = 4
for _h in range(HEADS):
    if _h + 1 < HEADS:
        for _w in "qkv":
            MIX += [(_w, DT * (_h + 1)), (_w, DT * (_h + 1) + 1)]
    else:
        MIX += [("gb", _j) for _j in range(EARLY)]
    MIX += [("o", DT * _h), ("o", DT * _h + 1)]
MIX.remove(("o", DT * (HEADS - 2)))
MIX.remove(("o", DT * (HEADS - 2) + 1))
_at = MIX.index(("gb", 0))
MIX[_at:_at] = [("o", DT * (HEADS - 2)), ("o", DT * (HEADS - 2) + 1)]
for _j in range(KT):
    MIX += [("gb", _j)] * (_j >= EARLY) + [("brb", _j)]
MIX += [("out", _j) for _j in range(KT)]
NMIX = len(MIX)
FIRST_OF = {what: min(i for i, key in enumerate(MIX) if key[0] == what) for what, _ in MIX}

C_FFI1 = ADA_FIRST
C_FFO1 = C_FFI1 + len(UP1) * UP1_LOOPS
C_MIX = C_FFO1 + 3 * KT
C_FFI2 = C_MIX + NMIX
C_FFO2 = C_FFI2 + 2 * FT
C_END = C_FFO2 + 3 * KT
T_FFI1 = 0
T_FFO1 = T_FFI1 + 2 * FT
T_MIX = T_FFO1 + KT
T_FFI2 = T_MIX + NMIX
T_FFO2 = T_FFI2 + 2 * FT
T_OF = {key: T_MIX + i for i, key in enumerate(MIX)}
C_OF = {key: C_MIX + i for i, key in enumerate(MIX)}


def head_jobs(h):
    return [
        [("kT", h, 0), ("kT", h, 1), ("Bt", h, 0)],
        [("vT", h, 0), ("vT", h, 1)],
        [("sm", h, 0), ("V", h, 0), ("V", h, 1)],
        [("S", h, c) for c in range(CH)],
        [("em", h, 0), ("den", h, 0), ("num", h, 0), ("num", h, 1)],
        [("sm", h, 1), ("V", h, 2), ("V", h, 3), ("C", h, 0), ("C", h, 1)],
    ]


AFTER = {i: [] for i in range(-1, NMIX)}
RG_AT = {}
for _j in range(0, KT, 2):
    _at = MIX.index(("xrg", _j + 1)) + 2
    RG_AT[_at] = (_j, _j + 1)
    for _jj in (_j, _j + 1):
        AFTER[_at] += [("rga", _jj, 0), ("rga", _jj, 1), ("rgi", _jj, 0), ("rgi", _jj, 1)]
ROWS_AT = {MIX.index(("bra", _j)): _n for _n, _j in enumerate((5, 7, 2, 3, 4))}
F_EXP_AT, ROW_EXP_AT = MIX.index(("bra", 6)), MIX.index(("ga", 0))
AFTER[MIX.index(("bra", 0))] += [("aT", 0, 0), ("srow", 0, 0)]
for _h in range(HEADS):
    _groups = head_jobs(_h)
    if _h + 1 < HEADS:
        _places = [MIX.index((w, DT * (_h + 1) + i)) for w in "qkv" for i in range(2)]
    else:
        _places = [MIX.index(("o", DT * _h - 2)), MIX.index(("o", DT * _h - 1))]
        _places += [MIX.index(("gb", j)) for j in range(EARLY)]
    for _p, _g in zip(_places, _groups):
        AFTER[_p] += _g

M_ADA0 = 0
M_NORM1 = M_ADA0 + (ADA_FIRST + 1) // 2
M_ADA1 = M_NORM1 + 2
M_NORM2 = M_ADA1 + UP1_LOOPS * BANKS
M_MIX = M_NORM2 + 2
JOB = {}
for _i in range(-1, NMIX):
    for _key in AFTER[_i]:
        JOB[_key] = M_MIX + len(JOB)
M_NORM3 = M_MIX + len(JOB)
M_NORM4 = M_NORM3 + 2

S_XN1 = 0
S_HID1 = S_XN1 + 1 + KT
S_XN2 = S_HID1 + FT
S_HA = S_XN2 + 1 + KT
S_HB = S_HA + KT
S_MG = S_HB + KT
S_XN3 = S_MG + KT
S_HID2 = S_XN3 + 1 + KT


def computed(m):
    return m + 1 - (M_NORM1 - M_ADA0) - (M_NORM2 - M_ADA1) * (m >= M_NORM2)


def sources(s):
    return s - FT * (s >= S_XN2) - FT * (s > S_HID2)


def build(nc, xT, cT, w_ada, b_ada, ff1_in, ff1_out, w_mix, ff2_in, ff2_out, vecs, conv_w, w_rg,
          gate_b, st_conv, st_h, st_C, st_n, st_m,
          yT, o_convp, o_convs, o_h, o_Cp, o_Cs, o_ns, o_m):
    ctx = ExitStack()
    with ctx:
        def sb(name, shape, dt=F32, stack=ctx):
            return stack.enter_context(nc.sbuf_tensor(name, shape, dt))

        def sem(name):
            return ctx.enter_context(nc.semaphore(name))

        x = sb("x", [P, KT, T])
        xn_h = sb("xn_h", [P, KT, T], F32R)
        xn_l = sb("xn_l", [P, KT, T], F32R)
        raw = sb("raw", [P, RING, KT * P])
        w_h = [sb(f"w_h{i}", [P, KT * P], F32R) for i in range(RING)]
        w_l = [sb(f"w_l{i}", [P, KT * P], F32R) for i in range(RING)]
        cst_c = sb("cst_c", [P, 4, DT, HD])
        cs_stack = ExitStack()
        cs = sb("cs", [P, KT, NB + 1], F32, cs_stack)
        cs_hl = sb("cs_hl", [P, KT, 2 * (NB + 1)], F32R, cs_stack)
        badat = sb("badat", [P, NMOD * KT], F32, cs_stack)
        cs_stack.close()
        stc = sb("stc", [P, KT, CONV_W - 1, NB])
        sth = sb("sth", [P, KT, NB])
        rs = sb("rs", [HEADS, 3, NB])
        rsb = sb("rsb", [P, HEADS, 3, NB])
        mod = sb("mod", [P, NMOD * KT, NB + 1])
        gain = sb("gain", [P, KT, NB + 1])
        vec = sb("vec", [P, NVEC, KT])
        cw = sb("cw", [P, KT, CONV_W])
        gb_t = sb("gb_t", [P, 1])
        eps_t = sb("eps_t", [P, 1])
        ident = sb("ident", [P, P])
        ones = sb("ones", [P, P])
        maskneg = sb("maskneg", [P, P])
        sel = sb("sel", [HEADS, HEADS, P])
        tb = [sb(f"tb{i}", [P, T]) for i in range(4)]
        ssq = sb("ssq", [P, T])
        rstd = ssq
        ys = sb("ys", [P, KT, NB])
        tmp8 = sb("tmp8", [P, NB])
        aT = sb("aT", [P, CH, HEADS])
        stn = sb("stn", [P, HEADS, DT, NB])
        stm = sb("stm", [HEADS, NB])
        hid_stack = ExitStack()
        hid_h = sb("hid_h", [P, FT, T], F32R, hid_stack)
        hid_l = sb("hid_l", [P, FT, T], F32R, hid_stack)
        hid_stack.close()
        mix_stack = ExitStack()
        ma = sb("ma", [P, KT, T], F32, mix_stack)
        hb_h = sb("hb_h", [P, KT, T], F32R, mix_stack)
        hb_l = sb("hb_l", [P, KT, T], F32R, mix_stack)
        row_i = sb("row_i", [HEADS, T], F32, mix_stack)
        row_f = sb("row_f", [HEADS, T], F32, mix_stack)
        row_m = sb("row_m", [HEADS, T], F32, mix_stack)
        heads_stack = ExitStack()
        q_0 = sb("q_0", [P, DT, T], F32, heads_stack)
        k_0 = sb("k_0", [P, DT, T], F32, heads_stack)
        rg_stack = ExitStack()
        ma_flat = ma[:, :, :].rearrange("p k t -> p (k t)")
        n_x = CONV_W - 1 + T
        rg_u = [sb(f"rg_u{i}", [P, T], F32, rg_stack)[:, :] for i in range(2)]
        rg_u += [ma[:, i, :] for i in range(2)]
        rg_x = [sb(f"rg_x{i}", [P, n_x], F32, rg_stack)[:, :] for i in range(2)]
        rg_x += [ma_flat[:, 2 * T + i * n_x:2 * T + (i + 1) * n_x] for i in range(2)]
        rg_r, rg_i, rg_a, rg_v = ([sb(f"rg_{n}{i}", [P, T], F32, rg_stack) for i in range(2)] for n in "riav")
        wrg = sb("wrg", [P, 2, KT, P], F32, rg_stack)
        c8 = sb("c8", [P, 2, KT], F32, rg_stack)
        rg_stack.close()
        mg_stack = ExitStack()
        mg_h = sb("mg_h", [P, KT, T], F32R, mg_stack)
        mg_l = sb("mg_l", [P, KT, T], F32R, mg_stack)
        mg_stack.close()
        q_t = [q_0, sb("q_1", [P, DT, T], F32, heads_stack)]
        k_t = [k_0, sb("k_1", [P, DT, T], F32, heads_stack)]
        v_t = sb("v_t", [P, DT, T], F32, heads_stack)
        ktok = sb("ktok", [P, CH, HD], F32, heads_stack)
        vtok = sb("vtok", [P, CH, HD + 1], F32, heads_stack)
        dmat = sb("dmat", [P, CH, NP_], F32, heads_stack)
        hm = sb("hm", [P, DT, T], F32, heads_stack)
        sm = sb("sm", [P, 3, DT, NB], F32, heads_stack)
        prod = sb("prod", [P, 2, DT, NB], F32, heads_stack)
        kd = sb("kd", [P, DT, NB], F32, heads_stack)
        sres = sb("sres", [P, 4, NB], F32, heads_stack)
        s8 = sb("s8", [P, 4, NB], F32, heads_stack)
        wcol = sb("wcol", [P, CH], F32, heads_stack)
        sgb = [(q_0, k_0)[j // 2][:, j % 2, :] for j in range(EARLY)]
        heads_stack.close()
        mix_stack.close()
        n_cs, n_ho = KT * (CONV_W - 1) * NB, KT * (NB + 1)
        convs = ssq[:, 0:n_cs].rearrange("p (k j b) -> p k j b", k=KT, j=CONV_W - 1)
        hout = ssq[:, n_cs:n_cs + n_ho].rearrange("p (k n) -> p k n", k=KT)
        convp = ssq[:, n_cs + n_ho:n_cs + n_ho + KT * (CONV_W - 1)].rearrange("p (k j) -> p k j", k=KT)
        sp = ssq[:, T - 4 * KT:T].rearrange("p (a k) -> p a k", a=4)
        cst = tb[1][:, 0:DT * (HD + 1)].rearrange("p (d e) -> p d e", d=DT)

        big = [ctx.enter_context(nc.psum_tensor(f"big{i}", [P, 2, 512], F32)) for i in range(2)]
        bank = [ctx.enter_context(nc.psum_tensor(f"bank{i}", [P, 512], F32)) for i in range(BANKS)]

        def two(ap):
            return ap.rearrange("p (h n) -> p h n", h=2)

        def slot_view(t):
            return big[t % 2][:, :, 0:HALF]

        raw_in = [sem(f"raw_in{i}") for i in range(RING)]
        w_hi_ready = sem("w_hi_ready")
        w_lo_ready = sem("w_lo_ready")
        chunk_done = sem("chunk_done")
        evac = [sem(f"evac{i}") for i in range(2)]
        job_done = sem("job_done")
        taken = [sem(f"taken{i}") for i in range(BANKS)]
        src_ready = sem("src_ready")
        hi_ready = sem("hi_ready")
        lo_ready = sem("lo_ready")
        const_ready = sem("const_ready")
        sel0 = sem("sel0")
        x_in = sem("x_in")
        small_in = sem("small_in")
        cond_in = sem("cond_in")
        mod_high = sem("mod_high")
        cs_ready = sem("cs_ready")
        sq_ready = sem("sq_ready")
        ssq_ready = sem("ssq_ready")
        x_ready = sem("x_ready")
        std_ready = sem("std_ready")
        nrm_ready = sem("nrm_ready")
        nrm_used = sem("nrm_used")
        gain_ready = sem("gain_ready")
        rg_in = sem("rg_in")
        conv_done = sem("conv_done")
        rg_ra = sem("rg_ra")
        rg_w = sem("rg_w")
        rg_sq = sem("rg_sq")
        exp_sp = sem("exp_sp")
        sp_abs = sem("sp_abs")
        f_abs = sem("f_abs")
        f_exp = sem("f_exp")
        row_arg = sem("row_arg")
        row_exp = sem("row_exp")
        rows_ready = sem("rows_ready")
        diag_ready = sem("diag_ready")
        d_ready = sem("d_ready")
        prod_ready = sem("prod_ready")
        vw_ready = sem("vw_ready")
        hm_ready = sem("hm_ready")
        c_in = [sem(f"c_in{i}") for i in range(4)]
        c_scaled = sem("c_scaled")
        c_out = [sem(f"c_out{i}") for i in range(4)]
        cp_out = sem("cp_out")
        state_out = sem("state_out")
        states_ready = sem("states_ready")
        y_ready = sem("y_ready")
        y_out = [sem(f"y_out{i}") for i in range(2)]
        dch = sem("dch")
        ach = sem("ach")

        block = ctx.enter_context(nc.Block())

        def wait_evac(eng, t):
            eng.wait_ge(evac[t % 2], t // 2 + 1)

        def wait_taken(eng, m):
            eng.wait_ge(taken[m % BANKS], m // BANKS + 1)

        @block.sync
        def _(sp_):
            def load(c_static, c_expr, src, width=KT * P):
                if not isinstance(c_expr, int) or c_expr >= RING:
                    sp_.wait_ge(w_lo_ready, c_expr - (RING - 1))
                sp_.dma_start(raw[:, c_static % RING, 0:width], src).then_inc(raw_in[c_static % RING], 16)

            def load_ffn(base, pattern, loops, w_i, w_o):
                n_p, n_m = pattern.count("P"), pattern.count("M")
                with sp_.Fori(0, loops) as i:
                    for k, kind in enumerate(pattern):
                        before = pattern[:k].count(kind)
                        src = w_i[i * n_p + before] if kind == "P" else w_ada[i * n_m + (ADA_FIRST + before)]
                        load(base + k, i * len(pattern) + (base + k), src)
                base += loops * len(pattern)
                for n in range(loops * n_p, 2 * FT):
                    load(base, base, w_i[n])
                    base += 1
                with sp_.Fori(0, KT) as i:
                    for k, (k0, n) in enumerate(FFO_CHUNKS):
                        load(base + k, i * 3 + (base + k), w_o[i, :, k0 * P:(k0 + n) * P], n * P)

            sp_.dma_start(cs[:, :, :], cT).then_inc(cond_in, 16)
            for c in range(ADA_FIRST):
                if c == RING:
                    sp_.dma_start(badat[:, :], b_ada).then_inc(small_in, 16)
                    sp_.dma_start(vec[:, :, :], vecs).then_inc(small_in, 16)
                load(c, c, w_ada[c])
            load_ffn(C_FFI1, UP1, UP1_LOOPS, ff1_in, ff1_out)
            with sp_.Fori(0, NMIX // RING) as i:
                for k in range(RING):
                    load(C_MIX + k, i * RING + (C_MIX + k), w_mix[i * RING + k])
            for k in range(NMIX // RING * RING, NMIX):
                load(C_MIX + k, C_MIX + k, w_mix[k])
            load_ffn(C_FFI2, UP2, UP2_LOOPS, ff2_in, ff2_out)

        @block.gpsimd
        def _(pool):
            nc.gpsimd.memset(ident[:, :], 0.0).then_inc(sel0, 1)
            nc.gpsimd.memset(maskneg[:, :], 0.0).then_inc(sel0, 1)
            nc.gpsimd.memset(sel[:, :, :], 0.0).then_inc(sel0, 1)
            pool.wait_ge(sel0, 3)
            nc.gpsimd.affine_select(out=ident[:, :], in_=ident[:, :], compare_op=ALU.not_equal, fill=1.0,
                                    base=0, pattern=[[-1, P]], channel_multiplier=1).then_inc(const_ready, 1)
            nc.gpsimd.affine_select(out=maskneg[:, :], in_=maskneg[:, :], compare_op=ALU.is_ge, fill=NEG,
                                    base=0, pattern=[[1, P]], channel_multiplier=-1).then_inc(const_ready, 1)
            nc.gpsimd.affine_select(out=sel[:, :, :], in_=sel[:, :, :], compare_op=ALU.not_equal, fill=1.0,
                                    base=0, pattern=[[-1, HEADS], [0, P]], channel_multiplier=1
                                    ).then_inc(const_ready, 1)
            nc.gpsimd.memset(ones[:, :], 1.0).then_inc(const_ready, 1)
            nc.gpsimd.memset(eps_t[:, :], EPS).then_inc(const_ready, 1)

            pool.dma_start(cw[:, :, :], conv_w).then_inc(rg_in, 16)
            pool.dma_start(gb_t[:, :], gate_b).then_inc(rg_in, 16)
            pool.dma_start(stn[:, :, :, :], st_n).then_inc(rg_in, 16)
            pool.dma_start(stm[:, :], st_m).then_inc(rg_in, 16)
            pool.wait_ge(chunk_done, C_MIX)
            pool.dma_start(wrg[:, :, :, :], w_rg).then_inc(rg_in, 16)
            pool.dma_start(stc[:, :, :, :], st_conv).then_inc(rg_in, 16)
            pool.dma_start(sth[:, :, :], st_h).then_inc(rg_in, 16)

            def load_state(n):
                if n >= 4:
                    pool.wait_ge(c_out[n % 4], 16 * (n // 4))
                pool.dma_start(cst_c[:, n % 4, :, :], st_C[n].rearrange("p (d e) -> p d e", d=DT)
                               ).then_inc(c_in[n % 4], 16)

            def store_state(n):
                wait_taken(pool, JOB["V", n // NB, n % NB // 2])
                pool.dma_start(o_Cs[n].rearrange("p (d e) -> p d e", d=DT), cst_c[:, n % 4, :, :]
                               ).then_inc(c_out[n % 4], 16)

            for n in range(4):
                load_state(n)
            pool.wait_ge(lo_ready, S_HA + KT)
            pool.dma_start(o_convp, convp[:, :, :]).then_inc(state_out, 16)
            pool.dma_start(o_convs, convs[:, :, :, :]).then_inc(state_out, 16)
            pool.dma_start(o_h, hout[:, :, :]).then_inc(state_out, 16)
            for h in range(HEADS):
                for b in range(NB):
                    n = h * NB + b
                    store_state(n)
                    if n + 4 < HEADS * NB:
                        load_state(n + 4)
                for dt in range(DT):
                    wait_taken(pool, JOB["C", h, dt])
                    pool.dma_start(o_Cp[h, dt], cst[:, dt, :]).then_inc(cp_out, 16)
            pool.wait_ge(states_ready, HEADS)
            pool.dma_start(o_ns, stn[:, :, :, :]).then_inc(state_out, 16)
            pool.dma_start(o_m, row_m[:, NP_ - 1:T]).then_inc(state_out, 16)
            for kt in range(KT):
                pool.wait_ge(y_ready, kt + 1)
                pool.dma_start(yT[:, kt, :], tb[2 + kt % 2][:, :]).then_inc(y_out[kt % 2], 16)
            for i in range(2):
                pool.wait_ge(y_out[i], 16 * (KT // 2))
            pool.wait_ge(state_out, 16 * 5)
            pool.wait_ge(cp_out, 16 * HEADS * DT)
            for i in range(4):
                pool.wait_ge(c_out[i], 16 * (HEADS * NB // 4))

        @block.tensor
        def _(pe):
            def product(c, c_expr, t, t_half, xh, xl, k0, n, first=True, last=True, ready=None):
                pe.wait_ge(w_lo_ready, c_expr + 1)
                if first and not (isinstance(t_half, int) and t_half == 0):
                    pe.wait_ge(evac[t % 2], t_half)
                out = big[t % 2]
                wh, wl = w_h[c % RING], w_l[c % RING]
                for i in range(n):
                    if ready is not None:
                        pe.wait_ge(lo_ready, ready(k0 + i))
                    w = slice(i * P, (i + 1) * P)
                    for s, (a, b) in enumerate(((wh, xh), (wh, xl), (wl, xh))):
                        for hf in range(2):
                            ins = nc.tensor.matmul(out[:, hf, 0:HALF], a[:, w],
                                                   b[:, k0 + i, hf * HALF:(hf + 1) * HALF],
                                                   start=first and i == 0 and s == 0,
                                                   stop=last and i == n - 1 and s == 2)
                ins.then_inc(chunk_done, 1)

            def job(m):
                if m >= BANKS:
                    pe.wait_ge(taken[m % BANKS], m // BANKS)
                return bank[m % BANKS]

            def modulation(c, c_expr, out):
                pe.wait_ge(w_lo_ready, c_expr + 1)
                for kt in range(KT):
                    for s, w in enumerate((w_h[c % RING], w_l[c % RING])):
                        ins = nc.tensor.matmul(out, w[:, kt * P:(kt + 1) * P], cs_hl[:, kt, :],
                                               start=kt == 0 and s == 0, stop=kt == KT - 1 and s == 1)
                ins.then_inc(chunk_done, 1)

            def mod_columns(n):
                return slice(n * 2 * (NB + 1), (n + 1) * 2 * (NB + 1))

            def norm_sums(m, ssq_count):
                pe.wait_ge(ssq_ready, ssq_count)
                for hf in range(2):
                    b = job(m + hf)
                    nc.tensor.matmul(b[:, 0:HALF], ones[:, :], ssq[:, hf * HALF:(hf + 1) * HALF],
                                     start=True, stop=True).then_inc(job_done, 1)

            def ffn(cb, tbase, pattern, loops, s_xn, s_hid):
                def xn_split(kt):
                    return s_xn + 2 + kt

                n_p = pattern.count("P")

                def turn(i):
                    n = a = 0
                    for k, kind in enumerate(pattern):
                        c = cb + k
                        if kind == "P":
                            t = tbase + n
                            product(c, i * len(pattern) + c, t, i * (n_p // 2) + t // 2, xn_h, xn_l, 0, KT,
                                    ready=xn_split if k == 0 else None)
                            n += 1
                        else:
                            m = M_ADA1 + MOD_JOBS[a]
                            first = MOD_JOBS.index(MOD_JOBS[a])
                            if a == first:
                                pe.wait_ge(taken[m % BANKS], i + m // BANKS)
                            modulation(c, i * len(pattern) + c, bank[m % BANKS][:, mod_columns(a - first)])
                            a += 1

                first = 1 if tbase == 0 else 0
                if first:
                    turn(0)
                with pe.Fori(first, loops) as i:
                    turn(i)
                cb += loops * len(pattern)
                for n in range(loops * n_p, 2 * FT):
                    product(cb, cb, tbase + n, (tbase + n) // 2, xn_h, xn_l, 0, KT)
                    cb += 1
                tbase += 2 * FT
                pe.wait_ge(lo_ready, s_hid + FT - 1)
                with pe.Fori(0, KT // 2) as i:
                    for jj in range(2):
                        for k, (k0, n) in enumerate(FFO_CHUNKS):
                            product(cb + 3 * jj + k, i * 6 + (cb + 3 * jj + k), tbase + jj,
                                    i + (tbase + jj) // 2, hid_h, hid_l, k0, n, first=k == 0, last=k == 2,
                                    ready=(lambda kt: s_hid + FT) if k == 2 and jj == 0 else None)

            pe.wait_ge(cs_ready, 3)
            for c in range(ADA_FIRST):
                modulation(c, c, job(M_ADA0 + c // 2)[:, mod_columns(c % 2)])
            pe.wait_ge(const_ready, 5)
            norm_sums(M_NORM1, KT)
            ffn(C_FFI1, T_FFI1, UP1, UP1_LOOPS, S_XN1, S_HID1)
            norm_sums(M_NORM2, 2 * KT)

            def small_job(key):
                kind, a, b = key
                m = JOB[key]
                out = job(m)
                h = a
                if kind in ("rga", "rgi"):
                    pe.wait_ge(rg_in, 16 * 7)
                    pe.wait_ge(conv_done, a + 1)
                    ins = nc.tensor.matmul(out[:, 0:HALF], wrg[:, 0 if kind == "rga" else 1, a, :],
                                           rg_u[a % RG_BUFS][:, b * HALF:(b + 1) * HALF], start=True, stop=True)
                elif kind == "aT":
                    pe.wait_ge(rows_ready, 1)
                    for c in range(CH):
                        ins = nc.tensor.transpose(out[:, c * HEADS:(c + 1) * HEADS],
                                                  row_i[0:HEADS, c * P:(c + 1) * P], ident[0:HEADS, 0:HEADS])
                elif kind == "srow":
                    pe.wait_ge(row_exp, 1)
                    for hh in range(HEADS):
                        ins = nc.tensor.matmul(out[:, hh * 3 * NB:(hh + 1) * 3 * NB], sel[:, hh, :],
                                               rs[:, :, :].rearrange("h a b -> h (a b)"), start=True, stop=True)
                elif kind in ("kT", "vT"):
                    src = k_t[h % 2] if kind == "kT" else v_t
                    wait_evac(pe, T_OF[kind[0], DT * h + b])
                    for c in range(CH):
                        ins = nc.tensor.transpose(out[:, c * P:(c + 1) * P], src[:, b, c * P:(c + 1) * P],
                                                  ident[:, :])
                elif kind == "Bt":
                    ins = nc.tensor.matmul(out[:, 0:NP_], sel[:, h, :], row_f[:, 0:NP_], start=True, stop=True)
                elif kind == "em":
                    ins = nc.tensor.matmul(out[:, 0:NP_], sel[:, h, :], row_m[:, 0:NP_], start=True, stop=True)
                elif kind == "S":
                    for dt in range(DT):
                        ins = nc.tensor.matmul(out[:, b * P:NP_], k_t[h % 2][:, dt, b * P:(b + 1) * P],
                                               q_t[h % 2][:, dt, b * P:NP_], start=dt == 0, stop=dt == DT - 1)
                elif kind in ("den", "num"):
                    for c in range(CH):
                        wait_taken(pe, JOB["S", h, c])
                        if kind == "num":
                            wait_taken(pe, JOB["vT", h, b])
                        lhs = ones[:, :] if kind == "den" else vtok[:, c, b * P:(b + 1) * P]
                        ins = nc.tensor.matmul(out[:, c * P:NP_], lhs, dmat[:, c, c * P:NP_],
                                               start=c == 0, stop=c == CH - 1)
                elif kind == "C":
                    pe.wait_ge(vw_ready, 5 * (h + 1))
                    for c in range(CH):
                        ins = nc.tensor.matmul(out[:, 0:HD + 1], ktok[:, c, b * P:(b + 1) * P], vtok[:, c, :],
                                               start=c == 0, stop=c == CH - 1)
                elif kind == "sm":
                    if b == 0:
                        pe.wait_ge(prod_ready, 2 * (h + 1))
                        for g in range(2):
                            for dt in range(DT):
                                nc.tensor.matmul(out[:, g * NB:(g + 1) * NB], ones[:, :], prod[:, g, dt, :],
                                                 start=dt == 0, stop=dt == DT - 1)
                    for bb in range(4):
                        n = h * NB + 4 * b + bb
                        pe.wait_ge(c_in[n % 4], 16 * (n // 4 + 1))
                        for et in range(DT):
                            col = 2 * NB + et * 4 + bb
                            for dt in range(DT):
                                ins = nc.tensor.matmul(out[:, col:col + 1],
                                                       cst_c[:, n % 4, dt, et * P:(et + 1) * P],
                                                       sm[:, 0, dt, 4 * b + bb:4 * b + bb + 1],
                                                       start=dt == 0, stop=dt == DT - 1)
                elif kind == "V":
                    pe.wait_ge(prod_ready, 2 * (h + 1))
                    for bb in range(2):
                        for et in range(DT):
                            v_col = sm[:, 2, et, 2 * b + bb:2 * b + bb + 1]
                            ins = nc.tensor.matmul(out[:, bb * HD + et * P:bb * HD + (et + 1) * P],
                                                   v_col.broadcast_to([P, P]), ident[:, :],
                                                   start=True, stop=True)
                ins.then_inc(job_done, 1)

            for i, (what, j) in enumerate(MIX):
                if what == "bra":
                    xh, xl, base = hb_h, hb_l, S_HA
                elif what == "brb":
                    xh, xl, base = hb_h, hb_l, S_HB
                elif what == "out":
                    xh, xl, base = mg_h, mg_l, S_MG
                else:
                    xh, xl, base = xn_h, xn_l, S_XN2 + 1
                t = T_MIX + i
                product(C_MIX + i, C_MIX + i, t, t // 2, xh, xl, 0, KT,
                        ready=(lambda kt: base + kt + 1)
                        if i == 0 or (i == FIRST_OF[what] and what in ("bra", "brb", "out")) else None)
                for key in AFTER[i]:
                    small_job(key)
            norm_sums(M_NORM3, 3 * KT)
            ffn(C_FFI2, T_FFI2, UP2, UP2_LOOPS, S_XN3, S_HID2)
            norm_sums(M_NORM4, 4 * KT)

        @block.scalar
        def _(act):
            A = nc.scalar.activation
            own = [0]

            def link(ins):
                own[0] += 1
                ins.then_inc(ach, 1)
                act.wait_ge(ach, own[0])

            def split(c, c_expr, need, width=KT * P):
                act.wait_ge(raw_in[c % RING], need)
                if not isinstance(c_expr, int) or c_expr >= RING:
                    act.wait_ge(chunk_done, c_expr - (RING - 1))
                A(w_h[c % RING][:, 0:width], raw[:, c % RING, 0:width], ACT.Copy).then_inc(w_hi_ready, 1)

            def arrivals(c):
                return 16 * (c // RING + 1)

            def high(s, out, src):
                act.wait_ge(src_ready, sources(s) + 1)
                A(out, src, ACT.Copy).then_inc(hi_ready, 1)

            def squares(n, kt):
                if not isinstance(n, int) or n >= 1:
                    act.wait_ge(ssq_ready, n)
                A(tb[2][:, :], x[:, kt, :], ACT.Square).then_inc(sq_ready, 1)

            def root(m):
                for hf in range(2):
                    act.wait_ge(job_done, computed(m + hf))
                    A(rstd[:, hf * HALF:(hf + 1) * HALF], bank[(m + hf) % BANKS][:, 0:HALF], ACT.Sqrt,
                      bias=eps_t[:, :], scale=1.0 / D).then_inc(taken[(m + hf) % BANKS], 1)

            def norm(index, m, shift, s_base):
                root(m)
                high(s_base, xn_h[:, :, NP_:T], ys[:, :, :])
                act.wait_ge(gain_ready, index + 1)
                for kt in range(KT):
                    act.wait_ge(nrm_ready, index * KT + kt + 1)
                    if kt >= 2:
                        act.wait_ge(lo_ready, s_base + kt)
                    A(tb[2 + kt % 2][:, 0:NP_], tb[kt % 2][:, 0:NP_], ACT.Identity,
                      bias=mod[:, shift * KT + kt, 0:1], scale=gain[:, kt, 0:1]).then_inc(src_ready, 1)
                    high(s_base + 1 + kt, xn_h[:, kt, 0:NP_], tb[2 + kt % 2][:, 0:NP_])

            def ffn(cb, tbase, pattern, loops, s_hid, sq_base, x_base):
                n_p = pattern.count("P")

                def step(c, t, i, kind):
                    after = i * len(pattern)
                    split(c + LEAD, after + (c + LEAD),
                          i * (16 * len(pattern) // RING) + arrivals(c + LEAD))
                    if kind == "P" and t % 2 == tbase % 2:
                        act.wait_ge(chunk_done, after + (c + 1))
                        A(two(tb[0][:, :]), slot_view(t), ACT.Silu).then_inc(evac[t % 2], 1)
                    elif kind == "P":
                        act.wait_ge(evac[t % 2], i * (n_p // 2) + (t // 2 + 1))
                        A(hid_h[:, i * (n_p // 2) + (t - tbase) // 2, :], tb[1][:, :], ACT.Copy).then_inc(hi_ready, 1)

                with act.Fori(0, loops) as i:
                    for k, kind in enumerate(pattern):
                        step(cb + k, tbase + pattern[:k].count("P"), i, kind)
                cb += loops * len(pattern)
                for n in range(loops * n_p, 2 * FT):
                    step(cb, tbase + n, 0, "P")
                    cb += 1
                co = cb

                def turn(i):
                    for jj in range(2):
                        for k in range(3):
                            c = co + 3 * jj + k + LEAD
                            if isinstance(i, int) and i * 6 + c >= C_END:
                                continue
                            split(c, i * 6 + c, i * (16 * 6 // RING) + arrivals(c), FFO_CHUNKS[(k + LEAD) % 3][1] * P)
                        act.wait_ge(x_ready, i * 2 + (x_base + jj + 1))
                        squares(i * 2 + (sq_base + jj), i * 2 + jj)

                with act.Fori(0, KT // 2 - 1) as i:
                    turn(i)
                turn(KT // 2 - 1)

            for n in range(2):
                tiles = slice(n * KT // 2, (n + 1) * KT // 2)
                act.dma_start(x[:, tiles, :], xT[:, tiles, :]).then_inc(x_in, 16)
            act.wait_ge(cond_in, 16)
            A(cs[:, :, :], cs[:, :, :], ACT.Silu).then_inc(cs_ready, 1)
            act.wait_ge(cs_ready, 1)
            A(cs_hl[:, :, 0:NB + 1], cs[:, :, :], ACT.Copy).then_inc(cs_ready, 1)
            for c in range(ADA_FIRST + LEAD):
                split(c, c, arrivals(c))
                if c >= SQ_FROM and c < SQ_FROM + KT:
                    if c == SQ_FROM:
                        act.wait_ge(x_in, 32)
                    squares(c - SQ_FROM, c - SQ_FROM)
            act.wait_ge(const_ready, 5)
            norm(0, M_NORM1, SH1, S_XN1)
            ffn(C_FFI1, T_FFI1, UP1, UP1_LOOPS, S_HID1, KT, 0)
            norm(1, M_NORM2, SH2, S_XN2)

            act.wait_ge(sp_abs, 1)
            A(sp[:, 1, :], sp[:, 0, :], ACT.Exp, scale=-1.0).then_inc(exp_sp, 1)

            def take(key, out, in_, func, **kw):
                m = JOB[key]
                act.wait_ge(job_done, computed(m))
                return A(out, in_, func, **kw).then_inc(taken[m % BANKS], 1)

            def rg_gates(pair):
                act.wait_ge(lo_ready, S_HA + pair[0])
                for j in pair:
                    p = j % 2
                    for dst, kind, bias in ((rg_r, "rga", V_BA), (rg_i, "rgi", V_BI)):
                        for hf in range(2):
                            key = (kind, j, hf)
                            take(key, dst[p][:, hf * HALF:(hf + 1) * HALF], bank[JOB[key] % BANKS][:, 0:HALF],
                                 ACT.Sigmoid, bias=vec[:, bias, j:j + 1])
                for j in pair:
                    p = j % 2
                    wait_taken(act, JOB["rga", j, 0])
                    wait_taken(act, JOB["rga", j, 1])
                    A(rg_a[p][:, :], rg_r[p][:, :], ACT.Exp, scale=c8[:, 0, j:j + 1]).then_inc(rg_ra, 1)
                    act.wait_ge(rg_ra, 2 * j + 1)
                    A(rg_r[p][:, :], rg_r[p][:, :], ACT.Tanh, scale=c8[:, 1, j:j + 1]).then_inc(rg_ra, 1)
                for j in pair:
                    act.wait_ge(rg_w, j + 1)
                    A(rg_v[j % 2][:, :], rg_v[j % 2][:, :], ACT.Sqrt).then_inc(rg_sq, 1)

            def small_job(key):
                kind, h, b = key
                m = JOB[key]
                src = bank[m % BANKS]
                if kind in ("rga", "rgi"):
                    if (kind, h % 2, b) == ("rgi", 1, 1):
                        rg_gates((h - 1, h))
                elif kind == "kT":
                    take(key, ktok[:, :, b * P:(b + 1) * P], src[:, :].rearrange("p (c f) -> p c f", c=CH), ACT.Copy)
                elif kind == "vT":
                    take(key, vtok[:, :, b * P:(b + 1) * P], src[:, :].rearrange("p (c f) -> p c f", c=CH), ACT.Copy)
                    if b == 1:
                        wait_taken(act, JOB["Bt", h, 0])
                        for c in range(CH - 1):
                            A(dmat[:, c, (c + 1) * P:NP_], tb[0][:, (c + 1) * P:NP_], ACT.Exp,
                              bias=aT[:, c, h:h + 1]).then_inc(d_ready, 1)
                        act.wait_ge(diag_ready, CH * (h + 1))
                        for c in range(CH):
                            A(dmat[:, c, c * P:(c + 1) * P], tb[3][:, c * P:(c + 1) * P], ACT.Exp).then_inc(d_ready, 1)
                elif kind == "em":
                    if h:
                        act.wait_ge(cp_out, 16 * DT * h)
                    take(key, tb[1][:, 0:NP_], src[:, 0:NP_], ACT.Exp, scale=-1.0)
                elif kind == "C":
                    take(key, cst[:, b, :], src[:, 0:HD + 1], ACT.Copy)
                elif kind == "sm":
                    act.wait_ge(job_done, computed(m))
                    for bb in range(4):
                        n = h * NB + 4 * b + bb
                        A(cst_c[:, n % 4, :, :], cst_c[:, n % 4, :, :], ACT.Identity,
                          scale=rsb[:, h, 1, 4 * b + bb:4 * b + bb + 1]).then_inc(c_scaled, 1)

            for i, (what, j) in enumerate(MIX):
                c = C_MIX + i + LEAD
                split(c, c, arrivals(c))
                t = T_MIX + i
                act.wait_ge(chunk_done, C_MIX + i + 1)
                src = slot_view(t)
                e = evac[t % 2]
                if what == "gates":
                    act.wait_ge(rg_in, 16 * 7)
                    A(two(row_i[:, :]), big[t % 2][0:HEADS, :, 0:HALF], ACT.Identity,
                      bias=gb_t[0:HEADS, :]).then_inc(ach, 1)
                    own[0] += 1
                    act.wait_ge(ach, own[0])
                    A(two(row_f[:, :]), big[t % 2][32:32 + HEADS, :, 0:HALF], ACT.Identity,
                      bias=gb_t[32:32 + HEADS, :]).then_inc(e, 1)
                elif what == "xrg":
                    if j >= RG_BUFS:
                        act.wait_ge(conv_done, j - RG_BUFS + 1)
                    A(two(rg_x[j % RG_BUFS][:, CONV_W - 1:]), src, ACT.Copy).then_inc(e, 1)
                elif what in "qkv":
                    h, dt = divmod(j, DT)
                    if what == "v":
                        dst = v_t
                        if h == 0:
                            act.wait_ge(lo_ready, S_HA + KT)
                            act.wait_ge(state_out, 16 * 3)
                    else:
                        dst = (q_t if what == "q" else k_t)[h % 2]
                    A(two(dst[:, dt, :]), src, ACT.Copy).then_inc(e, 1)
                elif what == "gb" and j < EARLY:
                    A(two(sgb[j]), src, ACT.Sigmoid).then_inc(e, 1)
                elif what == "ga":
                    if j < 2:
                        act.wait_ge(lo_ready, S_HA + KT)
                    elif j < 5:
                        act.wait_ge(conv_done, KT)
                    A(two(ma[:, j, :]), src, ACT.Sigmoid).then_inc(e, 1)
                elif what in ("gb", "o"):
                    if what == "o":
                        act.wait_ge(src_ready, sources(S_HB) + j)
                    else:
                        wait_evac(act, T_OF["brb", j - 1])
                    A(two(tb[0 if what != "o" else 2][:, :]), src, ACT.Sigmoid).then_inc(e, 1)
                for jj in RG_SCAN.get(i, ()):
                    high(S_HA + jj, hb_h[:, jj, :], rg_u[jj % RG_BUFS])
                if what == "o":
                    high(S_HB + j, hb_h[:, j, :], hm[:, j % DT, :])
                elif what == "brb":
                    high(S_MG + j, mg_h[:, j, :], tb[1][:, :])
                elif what == "out":
                    act.wait_ge(x_ready, KT + j + 1)
                    squares(2 * KT + j, j)
                if i == F_EXP_AT:
                    act.wait_ge(f_abs, 1)
                    A(tb[3][0:HEADS, :], tb[3][0:HEADS, :], ACT.Exp, scale=-1.0).then_inc(f_exp, 1)
                elif i == ROW_EXP_AT:
                    act.wait_ge(row_arg, 1)
                    A(rs[:, :, :], rs[:, :, :], ACT.Exp).then_inc(row_exp, 1)
                for key in AFTER[i]:
                    small_job(key)

            norm(2, M_NORM3, SH3, S_XN3)
            act.wait_ge(state_out, 16 * 5)
            ffn(C_FFI2, T_FFI2, UP2, UP2_LOOPS, S_HID2, 3 * KT, 2 * KT)
            root(M_NORM4)

        @block.vector
        def _(dve):
            V = nc.vector
            own = [0]

            def link(ins):
                own[0] += 1
                ins.then_inc(dch, 1)
                dve.wait_ge(dch, own[0])

            def split(c, c_expr, width=KT * P):
                dve.wait_ge(w_hi_ready, c_expr + 1)
                V.tensor_tensor(w_l[c % RING][:, 0:width], raw[:, c % RING, 0:width],
                                w_h[c % RING][:, 0:width], ALU.subtract).then_inc(w_lo_ready, 1)

            def low(s, out, src, hi):
                dve.wait_ge(hi_ready, s + 1)
                V.tensor_tensor(out, src, hi, ALU.subtract).then_inc(lo_ready, 1)

            def add_squares(n, first):
                dve.wait_ge(sq_ready, n + 1)
                if first:
                    V.tensor_copy(ssq[:, :], tb[2][:, :]).then_inc(ssq_ready, 1)
                else:
                    dve.wait_ge(ssq_ready, n)
                    V.tensor_tensor(ssq[:, :], ssq[:, :], tb[2][:, :], ALU.add).then_inc(ssq_ready, 1)

            def mod_tiles(m, c_done, index, tile, n):
                dve.wait_ge(chunk_done, c_done)
                out = mod[:, bass.ds(tile, n), :]
                src = bank[m % BANKS][:, 0:n * 2 * (NB + 1)].rearrange("p (t a n) -> p t a n", t=n, a=2)
                V.tensor_tensor(out, src[:, :, 0, :],
                                badat[:, bass.ds(tile, n)].unsqueeze(2).broadcast_to([P, n, NB + 1]),
                                ALU.add).then_inc(mod_high, 1)
                dve.wait_ge(mod_high, index + 1)
                V.tensor_tensor(out, out, src[:, :, 1, :], ALU.add).then_inc(taken[m % BANKS], 1)

            def set_gain(index, scale, g, last_job):
                if last_job is not None:
                    for m in range(last_job - BANKS, last_job):
                        wait_taken(dve, m)
                V.scalar_tensor_tensor(gain[:, :, :], mod[:, scale * KT:(scale + 1) * KT, :], 1.0,
                                       vec[:, g, :].unsqueeze(2).broadcast_to([P, KT, NB + 1]),
                                       ALU.add, ALU.mult).then_inc(gain_ready, 1)
                dve.wait_ge(gain_ready, index + 1)

            def inverse_root(m):
                for hf in range(2):
                    wait_taken(dve, m + hf)
                    s = slice(hf * HALF, (hf + 1) * HALF)
                    link(V.reciprocal(rstd[:, s], rstd[:, s]))

            def norm(index, m, shift, s_base):
                inverse_root(m)
                link(V.tensor_tensor(ys[:, :, :], x[:, :, NP_:T],
                                     rstd[:, NP_:T].unsqueeze(1).broadcast_to([P, KT, NB]), ALU.mult))
                link(V.tensor_tensor(ys[:, :, :], ys[:, :, :], gain[:, :, 1:], ALU.mult))
                V.tensor_tensor(ys[:, :, :], ys[:, :, :], mod[:, shift * KT:(shift + 1) * KT, 1:],
                                ALU.add).then_inc(src_ready, 1)
                def prompt(kt):
                    if kt >= 2:
                        dve.wait_ge(src_ready, sources(s_base) + kt)
                    V.tensor_tensor(tb[kt % 2][:, 0:NP_], x[:, kt, 0:NP_], rstd[:, 0:NP_],
                                    ALU.mult).then_inc(nrm_ready, 1)
                prompt(0)
                prompt(1)
                low(s_base, xn_l[:, :, NP_:T], ys[:, :, :], xn_h[:, :, NP_:T])
                for kt in range(KT):
                    low(s_base + 1 + kt, xn_l[:, kt, 0:NP_], tb[2 + kt % 2][:, 0:NP_], xn_h[:, kt, 0:NP_])
                    if kt + 2 < KT:
                        prompt(kt + 2)

            def add_gated(t, kt, gate, ready_count):
                big_t = big[t % 2]
                V.scalar_tensor_tensor(x[:, kt, 0:HALF], big_t[:, 0, 0:HALF], mod[:, gate, 0:1],
                                       x[:, kt, 0:HALF], ALU.mult, ALU.add)
                V.scalar_tensor_tensor(x[:, kt, HALF:NP_], big_t[:, 1, 0:NP_ - HALF], mod[:, gate, 0:1],
                                       x[:, kt, HALF:NP_], ALU.mult, ALU.add)
                V.tensor_tensor(tmp8[:, :], big_t[:, 1, NP_ - HALF:HALF], mod[:, gate, 1:],
                                ALU.mult).then_inc(evac[t % 2], 1)
                dve.wait_ge(evac[t % 2], ready_count)
                V.tensor_tensor(x[:, kt, NP_:T], x[:, kt, NP_:T], tmp8[:, :], ALU.add).then_inc(x_ready, 1)

            def ffn(cb, tbase, pattern, loops, s_hid, gate, sq_base):
                n_p = pattern.count("P")

                def step(c, t, i, kind, a):
                    after, third = i * len(pattern), i * (n_p // 2)
                    split(c + LEAD, after + (c + LEAD))
                    if kind == "P" and t % 2 != tbase % 2:
                        j = (t - tbase) // 2
                        dve.wait_ge(chunk_done, after + (c + 1))
                        dve.wait_ge(evac[(t - 1) % 2], third + ((t - 1) // 2 + 1))
                        dve.wait_ge(lo_ready, third + (s_hid + j))
                        V.tensor_tensor(two(tb[1][:, :]), two(tb[0][:, :]), slot_view(t),
                                        ALU.mult).then_inc(evac[t % 2], 1)
                        low(third + (s_hid + j), hid_l[:, third + j, :], tb[1][:, :], hid_h[:, third + j, :])
                    elif kind == "M" and MOD_JOBS[a] not in MOD_JOBS[a + 1:]:
                        first = MOD_JOBS.index(MOD_JOBS[a])
                        m = M_ADA1 + MOD_JOBS[a]
                        mod_tiles(m, after + (c + 1), i * BANKS + (M_NORM1 + MOD_JOBS[a]), i * len(MOD_JOBS) + (ADA_FIRST + first), a + 1 - first)

                with dve.Fori(0, loops) as i:
                    for k, kind in enumerate(pattern):
                        step(cb + k, tbase + pattern[:k].count("P"), i, kind, pattern[:k].count("M"))
                cb += loops * len(pattern)
                for n in range(loops * n_p, 2 * FT):
                    step(cb, tbase + n, 0, "P", 0)
                    cb += 1
                co = cb
                to = tbase + 2 * FT
                if tbase == T_FFI1:
                    for m in range(M_NORM2 - BANKS, M_NORM2):
                        wait_taken(dve, m)
                link(V.tensor_scalar(mod[:, gate:gate + KT, :], mod[:, gate:gate + KT, :], 0.5, None, ALU.mult))
                link(V.memset(ssq[:, :], 0.0))

                def turn(i):
                    for jj in range(2):
                        for k in range(3):
                            c = co + 3 * jj + k + LEAD
                            if isinstance(i, int) and i * 6 + c >= C_END:
                                continue
                            split(c, i * 6 + c, FFO_CHUNKS[(k + LEAD) % 3][1] * P)
                        dve.wait_ge(chunk_done, i * 6 + (co + 3 * jj + 3))
                        add_gated(to + jj, i * 2 + jj, i * 2 + (jj + gate), i + ((to + jj) // 2 + 1))
                        add_squares(i * 2 + (sq_base + jj), False)

                with dve.Fori(0, KT // 2 - 1) as i:
                    turn(i)
                turn(KT // 2 - 1)

            def log1p_times2z(z, z2, p):
                link(V.tensor_tensor(z2, z, z, ALU.mult))
                link(V.tensor_scalar(p, z2, 1.0 / 19, None, ALU.mult))
                for n in range(17, 1, -2):
                    link(V.scalar_tensor_tensor(p, p, 1.0 / n, z2, ALU.add, ALU.mult))
                link(V.scalar_tensor_tensor(p, p, 1.0, z, ALU.add, ALU.mult))
                link(V.tensor_scalar(p, p, 2.0, None, ALU.mult))

            dve.wait_ge(cs_ready, 2)
            V.tensor_tensor(cs_hl[:, :, NB + 1:], cs[:, :, :], cs_hl[:, :, 0:NB + 1],
                            ALU.subtract).then_inc(cs_ready, 1)
            for c in range(ADA_FIRST + LEAD):
                split(c, c)
                if c >= SQ_FROM and c < SQ_FROM + KT:
                    add_squares(c - SQ_FROM, c == SQ_FROM)
                done = c - LEAD + 1
                if done > 0 and (done % 2 == 0 or done == ADA_FIRST):
                    first = (done - 1) // 2 * 2
                    if first == 0:
                        dve.wait_ge(small_in, 16 * 2)
                    mod_tiles(M_ADA0 + first // 2, done, first // 2, first, done - first)
            set_gain(0, SC1, V_G1, M_NORM1)
            norm(0, M_NORM1, SH1, S_XN1)
            ffn(C_FFI1, T_FFI1, UP1, UP1_LOOPS, S_HID1, GA1 * KT, KT)
            set_gain(1, SC2, V_G2, None)
            norm(1, M_NORM2, SH2, S_XN2)

            lam = vec[:, V_LAM, :]
            V.scalar_tensor_tensor(sp[:, 0, :], lam, -1.0, lam, ALU.mult, ALU.max).then_inc(sp_abs, 1)
            for xr in rg_x:
                V.memset(xr[:, 0:CONV_W - 1], 0.0)
            dve.wait_ge(exp_sp, 1)
            link(V.tensor_scalar(sp[:, 2, :], sp[:, 1, :], 2.0, None, ALU.add))
            link(V.reciprocal(sp[:, 2, :], sp[:, 2, :]))
            link(V.tensor_tensor(sp[:, 2, :], sp[:, 2, :], sp[:, 1, :], ALU.mult))
            log1p_times2z(sp[:, 2, :], sp[:, 3, :], sp[:, 1, :])
            link(V.tensor_scalar(sp[:, 0, :], lam, -1.0, 0.0, ALU.mult, ALU.max))
            link(V.tensor_tensor(sp[:, 0, :], sp[:, 0, :], sp[:, 1, :], ALU.add))
            link(V.tensor_scalar(c8[:, 0, :], sp[:, 0, :], -8.0, None, ALU.mult))
            link(V.tensor_scalar(c8[:, 1, :], sp[:, 0, :], 8.0, None, ALU.mult))

            def conv(j):
                xr, u = rg_x[j % RG_BUFS], rg_u[j % RG_BUFS]
                wait_evac(dve, T_OF["xrg", j])
                if j == 0:
                    dve.wait_ge(rg_in, 16 * 7)
                if j >= RG_BUFS:
                    dve.wait_ge(lo_ready, S_HA + j - RG_BUFS + 1)
                NC = CONV_W - 1
                for w in range(CONV_W):
                    tap = cw[:, j, w:w + 1]
                    new = xr[:, NC + NP_:NC + T] if w == NC else stc[:, j, w, :]
                    if w == 0:
                        V.tensor_scalar(u[:, 0:NP_], xr[:, 0:NP_], tap, vec[:, V_CB, j:j + 1], ALU.mult, ALU.add)
                        link(V.tensor_scalar(u[:, NP_:T], new, tap, vec[:, V_CB, j:j + 1], ALU.mult, ALU.add))
                    else:
                        V.scalar_tensor_tensor(u[:, 0:NP_], xr[:, w:w + NP_], tap, u[:, 0:NP_], ALU.mult, ALU.add)
                        link(V.scalar_tensor_tensor(u[:, NP_:T], new, tap, u[:, NP_:T], ALU.mult, ALU.add))
                V.tensor_copy(convp[:, j, :], xr[:, NP_:NP_ + NC])
                V.tensor_copy(convs[:, j, 0:NC - 1, :], stc[:, j, 1:NC, :])
                V.tensor_copy(convs[:, j, NC - 1, :], xr[:, NC + NP_:NC + T]).then_inc(conv_done, 1)

            def rg_weight(j):
                p = j % 2
                a, v, th = rg_a[p], rg_v[p], rg_r[p]
                dve.wait_ge(rg_ra, 2 * j + 2)
                link(V.tensor_tensor(v[:, :], a[:, :], a[:, :], ALU.mult))
                V.scalar_tensor_tensor(v[:, :], v[:, :], 1.0, th[:, :], ALU.add, ALU.mult).then_inc(rg_w, 1)

            def rg_scan(j):
                p = j % 2
                a, v, u, ig = rg_a[p], rg_v[p], rg_u[j % RG_BUFS], rg_i[p]
                for hf in range(2):
                    wait_taken(dve, JOB["rgi", j, hf])
                link(V.tensor_tensor(ig[:, :], ig[:, :], u[:, :], ALU.mult))
                dve.wait_ge(rg_sq, j + 1)
                link(V.tensor_tensor(ig[:, :], ig[:, :], v[:, :], ALU.mult))
                V.tensor_tensor_scan(u[:, 0:NP_], a[:, 0:NP_], ig[:, 0:NP_], 0.0, ALU.mult, ALU.add)
                link(V.tensor_tensor(u[:, NP_:T], a[:, NP_:T], sth[:, j, :], ALU.mult))
                link(V.tensor_tensor(u[:, NP_:T], u[:, NP_:T], ig[:, NP_:T], ALU.add))
                V.tensor_copy(hout[:, j, :], u[:, NP_ - 1:T]).then_inc(src_ready, 1)

            def rg_low(j):
                low(S_HA + j, hb_l[:, j, :], rg_u[j % RG_BUFS], hb_h[:, j, :])

            def gate_rows(stage):
                f, ig, m = row_f[:, :], row_i[:, :], row_m[:, :]
                t1, t2, t3 = (t[0:HEADS, :] for t in tb[1:])
                s = slice(NP_, T)
                if stage == 0:
                    wait_evac(dve, T_OF["gates", 0])
                    V.scalar_tensor_tensor(t3, f, -1.0, f, ALU.mult, ALU.max).then_inc(f_abs, 1)
                elif stage == 1:
                    dve.wait_ge(f_exp, 1)
                    link(V.tensor_scalar(t1, t3, 2.0, None, ALU.add))
                    link(V.reciprocal(t1, t1))
                    link(V.tensor_tensor(t1, t1, t3, ALU.mult))
                elif stage == 2:
                    log1p_times2z(t1, t2, t3)
                elif stage == 3:
                    link(V.scalar_tensor_tensor(f, f, 0.0, t3, ALU.min, ALU.subtract))
                    link(V.tensor_tensor_scan(m[:, 0:NP_], f[:, 0:NP_], ig[:, 0:NP_], 0.0, ALU.add, ALU.max))
                    link(V.memset(t2[:, 0:NP_], 0.0))
                    link(V.tensor_tensor_scan(t1[:, 0:NP_], f[:, 0:NP_], t2[:, 0:NP_], 0.0, ALU.add, ALU.add))
                    link(V.tensor_tensor(t1[:, s], f[:, s], stm[:, :], ALU.add))
                    link(V.tensor_tensor(m[:, s], t1[:, s], ig[:, s], ALU.max))
                    link(V.tensor_tensor(rs[:, 0, :], ig[:, s], m[:, s], ALU.subtract))
                    link(V.tensor_tensor(rs[:, 1, :], t1[:, s], m[:, s], ALU.subtract))
                    V.tensor_scalar(rs[:, 2, :], m[:, s], -1.0, None, ALU.mult).then_inc(row_arg, 1)
                else:
                    link(V.tensor_tensor(f[:, 0:NP_], t1[:, 0:NP_], m[:, 0:NP_], ALU.subtract))
                    V.tensor_tensor(ig[:, 0:NP_], ig[:, 0:NP_], t1[:, 0:NP_], ALU.subtract).then_inc(rows_ready, 1)

            def sample_products(h):
                p = h % 2
                if h:
                    wait_taken(dve, JOB["V", h - 1, 3])
                for n, src, w in ((0, q_t[p], "q"), (1, k_t[p], "k"), (2, v_t, "v")):
                    for dt in range(DT):
                        wait_evac(dve, T_OF[w, DT * h + dt])
                    link(V.tensor_copy(sm[:, n, :, :], src[:, :, NP_:T]))
                V.tensor_tensor(prod[:, 0, :, :], sm[:, 0, :, :], sm[:, 1, :, :], ALU.mult).then_inc(prod_ready, 1)
                V.tensor_tensor(prod[:, 1, :, :], sm[:, 0, :, :], stn[:, h, :, :], ALU.mult).then_inc(prod_ready, 1)
                dve.wait_ge(prod_ready, 2 * (h + 1))
                link(V.tensor_tensor(kd[:, :, :], sm[:, 1, :, :],
                                     rsb[:, h, 0, :].unsqueeze(1).broadcast_to([P, DT, NB]), ALU.mult))
                link(V.tensor_tensor(stn[:, h, :, :], stn[:, h, :, :],
                                     rsb[:, h, 1, :].unsqueeze(1).broadcast_to([P, DT, NB]), ALU.mult))
                V.tensor_tensor(stn[:, h, :, :], stn[:, h, :, :], kd[:, :, :], ALU.add).then_inc(states_ready, 1)

            def sample_outputs(h):
                wi, wp, em = (rsb[:, h, n, :] for n in range(3))
                s, den = s8[:, 0, :], s8[:, 1, :]
                link(V.scalar_tensor_tensor(s, sres[:, 0, :], QSCALE, wi, ALU.mult, ALU.mult))
                link(V.scalar_tensor_tensor(den, sres[:, 1, :], QSCALE, wp, ALU.mult, ALU.mult))
                link(V.tensor_tensor(den, den, s, ALU.add))
                link(V.scalar_tensor_tensor(s8[:, 2, :], den, -1.0, em, ALU.mult, ALU.max))
                link(V.tensor_tensor(den, den, s8[:, 2, :], ALU.max))
                link(V.reciprocal(den, den))
                for et in range(DT):
                    num, sv = sres[:, 2 + et, :], s8[:, 2 + et, :]
                    link(V.scalar_tensor_tensor(num, num, QSCALE, wp, ALU.mult, ALU.mult))
                    link(V.tensor_tensor(sv, s, sm[:, 2, et, :], ALU.mult))
                    link(V.tensor_tensor(num, num, sv, ALU.add))
                    link(V.tensor_tensor(hm[:, et, NP_:T], num, den, ALU.mult))

            def small_job(key):
                kind, h, b = key
                m = JOB[key]
                src = bank[m % BANKS]

                def done():
                    dve.wait_ge(job_done, computed(m))

                free = taken[m % BANKS]
                if kind == "aT":
                    done()
                    V.tensor_copy(aT[:, :, :], src[:, 0:CH * HEADS].rearrange("p (c h) -> p c h", c=CH)
                                  ).then_inc(free, 1)
                elif kind == "srow":
                    done()
                    V.tensor_copy(rsb[:, :, :, :], src[:, 0:HEADS * 3 * NB].rearrange("p (h a b) -> p h a b", h=HEADS, a=3)
                                  ).then_inc(free, 1)
                elif kind == "Bt":
                    if h:
                        dve.wait_ge(d_ready, (2 * CH - 1) * h)
                        wait_taken(dve, JOB["num", h - 1, 1])
                    done()
                    V.tensor_copy(tb[0][:, 0:NP_], src[:, 0:NP_]).then_inc(free, 1)
                    wait_taken(dve, m)
                    for c in range(CH):
                        cc = slice(c * P, (c + 1) * P)
                        V.scalar_tensor_tensor(tb[3][:, cc], tb[0][:, cc], aT[:, c, h:h + 1], maskneg[:, :],
                                               ALU.add, ALU.add).then_inc(diag_ready, 1)
                elif kind == "vT" and b == 1:
                    sample_products(h)
                elif kind == "S":
                    if b == 0:
                        dve.wait_ge(d_ready, (2 * CH - 1) * (h + 1))
                        if h:
                            dve.wait_ge(vw_ready, 5 * h)
                        link(V.tensor_copy(wcol[:, :], dmat[:, :, NP_ - 1]))
                    done()
                    V.scalar_tensor_tensor(dmat[:, b, b * P:NP_], src[:, b * P:NP_], QSCALE, dmat[:, b, b * P:NP_],
                                           ALU.mult, ALU.mult).then_inc(free, 1)
                elif kind == "den":
                    done()
                    wait_taken(dve, JOB["em", h, 0])
                    link(V.scalar_tensor_tensor(tb[3][:, 0:NP_], src[:, 0:NP_], -1.0, tb[1][:, 0:NP_], ALU.mult, ALU.max))
                    V.tensor_tensor(tb[3][:, 0:NP_], src[:, 0:NP_], tb[3][:, 0:NP_], ALU.max).then_inc(free, 1)
                    wait_taken(dve, m)
                    link(V.reciprocal(tb[3][:, 0:NP_], tb[3][:, 0:NP_]))
                elif kind == "num":
                    if h:
                        dve.wait_ge(lo_ready, S_HB + DT * h)
                    done()
                    V.tensor_tensor(hm[:, b, 0:NP_], src[:, 0:NP_], tb[3][:, 0:NP_], ALU.mult).then_inc(free, 1)
                    wait_taken(dve, m)
                    if b == 1:
                        for c in range(CH):
                            V.tensor_scalar(vtok[:, c, 0:HD], vtok[:, c, 0:HD], wcol[:, c:c + 1], None,
                                            ALU.mult).then_inc(vw_ready, 1)
                        V.tensor_copy(vtok[:, :, HD], wcol[:, :]).then_inc(vw_ready, 1)
                elif kind == "sm":
                    done()
                    if b == 0:
                        V.tensor_copy(sres[:, 0:2, :], src[:, 0:2 * NB].rearrange("p (g b) -> p g b", g=2))
                    V.tensor_copy(sres[:, 2:4, 4 * b:4 * b + 4],
                                  src[:, 2 * NB:2 * NB + 2 * 4].rearrange("p (e b) -> p e b", e=DT)).then_inc(free, 1)
                    wait_taken(dve, m)
                    if b == 1:
                        sample_outputs(h)
                elif kind == "V":
                    done()
                    for bb in range(2):
                        n = h * NB + 2 * b + bb
                        dve.wait_ge(c_scaled, n + 1)
                        for dt in range(DT):
                            ins = V.scalar_tensor_tensor(cst_c[:, n % 4, dt, :], src[:, bb * HD:(bb + 1) * HD],
                                                         kd[:, dt, 2 * b + bb:2 * b + bb + 1],
                                                         cst_c[:, n % 4, dt, :], ALU.mult, ALU.add)
                    ins.then_inc(free, 1)

            for i, (what, j) in enumerate(MIX):
                c = C_MIX + i + LEAD
                split(c, c)
                t = T_MIX + i
                for jj in RG_SCAN.get(i, ()):
                    rg_scan(jj)
                    rg_low(jj)
                if what == "xrg":
                    conv(j)
                elif what == "bra":
                    dve.wait_ge(chunk_done, C_MIX + i + 1)
                    wait_evac(dve, T_OF["ga", j])
                    V.tensor_tensor(two(ma[:, j, :]), two(ma[:, j, :]), slot_view(t), ALU.mult).then_inc(evac[t % 2], 1)
                elif what == "brb":
                    dve.wait_ge(chunk_done, C_MIX + i + 1)
                    wait_evac(dve, T_OF["gb", j])
                    if j:
                        dve.wait_ge(lo_ready, S_MG + j)
                    else:
                        dve.wait_ge(cp_out, 16 * DT * HEADS)
                    gate = sgb[j] if j < EARLY else tb[0][:, :]
                    V.tensor_tensor(two(tb[1][:, :]), two(gate), slot_view(t), ALU.mult).then_inc(evac[t % 2], 1)
                    wait_evac(dve, t)
                    V.tensor_tensor(tb[1][:, :], tb[1][:, :], ma[:, j, :], ALU.add).then_inc(src_ready, 1)
                    low(S_MG + j, mg_l[:, j, :], tb[1][:, :], mg_h[:, j, :])
                elif what == "o":
                    wait_evac(dve, t)
                    V.tensor_tensor(hm[:, j % DT, :], hm[:, j % DT, :], tb[2][:, :], ALU.mult).then_inc(src_ready, 1)
                    low(S_HB + j, hb_l[:, j, :], hm[:, j % DT, :], hb_h[:, j, :])
                elif what == "out":
                    dve.wait_ge(chunk_done, C_MIX + i + 1)
                    add_gated(t, j, GA2 * KT + j, t // 2 + 1)
                    add_squares(2 * KT + j, j == 0)
                if i in ROWS_AT:
                    gate_rows(ROWS_AT[i])
                for key in AFTER[i]:
                    small_job(key)
                for jj in RG_AT.get(i, ()):
                    rg_weight(jj)

            set_gain(2, SC3, V_G3, None)
            norm(2, M_NORM3, SH3, S_XN3)
            dve.wait_ge(state_out, 16 * 5)
            ffn(C_FFI2, T_FFI2, UP2, UP2_LOOPS, S_HID2, GA3 * KT, 3 * KT)
            inverse_root(M_NORM4)
            for kt in range(KT):
                if kt >= 2:
                    dve.wait_ge(y_out[kt % 2], 16 * (kt // 2))
                V.scalar_tensor_tensor(tb[2 + kt % 2][:, :], x[:, kt, :], vec[:, V_GF, kt:kt + 1], rstd[:, :],
                                       ALU.mult, ALU.mult).then_inc(y_ready, 1)


RG_SCAN = {at + 1 + n: (pair[n],) for at, pair in RG_AT.items() for n in range(2)}


def _tiles(w):
    w = np.asarray(w)
    k, n = w.shape
    return np.ascontiguousarray(w.reshape(k // P, P, n // P, P).transpose(2, 1, 0, 3)).reshape(n // P, P, k)


def _features(a):
    a = np.asarray(a)
    lead = a.shape[:-1]
    a = a.reshape(lead + (KT, P))
    return np.ascontiguousarray(np.moveaxis(np.moveaxis(a, -1, 0), -1, 1))


def kernel(**inputs):
    import concourse.bacc as bacc
    from concourse.bass_utils import run_bass_kernel_spmd

    g = {k: np.asarray(v) for k, v in inputs.items()}
    f32 = np.float32
    x_all = np.concatenate([g["x_prompt"][0], g["x_sample"][:, 0]], 0)
    c_all = np.concatenate([g["c_prompt"], g["c_sample"]], 0)
    w_in = g["w_in"][0]
    q0, k0, v0, o0 = (D * n for n in (1, 2, 3, 4))
    i0 = 5 * D
    f0 = i0 + HEADS
    a0 = f0 + HEADS
    b0 = a0 + D
    gates = np.zeros((D, P), f32)
    gates[:, 0:HEADS] = w_in[:, i0:i0 + HEADS]
    gates[:, 32:32 + HEADS] = w_in[:, f0:f0 + HEADS]
    sources = {
        "gates": gates, "xrg": w_in[:, 0:D], "q": w_in[:, q0:q0 + D], "k": w_in[:, k0:k0 + D],
        "v": w_in[:, v0:v0 + D], "o": w_in[:, o0:o0 + D], "ga": w_in[:, a0:a0 + D], "gb": w_in[:, b0:b0 + D],
        "bra": g["w_br_a"][0], "brb": g["w_br_b"][0], "out": g["w_out"][0],
    }
    tiled = {k: _tiles(w) for k, w in sources.items()}
    w_mix = np.stack([tiled[what][j] for what, j in MIX])

    def up(w):
        t = _tiles(w)
        return np.ascontiguousarray(np.stack([t[:FT], t[FT:]], 1)).reshape(2 * FT, P, D)

    gate_b = np.zeros((P, 1), f32)
    gate_b[0:HEADS, 0] = g["b_ig"][0]
    gate_b[32:32 + HEADS, 0] = g["b_fg"][0]
    vecs = np.stack([g["g_norm1"][0], g["g_norm2"][0], g["g_norm3"][0], g["g_final"], g["conv_b"][0],
                     g["b_rg_a"][0], g["b_rg_i"][0], g["rg_lambda"][0]])
    arrays = {
        "xT": _features(x_all),
        "cT": _features(c_all),
        "w_ada": _tiles(g["w_ada"][0]),
        "b_ada": np.ascontiguousarray(g["b_ada"][0].reshape(NMOD * KT, P).T),
        "ff1_in": up(g["w_ff1_in"][0]),
        "ff1_out": _tiles(g["w_ff1_out"][0]),
        "w_mix": w_mix,
        "ff2_in": up(g["w_ff2_in"][0]),
        "ff2_out": _tiles(g["w_ff2_out"][0]),
        "vecs": np.ascontiguousarray(_features(vecs).transpose(0, 2, 1)),
        "conv_w": _features(g["conv_w"][0]),
        "w_rg": np.ascontiguousarray(np.stack([g["w_rg_a"][0], g["w_rg_i"][0]]).transpose(2, 0, 1, 3)),
        "gate_b": gate_b,
        "st_conv": np.ascontiguousarray(_features(g["state_conv"][0]).transpose(0, 1, 3, 2)),
        "st_h": _features(g["state_rg_h"][0]),
        "st_C": np.ascontiguousarray(
            g["state_C"][0].reshape(NB, HEADS, DT, P, HD).transpose(1, 0, 3, 2, 4)).reshape(HEADS * NB, P, DT * HD),
        "st_n": np.ascontiguousarray(g["state_n"][0].reshape(NB, HEADS, DT, P).transpose(3, 1, 2, 0)),
        "st_m": np.ascontiguousarray(g["state_m"][0].T),
    }
    outs = {
        "yT": (P, KT, T), "o_convp": (P, KT, CONV_W - 1), "o_convs": (P, KT, CONV_W - 1, NB),
        "o_h": (P, KT, NB + 1), "o_Cp": (HEADS, DT, P, HD + 1), "o_Cs": (HEADS * NB, P, DT * HD),
        "o_ns": (P, HEADS, DT, NB), "o_m": (HEADS, NB + 1),
    }
    nc = bacc.Bacc("TRN2", target_bir_lowering=False, num_devices=1)
    args = [nc.dram_tensor(n, a.shape, F32, kind="ExternalInput").ap() for n, a in arrays.items()]
    args += [nc.dram_tensor(n, s, F32, kind="ExternalOutput").ap() for n, s in outs.items()]
    build(nc, *args)
    r = run_bass_kernel_spmd(nc, [arrays], core_ids=[0]).results[0]

    def tokens(a):
        return np.ascontiguousarray(a.transpose(2, 1, 0)).reshape(a.shape[2], D)

    y = tokens(r["yT"])
    y_p, y_s = y[None, :NP_], y[NP_:, None]
    conv_p = tokens(r["o_convp"])[None, None]
    conv_s = np.ascontiguousarray(r["o_convs"].transpose(3, 2, 1, 0)).reshape(1, NB, CONV_W - 1, D)
    hh = tokens(r["o_h"])
    h_p, h_s = hh[None, 0:1], hh[None, 1:]
    cp = r["o_Cp"].reshape(HEADS, HD, HD + 1)
    C_p = np.ascontiguousarray(cp[None, None, :, :, :HD])
    n_p = np.ascontiguousarray(cp[None, None, :, :, HD])
    C_s = np.ascontiguousarray(
        r["o_Cs"].reshape(HEADS, NB, P, DT, HD).transpose(1, 0, 3, 2, 4)).reshape(1, NB, HEADS, HD, HD)
    n_s = np.ascontiguousarray(r["o_ns"].transpose(3, 1, 2, 0)).reshape(1, NB, HEADS, HD)
    m_p = np.ascontiguousarray(r["o_m"][:, 0])[None, None]
    m_s = np.ascontiguousarray(r["o_m"][:, 1:].T)[None]
    return tuple(np.ascontiguousarray(a) for a in
                 (y_p, y_s, conv_p, h_p, C_p, n_p, m_p, conv_s, h_s, C_s, n_s, m_s))
```

```python
from contextlib import ExitStack

import numpy as np

import concourse.bass as bass
from concourse import mybir
from concourse.alu_op_type import AluOpType as ALU

F32 = mybir.dt.float32
F32R = mybir.dt.float32r
ACT = mybir.ActivationFunctionType

P = 128
D = 1024
KT = D // P
NP_ = 512
NB = 8
T = NP_ + NB
HALF = T // 2
D_FF = 2816
FT = D_FF // P
HEADS = 4
DT = 2
HD = DT * P
CH = NP_ // P
CONV_W = 4
NMOD = 9
NR = 2 * (NB + 1)
EPS = 1e-6
QSCALE = HD ** -0.5
NEG = -1e30

RING = 3
LEAD = 2
BANKS = 4

ADA_FIRST = 2 * KT + 1
UP1 = "PMPMPMPMM"
UP2 = "PPPPPP"
URGENT = 7
UP1_LOOPS, UP2_LOOPS = 2 * FT // 4, 2 * FT // 6
SQ_FROM = 6
MOD_GROUPS = ((0, 3), (3, 2))
TURN_BACK = 2
FFO_CHUNKS = ((0, 8), (8, 8), (16, 6))

(SH1, SC1, GA1, SH2, SC2, GA2, SH3, SC3, GA3) = range(NMOD)
(V_G1, V_G2, V_G3, V_GF, V_CB, V_BA, V_BI, V_LAM, NVEC) = range(9)

RG_BUFS = 4
MIX = [("gates", 0)]
for _p, _keys in enumerate([[("q", 0)], [("q", 1), ("ga", 5)], [("k", 0), ("ga", 6)], [("k", 1), ("ga", 7)]]):
    MIX += [("xrg", 2 * _p), ("xrg", 2 * _p + 1)] + _keys
MIX += [("ga", 2), ("ga", 3), ("ga", 4)] + [("bra", _j) for _j in (5, 6, 7, 2, 3, 4)]
MIX += [("ga", 0), ("bra", 0), ("ga", 1), ("bra", 1)]
MIX += [("v", 0), ("v", 1)]
EARLY = 4
for _h in range(HEADS):
    if _h + 1 < HEADS:
        for _w in "qkv":
            MIX += [(_w, DT * (_h + 1)), (_w, DT * (_h + 1) + 1)]
    else:
        MIX += [("gb", _j) for _j in range(EARLY)]
    MIX += [("o", DT * _h), ("o", DT * _h + 1)]
MIX.remove(("o", DT * (HEADS - 2)))
MIX.remove(("o", DT * (HEADS - 2) + 1))
_at = MIX.index(("gb", 0))
MIX[_at:_at] = [("o", DT * (HEADS - 2)), ("o", DT * (HEADS - 2) + 1)]
for _j in range(KT):
    MIX += [("gb", _j)] * (_j >= EARLY) + [("brb", _j)]
MIX += [("out", _j) for _j in range(KT)]
NMIX = len(MIX)
FIRST_OF = {what: min(i for i, key in enumerate(MIX) if key[0] == what) for what, _ in MIX}

C_FFI1 = ADA_FIRST
C_FFO1 = C_FFI1 + len(UP1) * UP1_LOOPS
C_MIX = C_FFO1 + 3 * KT
C_FFI2 = C_MIX + NMIX
C_FFO2 = C_FFI2 + 2 * FT
C_END = C_FFO2 + 3 * KT
T_FFI1 = 0
T_FFO1 = T_FFI1 + 2 * FT
T_MIX = T_FFO1 + KT
T_FFI2 = T_MIX + NMIX
T_FFO2 = T_FFI2 + 2 * FT
T_OF = {key: T_MIX + i for i, key in enumerate(MIX)}
C_OF = {key: C_MIX + i for i, key in enumerate(MIX)}


POOL_CHUNKS = range(C_OF["xrg", 2], C_OF["ga", 0])


def head_jobs(h):
    return [
        [("kT", h, 0), ("kT", h, 1), ("Bt", h, 0)],
        [("vT", h, 0), ("vT", h, 1)],
        [("sm", h, 0), ("V", h, 0), ("V", h, 1)],
        [("S", h, c) for c in range(CH)],
        [("em", h, 0), ("den", h, 0), ("num", h, 0), ("num", h, 1)],
        [("sm", h, 1), ("V", h, 2), ("V", h, 3), ("C", h, 0), ("C", h, 1)],
    ]


AFTER = {i: [] for i in range(-1, NMIX)}
RG_AT = {}
for _j in range(0, KT, 2):
    _at = MIX.index(("xrg", _j + 1)) + 2
    RG_AT[_at] = (_j, _j + 1)
    for _jj in (_j, _j + 1):
        AFTER[_at] += [("rga", _jj, 0), ("rga", _jj, 1), ("rgi", _jj, 0), ("rgi", _jj, 1)]
ROWS_AT = {MIX.index(("bra", _j)): _n for _n, _j in enumerate((5, 7, 2, 3, 4))}
F_EXP_AT, ROW_EXP_AT = MIX.index(("bra", 6)), MIX.index(("ga", 0))
AFTER[MIX.index(("bra", 0))] += [("aT", 0, 0), ("srow", 0, 0)]
for _h in range(HEADS):
    _groups = head_jobs(_h)
    if _h + 1 < HEADS:
        _places = [MIX.index((w, DT * (_h + 1) + i)) for w in "qkv" for i in range(2)]
    else:
        _places = [MIX.index(("o", DT * _h - 2)), MIX.index(("o", DT * _h - 1))]
        _places += [MIX.index(("gb", j)) for j in range(EARLY)]
    for _p, _g in zip(_places, _groups):
        AFTER[_p] += _g

M_ADA0 = 0
ADA_GROUPS = [(g, min(4, ADA_FIRST - g)) for g in range(0, ADA_FIRST, 4)]
ADA_JOBS = [("rows", 0)]
for _g in range(1, len(ADA_GROUPS)):
    ADA_JOBS += [("rows", _g), ("back", _g - 1)]
ADA_JOBS += [("back", len(ADA_GROUPS) - 1)]
M_NORM1 = M_ADA0 + len(ADA_JOBS)
M_ADA1 = M_NORM1 + 3
M_NORM2 = M_ADA1 + UP1_LOOPS * BANKS
M_MIX = M_NORM2 + 3
JOB = {}
for _i in range(-1, NMIX):
    for _key in AFTER[_i]:
        JOB[_key] = M_MIX + len(JOB)
M_NORM3 = M_MIX + len(JOB)
M_NORM4 = M_NORM3 + 3

S_XN1 = 0
S_HID1 = S_XN1 + 1 + KT
S_XN2 = S_HID1 + FT
S_HA = S_XN2 + 1 + KT
S_HB = S_HA + KT
S_MG = S_HB + KT
S_XN3 = S_MG + KT
S_HID2 = S_XN3 + 1 + KT


def computed(m):
    return m + 1 - len(ADA_GROUPS) - len(MOD_GROUPS) * UP1_LOOPS * (m >= M_NORM2)


def sources(s):
    return s - FT * ((s >= S_XN2) + (s > S_HID2)) - KT * ((s >= S_HID1) + (s >= S_HA) + (s >= S_HID2))


def build(nc, xT, cT, w_ada, b_ada, ff1_in, ff1_out, w_mix, ff2_in, ff2_out, vecs, conv_w, w_rg,
          gate_b, st_conv, st_h, st_C, st_n, st_m,
          yT, o_convp, o_convs, o_h, o_Cp, o_Cs, o_ns, o_m):
    ctx = ExitStack()
    with ctx:
        def sb(name, shape, dt=F32, stack=ctx):
            return stack.enter_context(nc.sbuf_tensor(name, shape, dt))

        def sem(name):
            return ctx.enter_context(nc.semaphore(name))

        x = sb("x", [P, KT, T])
        xn_h = sb("xn_h", [P, KT, T], F32R)
        xn_l = sb("xn_l", [P, KT, T], F32R)
        raw = sb("raw", [P, RING, KT * P])
        w_h = [sb(f"w_h{i}", [P, KT * P], F32R) for i in range(RING)]
        w_l = [sb(f"w_l{i}", [P, KT * P], F32R) for i in range(RING)]
        cst_c = sb("cst_c", [P, 4, DT, HD])
        cs_stack = ExitStack()
        cs = sb("cs", [P, KT, NB + 1], F32, cs_stack)
        cs_hl = sb("cs_hl", [P, KT, 2 * (NB + 1)], F32R, cs_stack)
        badat = sb("badat", [P, NMOD * KT], F32, cs_stack)
        cs_stack.close()
        stc = sb("stc", [P, KT, CONV_W - 1, NB])
        sth = sb("sth", [P, KT, NB])
        rs = sb("rs", [HEADS, 3, NB])
        rsb = sb("rsb", [P, HEADS, 3, NB])
        mod = sb("mod", [P, NMOD * KT, NB + 1])
        gain = sb("gain", [P, KT, NB + 1])
        vec = sb("vec", [P, NVEC, KT])
        cw = sb("cw", [P, KT, CONV_W])
        gb_t = sb("gb_t", [P, 1])
        warm = sb("warm", [1, 1])
        rroot = sb("rroot", [P, CH + 1])
        eps_t = sb("eps_t", [P, 1])
        ident = sb("ident", [P, P])
        ones = sb("ones", [P, P])
        maskneg = sb("maskneg", [P, P])
        sel = sb("sel", [HEADS, HEADS, P])
        tb = [sb(f"tb{i}", [P, T]) for i in range(4)]
        ssq = sb("ssq", [P, T])
        ys = sb("ys", [P, KT, NB])
        tmp8 = sb("tmp8", [P, NB])
        aT = sb("aT", [P, CH, HEADS])
        stn = sb("stn", [P, HEADS, DT, NB])
        stm = sb("stm", [HEADS, NB])
        hid_stack = ExitStack()
        hid_h = sb("hid_h", [P, FT, T], F32R, hid_stack)
        hid_l = sb("hid_l", [P, FT, T], F32R, hid_stack)
        hid_stack.close()
        mix_stack = ExitStack()
        ma = sb("ma", [P, KT, T], F32, mix_stack)
        hb_h = sb("hb_h", [P, KT, T], F32R, mix_stack)
        hb_l = sb("hb_l", [P, KT, T], F32R, mix_stack)
        row_i = sb("row_i", [HEADS, T], F32, mix_stack)
        row_f = sb("row_f", [HEADS, T], F32, mix_stack)
        row_m = sb("row_m", [HEADS, T], F32, mix_stack)
        heads_stack = ExitStack()
        q_0 = sb("q_0", [P, DT, T], F32, heads_stack)
        k_0 = sb("k_0", [P, DT, T], F32, heads_stack)
        rg_stack = ExitStack()
        ma_flat = ma[:, :, :].rearrange("p k t -> p (k t)")
        n_x = CONV_W - 1 + T
        rg_u = [sb(f"rg_u{i}", [P, T], F32, rg_stack)[:, :] for i in range(2)]
        rg_u += [ma[:, i, :] for i in range(2)]
        rg_x = [sb(f"rg_x{i}", [P, n_x], F32, rg_stack)[:, :] for i in range(2)]
        rg_x += [ma_flat[:, 2 * T + i * n_x:2 * T + (i + 1) * n_x] for i in range(2)]
        rg_r, rg_i, rg_a, rg_v = ([sb(f"rg_{n}{i}", [P, T], F32, rg_stack) for i in range(2)] for n in "riav")
        wrg = sb("wrg", [P, 2, KT, P], F32, rg_stack)
        c8 = sb("c8", [P, 2, KT], F32, rg_stack)
        rg_stack.close()
        mg_stack = ExitStack()
        mg_h = sb("mg_h", [P, KT, T], F32R, mg_stack)
        mg_l = sb("mg_l", [P, KT, T], F32R, mg_stack)
        mg_stack.close()
        q_t = [q_0, sb("q_1", [P, DT, T], F32, heads_stack)]
        k_t = [k_0, sb("k_1", [P, DT, T], F32, heads_stack)]
        v_t = sb("v_t", [P, DT, T], F32, heads_stack)
        ktok = sb("ktok", [P, CH, HD], F32, heads_stack)
        vtok = sb("vtok", [P, CH, HD + 1], F32, heads_stack)
        dmat = sb("dmat", [P, CH, NP_], F32, heads_stack)
        hm = sb("hm", [P, DT, T], F32, heads_stack)
        sm = sb("sm", [P, 3, DT, NB], F32, heads_stack)
        prod = sb("prod", [P, 2, DT, NB], F32, heads_stack)
        kd = sb("kd", [P, DT, NB], F32, heads_stack)
        sres = sb("sres", [P, 4, NB], F32, heads_stack)
        s8 = sb("s8", [P, 4, NB], F32, heads_stack)
        wcol = sb("wcol", [P, CH], F32, heads_stack)
        sgb = [(q_0, k_0)[j // 2][:, j % 2, :] for j in range(EARLY)]
        heads_stack.close()
        mix_stack.close()
        n_cs, n_ho = KT * (CONV_W - 1) * NB, KT * (NB + 1)
        convs = ssq[:, 0:n_cs].rearrange("p (k j b) -> p k j b", k=KT, j=CONV_W - 1)
        hout = ssq[:, n_cs:n_cs + n_ho].rearrange("p (k n) -> p k n", k=KT)
        convp = ssq[:, n_cs + n_ho:n_cs + n_ho + KT * (CONV_W - 1)].rearrange("p (k j) -> p k j", k=KT)
        sp = ssq[:, T - 4 * KT:T].rearrange("p (a k) -> p a k", a=4)
        cst = tb[1][:, 0:DT * (HD + 1)].rearrange("p (d e) -> p d e", d=DT)

        big = [ctx.enter_context(nc.psum_tensor(f"big{i}", [P, 2, 512], F32)) for i in range(2)]
        bank = [ctx.enter_context(nc.psum_tensor(f"bank{i}", [P, 512], F32)) for i in range(BANKS)]

        def two(ap):
            return ap.rearrange("p (h n) -> p h n", h=2)

        def slot_view(t):
            return big[t % 2][:, :, 0:HALF]

        raw_in = [sem(f"raw_in{i}") for i in range(RING)]
        first_half = sem("first_half")
        w_hi_ready = sem("w_hi_ready")
        w_lo_ready = sem("w_lo_ready")
        chunk_done = sem("chunk_done")
        evac = [sem(f"evac{i}") for i in range(2)]
        job_done = sem("job_done")
        taken = [sem(f"taken{i}") for i in range(BANKS)]
        src_ready = sem("src_ready")
        hi_ready = sem("hi_ready")
        lo_ready = sem("lo_ready")
        const_ready = sem("const_ready")
        sel0 = sem("sel0")
        x_in = sem("x_in")
        small_in = sem("small_in")
        cond_in = sem("cond_in")
        mod_high = sem("mod_high")
        cs_ready = sem("cs_ready")
        sq_ready = sem("sq_ready")
        ssq_ready = sem("ssq_ready")
        x_ready = sem("x_ready")
        nrm_ready = sem("nrm_ready")
        root_ready = sem("root_ready")
        gain_ready = sem("gain_ready")
        rg_in = sem("rg_in")
        conv_done = sem("conv_done")
        rg_ra = sem("rg_ra")
        rg_w = sem("rg_w")
        rg_sq = sem("rg_sq")
        exp_sp = sem("exp_sp")
        sp_abs = sem("sp_abs")
        f_abs = sem("f_abs")
        f_exp = sem("f_exp")
        row_arg = sem("row_arg")
        row_exp = sem("row_exp")
        rows_ready = sem("rows_ready")
        diag_ready = sem("diag_ready")
        d_ready = sem("d_ready")
        prod_ready = sem("prod_ready")
        vw_ready = sem("vw_ready")
        c_in = [sem(f"c_in{i}") for i in range(4)]
        c_scaled = sem("c_scaled")
        c_out = [sem(f"c_out{i}") for i in range(4)]
        cp_out = sem("cp_out")
        state_out = sem("state_out")
        states_ready = sem("states_ready")
        y_ready = sem("y_ready")
        y_out = [sem(f"y_out{i}") for i in range(4)]
        dch = sem("dch")
        ach = sem("ach")

        block = ctx.enter_context(nc.Block())

        def wait_evac(eng, t):
            eng.wait_ge(evac[t % 2], t // 2 + 1)

        def wait_taken(eng, m):
            eng.wait_ge(taken[m % BANKS], m // BANKS + 1)

        @block.sync
        def _(sp_):
            def load(c_static, c_expr, src, width=KT * P):
                if not isinstance(c_expr, int) or c_expr >= RING:
                    sp_.wait_ge(w_lo_ready, c_expr - (RING - 1))
                sp_.dma_start(raw[:, c_static % RING, 0:width], src).then_inc(raw_in[c_static % RING], 16)

            def load_ffn(base, pattern, loops, w_i, w_o):
                n_p, n_m = pattern.count("P"), pattern.count("M")
                with sp_.Fori(0, loops) as i:
                    for k, kind in enumerate(pattern):
                        before = pattern[:k].count(kind)
                        src = w_i[i * n_p + before] if kind == "P" else w_ada[i * n_m + (ADA_FIRST + before)]
                        load(base + k, i * len(pattern) + (base + k), src)
                base += loops * len(pattern)
                for n in range(loops * n_p, 2 * FT):
                    load(base, base, w_i[n])
                    base += 1
                with sp_.Fori(0, KT) as i:
                    for k, (k0, n) in enumerate(FFO_CHUNKS):
                        load(base + k, i * 3 + (base + k), w_o[i, :, k0 * P:(k0 + n) * P], n * P)

            sp_.dma_start(cs[:, :, :], cT).then_inc(cond_in, 16)
            for c in range(ADA_FIRST):
                if c == RING:
                    sp_.dma_start(badat[:, :], b_ada).then_inc(small_in, 16)
                    sp_.dma_start(vec[:, :, :], vecs).then_inc(small_in, 16)
                load(c, c, w_ada[c])
            load_ffn(C_FFI1, UP1, UP1_LOOPS, ff1_in, ff1_out)
            with sp_.Fori(0, NMIX // RING) as i:
                for k in range(RING):
                    load(C_MIX + k, i * RING + (C_MIX + k), w_mix[i * RING + k])
            for k in range(NMIX // RING * RING, NMIX):
                load(C_MIX + k, C_MIX + k, w_mix[k])
            load_ffn(C_FFI2, UP2, UP2_LOOPS, ff2_in, ff2_out)
            for kt in range(KT):
                sp_.wait_ge(y_ready, 2 * (kt + 1))
                sp_.dma_start(yT[:, kt, :], tb[kt % 4][:, :]).then_inc(y_out[kt % 4], 16)
            for i in range(4):
                sp_.wait_ge(y_out[i], 16 * (KT // 4))

        @block.gpsimd
        def _(pool):
            nc.gpsimd.memset(ident[:, :], 0.0).then_inc(sel0, 1)
            nc.gpsimd.memset(maskneg[:, :], 0.0).then_inc(sel0, 1)
            nc.gpsimd.memset(sel[:, :, :], 0.0).then_inc(sel0, 1)
            pool.wait_ge(sel0, 3)
            nc.gpsimd.affine_select(out=ident[:, :], in_=ident[:, :], compare_op=ALU.not_equal, fill=1.0,
                                    base=0, pattern=[[-1, P]], channel_multiplier=1).then_inc(const_ready, 1)
            nc.gpsimd.affine_select(out=maskneg[:, :], in_=maskneg[:, :], compare_op=ALU.is_ge, fill=NEG,
                                    base=0, pattern=[[1, P]], channel_multiplier=-1).then_inc(const_ready, 1)
            nc.gpsimd.affine_select(out=sel[:, :, :], in_=sel[:, :, :], compare_op=ALU.not_equal, fill=1.0,
                                    base=0, pattern=[[-1, HEADS], [0, P]], channel_multiplier=1
                                    ).then_inc(const_ready, 1)
            nc.gpsimd.memset(ones[:, :], 1.0).then_inc(const_ready, 1)
            nc.gpsimd.memset(eps_t[:, :], EPS).then_inc(const_ready, 1)

            pool.dma_start(cw[:, :, :], conv_w).then_inc(rg_in, 16)
            pool.dma_start(gb_t[:, :], gate_b).then_inc(rg_in, 16)
            pool.dma_start(stn[:, :, :, :], st_n).then_inc(rg_in, 16)
            pool.dma_start(stm[:, :], st_m).then_inc(rg_in, 16)
            pool.wait_ge(chunk_done, C_MIX)
            pool.dma_start(wrg[:, :, :, :], w_rg).then_inc(rg_in, 16)
            pool.dma_start(stc[:, :, :, :], st_conv).then_inc(rg_in, 16)
            pool.dma_start(sth[:, :, :], st_h).then_inc(rg_in, 16)

            def load_state(n):
                if n >= 4:
                    pool.wait_ge(c_out[n % 4], 16 * (n // 4))
                pool.dma_start(cst_c[:, n % 4, :, :], st_C[n].rearrange("p (d e) -> p d e", d=DT)
                               ).then_inc(c_in[n % 4], 16)

            def store_state(n):
                wait_taken(pool, JOB["V", n // NB, n % NB // 2])
                pool.dma_start(o_Cs[n].rearrange("p (d e) -> p d e", d=DT), cst_c[:, n % 4, :, :]
                               ).then_inc(c_out[n % 4], 16)

            for n in range(4):
                load_state(n)
            pool.wait_ge(w_lo_ready, POOL_CHUNKS[0])
            for c in POOL_CHUNKS:
                pool.wait_ge(w_hi_ready, c + 1)
                nc.gpsimd.tensor_tensor(w_l[c % RING][:, :], raw[:, c % RING, :], w_h[c % RING][:, :],
                                        ALU.subtract).then_inc(w_lo_ready, 1)
            pool.wait_ge(lo_ready, S_HA + KT)
            pool.dma_start(o_convp, convp[:, :, :]).then_inc(state_out, 16)
            pool.dma_start(o_convs, convs[:, :, :, :]).then_inc(state_out, 16)
            pool.dma_start(o_h, hout[:, :, :]).then_inc(state_out, 16)
            for h in range(HEADS):
                for b in range(NB):
                    n = h * NB + b
                    store_state(n)
                    if n + 4 < HEADS * NB:
                        load_state(n + 4)
                for dt in range(DT):
                    wait_taken(pool, JOB["C", h, dt])
                    pool.dma_start(o_Cp[h, dt], cst[:, dt, :]).then_inc(cp_out, 16)
            pool.wait_ge(states_ready, HEADS)
            pool.dma_start(o_ns, stn[:, :, :, :]).then_inc(state_out, 16)
            pool.dma_start(o_m, row_m[:, NP_ - 1:T]).then_inc(state_out, 16)
            pool.wait_ge(state_out, 16 * 5)
            pool.wait_ge(cp_out, 16 * HEADS * DT)
            for i in range(4):
                pool.wait_ge(c_out[i], 16 * (HEADS * NB // 4))

        @block.tensor
        def _(pe):
            def product(c, c_expr, t, t_half, xh, xl, k0, n, first=True, last=True, ready=None):
                pe.wait_ge(w_lo_ready, c_expr + 1)
                if first and not (isinstance(t_half, int) and t_half == 0):
                    pe.wait_ge(evac[t % 2], t_half)
                out = big[t % 2]
                wh, wl = w_h[c % RING], w_l[c % RING]
                for i in range(n):
                    if ready is not None:
                        pe.wait_ge(lo_ready, ready(k0 + i))
                    w = slice(i * P, (i + 1) * P)
                    for s, (a, b) in enumerate(((wh, xh), (wh, xl), (wl, xh))):
                        for hf in range(2):
                            ins = nc.tensor.matmul(out[:, hf, 0:HALF], a[:, w],
                                                   b[:, k0 + i, hf * HALF:(hf + 1) * HALF],
                                                   start=first and i == 0 and s == 0,
                                                   stop=last and i == n - 1 and s == 2)
                ins.then_inc(chunk_done, 1)

            def job(m):
                if m >= BANKS:
                    pe.wait_ge(taken[m % BANKS], m // BANKS)
                return bank[m % BANKS]

            def modulation(c, c_expr, out, n):
                pe.wait_ge(w_lo_ready, c_expr + 1)
                for kt in range(KT):
                    for s, w in enumerate((w_h[c % RING], w_l[c % RING])):
                        ins = nc.tensor.matmul(out[0:NR, n * P:(n + 1) * P], cs_hl[:, kt, :],
                                               w[:, kt * P:(kt + 1) * P],
                                               start=kt == 0 and s == 0, stop=kt == KT - 1 and s == 1)
                ins.then_inc(chunk_done, 1)

            def turn_back(out, rows, n):
                for t in range(n):
                    ins = nc.tensor.transpose(out[:, t * NR:(t + 1) * NR], rows[0:NR, t * P:(t + 1) * P],
                                              ident[0:NR, 0:NR])
                ins.then_inc(job_done, 1)

            def norm_sums(index, m, ssq_count):
                pe.wait_ge(ssq_ready, ssq_count)
                b = job(m)
                for c in range(CH + 1):
                    t0 = min(c * P, T - P)
                    ins = nc.tensor.matmul(b[:, c:c + 1], ssq[:, t0:t0 + P], ones[:, 0:1], start=True, stop=True)
                ins.then_inc(job_done, 1)
                prompt, samples = job(m + 1), job(m + 2)
                pe.wait_ge(root_ready, index + 1)
                for c in range(CH):
                    ins = nc.tensor.matmul(prompt[:, c * P:(c + 1) * P], rroot[:, c:c + 1].broadcast_to([P, P]),
                                           ident[:, :], start=True, stop=True)
                ins.then_inc(job_done, 1)
                nc.tensor.matmul(samples[:, 0:NB], rroot[:, CH:CH + 1].broadcast_to([P, P]), ident[:, P - NB:P],
                                 start=True, stop=True).then_inc(job_done, 1)

            def ffn(cb, tbase, pattern, loops, s_xn, s_hid):
                def xn_split(kt):
                    return s_xn + 2 + kt

                n_p = pattern.count("P")

                def backs(i, step):
                    for g, (t0, n) in enumerate(MOD_GROUPS):
                        mr, mb = M_ADA1 + g, M_ADA1 + len(MOD_GROUPS) + g
                        if step == "wait":
                            pe.wait_ge(taken[mr % BANKS], i + mr // BANKS)
                            pe.wait_ge(taken[mb % BANKS], i + (mb // BANKS - 1))
                        else:
                            turn_back(bank[mb % BANKS], tb[2 + g], n)

                def turn(i):
                    n = a = 0
                    for k, kind in enumerate(pattern):
                        c = cb + k
                        back = k == TURN_BACK and "M" in pattern and not (isinstance(i, int) and i == 0)
                        if back:
                            backs(i, "wait")
                        if kind == "P":
                            t = tbase + n
                            product(c, i * len(pattern) + c, t, i * (n_p // 2) + t // 2, xn_h, xn_l, 0, KT,
                                    ready=xn_split if k == 0 else None)
                            n += 1
                        else:
                            g = sum(a >= t0 + size for t0, size in MOD_GROUPS)
                            m = M_ADA1 + g
                            if a == MOD_GROUPS[g][0]:
                                pe.wait_ge(taken[m % BANKS], i + m // BANKS)
                            modulation(c, i * len(pattern) + c, bank[m % BANKS], a - MOD_GROUPS[g][0])
                            a += 1
                        if back:
                            backs(i, "work")

                first = 1 if tbase == 0 else 0
                if first:
                    turn(0)
                with pe.Fori(first, loops) as i:
                    turn(i)
                cb += loops * len(pattern)
                if "M" in pattern:
                    backs(loops, "wait")
                    backs(loops, "work")
                for n in range(loops * n_p, 2 * FT):
                    product(cb, cb, tbase + n, (tbase + n) // 2, xn_h, xn_l, 0, KT)
                    cb += 1
                tbase += 2 * FT
                pe.wait_ge(lo_ready, s_hid + FT - 1)
                with pe.Fori(0, KT // 2) as i:
                    for jj in range(2):
                        for k, (k0, n) in enumerate(FFO_CHUNKS):
                            product(cb + 3 * jj + k, i * 6 + (cb + 3 * jj + k), tbase + jj,
                                    i + (tbase + jj) // 2, hid_h, hid_l, k0, n, first=k == 0, last=k == 2,
                                    ready=(lambda kt: s_hid + FT) if k == 2 and jj == 0 else None)

            pe.wait_ge(cs_ready, 3)
            pe.wait_ge(const_ready, 5)
            for m, (kind, g) in enumerate(ADA_JOBS, M_ADA0):
                first, n = ADA_GROUPS[g]
                out = job(m)
                if kind == "rows":
                    for c in range(first, first + n):
                        modulation(c, c, out, c - first)
                else:
                    wait_taken(pe, M_ADA0 + ADA_JOBS.index(("rows", g)))
                    turn_back(out, tb[g % 2], n)
            norm_sums(0, M_NORM1, KT)
            ffn(C_FFI1, T_FFI1, UP1, UP1_LOOPS, S_XN1, S_HID1)
            norm_sums(1, M_NORM2, 2 * KT)

            def small_job(key):
                kind, a, b = key
                m = JOB[key]
                out = job(m)
                h = a
                if kind in ("rga", "rgi"):
                    pe.wait_ge(rg_in, 16 * 7)
                    pe.wait_ge(conv_done, a + 1)
                    ins = nc.tensor.matmul(out[:, 0:HALF], wrg[:, 0 if kind == "rga" else 1, a, :],
                                           rg_u[a % RG_BUFS][:, b * HALF:(b + 1) * HALF], start=True, stop=True)
                elif kind == "aT":
                    pe.wait_ge(rows_ready, 1)
                    for c in range(CH):
                        ins = nc.tensor.transpose(out[:, c * HEADS:(c + 1) * HEADS],
                                                  row_i[0:HEADS, c * P:(c + 1) * P], ident[0:HEADS, 0:HEADS])
                elif kind == "srow":
                    pe.wait_ge(row_exp, 1)
                    for hh in range(HEADS):
                        ins = nc.tensor.matmul(out[:, hh * 3 * NB:(hh + 1) * 3 * NB], sel[:, hh, :],
                                               rs[:, :, :].rearrange("h a b -> h (a b)"), start=True, stop=True)
                elif kind in ("kT", "vT"):
                    src = k_t[h % 2] if kind == "kT" else v_t
                    wait_evac(pe, T_OF[kind[0], DT * h + b])
                    for c in range(CH):
                        ins = nc.tensor.transpose(out[:, c * P:(c + 1) * P], src[:, b, c * P:(c + 1) * P],
                                                  ident[:, :])
                elif kind == "Bt":
                    ins = nc.tensor.matmul(out[:, 0:NP_], sel[:, h, :], row_f[:, 0:NP_], start=True, stop=True)
                elif kind == "em":
                    ins = nc.tensor.matmul(out[:, 0:NP_], sel[:, h, :], row_m[:, 0:NP_], start=True, stop=True)
                elif kind == "S":
                    for dt in range(DT):
                        ins = nc.tensor.matmul(out[:, b * P:NP_], k_t[h % 2][:, dt, b * P:(b + 1) * P],
                                               q_t[h % 2][:, dt, b * P:NP_], start=dt == 0, stop=dt == DT - 1)
                elif kind in ("den", "num"):
                    for c in range(CH):
                        wait_taken(pe, JOB["S", h, c])
                        if kind == "num":
                            wait_taken(pe, JOB["vT", h, b])
                        lhs = ones[:, :] if kind == "den" else vtok[:, c, b * P:(b + 1) * P]
                        ins = nc.tensor.matmul(out[:, c * P:NP_], lhs, dmat[:, c, c * P:NP_],
                                               start=c == 0, stop=c == CH - 1)
                elif kind == "C":
                    pe.wait_ge(vw_ready, 5 * (h + 1))
                    for c in range(CH):
                        ins = nc.tensor.matmul(out[:, 0:HD + 1], ktok[:, c, b * P:(b + 1) * P], vtok[:, c, :],
                                               start=c == 0, stop=c == CH - 1)
                elif kind == "sm":
                    if b == 0:
                        pe.wait_ge(prod_ready, 2 * (h + 1))
                        for g in range(2):
                            for dt in range(DT):
                                nc.tensor.matmul(out[:, g * NB:(g + 1) * NB], ones[:, :], prod[:, g, dt, :],
                                                 start=dt == 0, stop=dt == DT - 1)
                    for bb in range(4):
                        n = h * NB + 4 * b + bb
                        pe.wait_ge(c_in[n % 4], 16 * (n // 4 + 1))
                        for et in range(DT):
                            col = 2 * NB + et * 4 + bb
                            for dt in range(DT):
                                ins = nc.tensor.matmul(out[:, col:col + 1],
                                                       cst_c[:, n % 4, dt, et * P:(et + 1) * P],
                                                       sm[:, 0, dt, 4 * b + bb:4 * b + bb + 1],
                                                       start=dt == 0, stop=dt == DT - 1)
                elif kind == "V":
                    pe.wait_ge(prod_ready, 2 * (h + 1))
                    for bb in range(2):
                        for et in range(DT):
                            v_col = sm[:, 2, et, 2 * b + bb:2 * b + bb + 1]
                            ins = nc.tensor.matmul(out[:, bb * HD + et * P:bb * HD + (et + 1) * P],
                                                   v_col.broadcast_to([P, P]), ident[:, :],
                                                   start=True, stop=True)
                ins.then_inc(job_done, 1)

            for i, (what, j) in enumerate(MIX):
                if what == "bra":
                    xh, xl, base = hb_h, hb_l, S_HA
                elif what == "brb":
                    xh, xl, base = hb_h, hb_l, S_HB
                elif what == "out":
                    xh, xl, base = mg_h, mg_l, S_MG
                else:
                    xh, xl, base = xn_h, xn_l, S_XN2 + 1
                t = T_MIX + i
                product(C_MIX + i, C_MIX + i, t, t // 2, xh, xl, 0, KT,
                        ready=(lambda kt: base + kt + 1)
                        if i == 0 or (i == FIRST_OF[what] and what in ("bra", "brb", "out")) else None)
                for key in AFTER[i]:
                    small_job(key)
            norm_sums(2, M_NORM3, 3 * KT)
            ffn(C_FFI2, T_FFI2, UP2, UP2_LOOPS, S_XN3, S_HID2)
            norm_sums(3, M_NORM4, 4 * KT)

        @block.scalar
        def _(act):
            A = nc.scalar.activation
            own = [0]

            def link(ins):
                own[0] += 1
                ins.then_inc(ach, 1)
                act.wait_ge(ach, own[0])

            def split(c, c_expr, need, width=KT * P, urgent=False):
                act.wait_ge(raw_in[c % RING], need)
                if not isinstance(c_expr, int) or c_expr >= RING:
                    act.wait_ge(chunk_done, c_expr - (RING - 1))
                from_ = 0
                if urgent:
                    from_ = width // 2
                    A(w_h[c % RING][:, 0:from_], raw[:, c % RING, 0:from_], ACT.Copy).then_inc(first_half, 1)
                A(w_h[c % RING][:, from_:width], raw[:, c % RING, from_:width], ACT.Copy).then_inc(w_hi_ready, 1)

            def arrivals(c):
                return 16 * (c // RING + 1)

            def high(s, out, src):
                act.wait_ge(src_ready, sources(s) + 1)
                A(out, src, ACT.Copy).then_inc(hi_ready, 1)

            def squares(n, kt):
                if not isinstance(n, int) or n >= 1:
                    act.wait_ge(ssq_ready, n)
                A(tb[2][:, :], x[:, kt, :], ACT.Square).then_inc(sq_ready, 1)

            def root(m):
                act.wait_ge(job_done, computed(m))
                A(rroot[:, :], bank[m % BANKS][:, 0:CH + 1], ACT.Sqrt, bias=eps_t[:, :],
                  scale=1.0 / D).then_inc(taken[m % BANKS], 1)

            def norm(index, m, shift, s_base):
                root(m)
                high(s_base, xn_h[:, :, NP_:T], ys[:, :, :])
                for kt in range(KT):
                    if kt < KT - 1:
                        act.wait_ge(nrm_ready, index * (KT - 1) + kt + 1)
                    else:
                        wait_taken(act, m + 1)
                    A(xn_h[:, kt, 0:NP_], tb[kt % 4][:, 0:NP_], ACT.Identity,
                      bias=mod[:, shift * KT + kt, 0:1]).then_inc(hi_ready, 1)

            def take_rows(m, c_done, out, n, turned):
                act.wait_ge(chunk_done, c_done)
                if not isinstance(turned, int) or turned > 0:
                    act.wait_ge(job_done, turned)
                A(out[0:NR, 0:n * P], bank[m % BANKS][0:NR, 0:n * P], ACT.Copy).then_inc(taken[m % BANKS], 1)

            def ffn(cb, tbase, pattern, loops, s_hid, sq_base, x_base):
                n_p = pattern.count("P")

                late = []

                def step(k, c, t, i, kind, defer):
                    after = i * len(pattern)
                    split(c + LEAD, after + (c + LEAD),
                          i * (16 * len(pattern) // RING) + arrivals(c + LEAD), urgent=k == URGENT and "M" in pattern)
                    while late:
                        high_hidden(*late.pop())
                    if kind == "P" and t % 2 == tbase % 2:
                        act.wait_ge(chunk_done, after + (c + 1))
                        A(two(tb[0][:, :]), slot_view(t), ACT.Silu).then_inc(evac[t % 2], 1)
                    elif kind == "P":
                        late.append((t, i))
                        if not defer:
                            high_hidden(*late.pop())

                def high_hidden(t, i):
                    act.wait_ge(evac[t % 2], i * (n_p // 2) + (t // 2 + 1))
                    A(hid_h[:, i * (n_p // 2) + (t - tbase) // 2, :], tb[1][:, :], ACT.Copy).then_inc(hi_ready, 1)

                with act.Fori(0, loops) as i:
                    A(warm[:, :], eps_t[0:1, :], ACT.Silu)
                    for k, kind in enumerate(pattern):
                        step(k, cb + k, tbase + pattern[:k].count("P"), i, kind, k + 1 < len(pattern))
                        for g, (t0, n) in enumerate(MOD_GROUPS):
                            if kind == "M" and pattern[:k + 1].count("M") == t0 + n:
                                take_rows(M_ADA1 + g, i * len(pattern) + (cb + k + 1), tb[2 + g], n,
                                          i * len(MOD_GROUPS) + computed(M_ADA1 - 1))
                cb += loops * len(pattern)
                for n in range(loops * n_p, 2 * FT):
                    step(None, cb, tbase + n, 0, "P", False)
                    cb += 1
                co = cb

                def turn(i):
                    for jj in range(2):
                        for k in range(3):
                            c = co + 3 * jj + k + LEAD
                            if isinstance(i, int) and i * 6 + c >= C_END:
                                continue
                            split(c, i * 6 + c, i * (16 * 6 // RING) + arrivals(c), FFO_CHUNKS[(k + LEAD) % 3][1] * P)
                        act.wait_ge(x_ready, i * 2 + (x_base + jj + 1))
                        squares(i * 2 + (sq_base + jj), i * 2 + jj)

                with act.Fori(0, KT // 2 - 1) as i:
                    turn(i)
                turn(KT // 2 - 1)

            for n in range(2):
                tiles = slice(n * KT // 2, (n + 1) * KT // 2)
                act.dma_start(x[:, tiles, :], xT[:, tiles, :]).then_inc(x_in, 16)
            act.wait_ge(cond_in, 16)
            A(cs[:, :, :], cs[:, :, :], ACT.Silu).then_inc(cs_ready, 1)
            act.wait_ge(cs_ready, 1)
            A(cs_hl[:, :, 0:NB + 1], cs[:, :, :], ACT.Copy).then_inc(cs_ready, 1)
            for c in range(ADA_FIRST + LEAD):
                split(c, c, arrivals(c))
                if c >= SQ_FROM and c < SQ_FROM + KT:
                    if c == SQ_FROM:
                        act.wait_ge(x_in, 32)
                    squares(c - SQ_FROM, c - SQ_FROM)
                for g, (first, n) in enumerate(ADA_GROUPS):
                    if first + n == c - LEAD + 1:
                        take_rows(M_ADA0 + ADA_JOBS.index(("rows", g)), first + n, tb[g % 2], n, max(0, g - 1))
            act.wait_ge(const_ready, 5)
            norm(0, M_NORM1, SH1, S_XN1)
            ffn(C_FFI1, T_FFI1, UP1, UP1_LOOPS, S_HID1, KT, 0)
            norm(1, M_NORM2, SH2, S_XN2)

            act.wait_ge(sp_abs, 1)
            A(sp[:, 1, :], sp[:, 0, :], ACT.Exp, scale=-1.0).then_inc(exp_sp, 1)

            def take(key, out, in_, func, **kw):
                m = JOB[key]
                act.wait_ge(job_done, computed(m))
                return A(out, in_, func, **kw).then_inc(taken[m % BANKS], 1)

            def rg_gates(pair):
                act.wait_ge(lo_ready, S_HA + pair[0])
                for j in pair:
                    p = j % 2
                    for dst, kind, bias in ((rg_r, "rga", V_BA), (rg_i, "rgi", V_BI)):
                        for hf in range(2):
                            key = (kind, j, hf)
                            take(key, dst[p][:, hf * HALF:(hf + 1) * HALF], bank[JOB[key] % BANKS][:, 0:HALF],
                                 ACT.Sigmoid, bias=vec[:, bias, j:j + 1])
                for j in pair:
                    p = j % 2
                    wait_taken(act, JOB["rga", j, 0])
                    wait_taken(act, JOB["rga", j, 1])
                    A(rg_a[p][:, :], rg_r[p][:, :], ACT.Exp, scale=c8[:, 0, j:j + 1]).then_inc(rg_ra, 1)
                    act.wait_ge(rg_ra, 2 * j + 1)
                    A(rg_r[p][:, :], rg_r[p][:, :], ACT.Tanh, scale=c8[:, 1, j:j + 1]).then_inc(rg_ra, 1)
                for j in pair:
                    act.wait_ge(rg_w, j + 1)
                    A(rg_v[j % 2][:, :], rg_v[j % 2][:, :], ACT.Sqrt).then_inc(rg_sq, 1)

            def small_job(key):
                kind, h, b = key
                m = JOB[key]
                src = bank[m % BANKS]
                if kind in ("rga", "rgi"):
                    if (kind, h % 2, b) == ("rgi", 1, 1):
                        rg_gates((h - 1, h))
                elif kind == "kT":
                    take(key, ktok[:, :, b * P:(b + 1) * P], src[:, :].rearrange("p (c f) -> p c f", c=CH), ACT.Copy)
                elif kind == "vT":
                    take(key, vtok[:, :, b * P:(b + 1) * P], src[:, :].rearrange("p (c f) -> p c f", c=CH), ACT.Copy)
                    if b == 1:
                        wait_taken(act, JOB["Bt", h, 0])
                        for c in range(CH - 1):
                            A(dmat[:, c, (c + 1) * P:NP_], tb[0][:, (c + 1) * P:NP_], ACT.Exp,
                              bias=aT[:, c, h:h + 1]).then_inc(d_ready, 1)
                        act.wait_ge(diag_ready, CH * (h + 1))
                        for c in range(CH):
                            A(dmat[:, c, c * P:(c + 1) * P], tb[3][:, c * P:(c + 1) * P], ACT.Exp).then_inc(d_ready, 1)
                elif kind == "em":
                    if h:
                        act.wait_ge(cp_out, 16 * DT * h)
                    take(key, tb[1][:, 0:NP_], src[:, 0:NP_], ACT.Exp, scale=-1.0)
                elif kind == "C":
                    take(key, cst[:, b, :], src[:, 0:HD + 1], ACT.Copy)
                elif kind == "sm":
                    act.wait_ge(job_done, computed(m))
                    for bb in range(4):
                        n = h * NB + 4 * b + bb
                        A(cst_c[:, n % 4, :, :], cst_c[:, n % 4, :, :], ACT.Identity,
                          scale=rsb[:, h, 1, 4 * b + bb:4 * b + bb + 1]).then_inc(c_scaled, 1)

            for i, (what, j) in enumerate(MIX):
                c = C_MIX + i + LEAD
                split(c, c, arrivals(c))
                t = T_MIX + i
                act.wait_ge(chunk_done, C_MIX + i + 1)
                src = slot_view(t)
                e = evac[t % 2]
                if what == "gates":
                    act.wait_ge(rg_in, 16 * 7)
                    A(two(row_i[:, :]), big[t % 2][0:HEADS, :, 0:HALF], ACT.Identity,
                      bias=gb_t[0:HEADS, :]).then_inc(ach, 1)
                    own[0] += 1
                    act.wait_ge(ach, own[0])
                    A(two(row_f[:, :]), big[t % 2][32:32 + HEADS, :, 0:HALF], ACT.Identity,
                      bias=gb_t[32:32 + HEADS, :]).then_inc(e, 1)
                elif what == "xrg":
                    if j >= RG_BUFS:
                        act.wait_ge(conv_done, j - RG_BUFS + 1)
                    A(two(rg_x[j % RG_BUFS][:, CONV_W - 1:]), src, ACT.Copy).then_inc(e, 1)
                elif what in "qkv":
                    h, dt = divmod(j, DT)
                    if what == "v":
                        dst = v_t
                        if h == 0:
                            act.wait_ge(lo_ready, S_HA + KT)
                            act.wait_ge(state_out, 16 * 3)
                    else:
                        dst = (q_t if what == "q" else k_t)[h % 2]
                    A(two(dst[:, dt, :]), src, ACT.Copy).then_inc(e, 1)
                elif what == "gb" and j < EARLY:
                    A(two(sgb[j]), src, ACT.Sigmoid).then_inc(e, 1)
                elif what == "ga":
                    if j < 2:
                        act.wait_ge(lo_ready, S_HA + KT)
                    elif j < 5:
                        act.wait_ge(conv_done, KT)
                    A(two(ma[:, j, :]), src, ACT.Sigmoid).then_inc(e, 1)
                elif what in ("gb", "o"):
                    if what == "o":
                        act.wait_ge(src_ready, sources(S_HB) + j)
                    else:
                        wait_evac(act, T_OF["brb", j - 1])
                    A(two(tb[0 if what != "o" else 2][:, :]), src, ACT.Sigmoid).then_inc(e, 1)
                for jj in RG_SCAN.get(i, ()):
                    high(S_HA + jj, hb_h[:, jj, :], rg_u[jj % RG_BUFS])
                if what == "o":
                    high(S_HB + j, hb_h[:, j, :], hm[:, j % DT, :])
                elif what == "brb":
                    high(S_MG + j, mg_h[:, j, :], tb[1][:, :])
                elif what == "out":
                    act.wait_ge(x_ready, KT + j + 1)
                    squares(2 * KT + j, j)
                if i == F_EXP_AT:
                    act.wait_ge(f_abs, 1)
                    A(tb[3][0:HEADS, :], tb[3][0:HEADS, :], ACT.Exp, scale=-1.0).then_inc(f_exp, 1)
                elif i == ROW_EXP_AT:
                    act.wait_ge(row_arg, 1)
                    A(rs[:, :, :], rs[:, :, :], ACT.Exp).then_inc(row_exp, 1)
                for key in AFTER[i]:
                    small_job(key)

            norm(2, M_NORM3, SH3, S_XN3)
            act.wait_ge(state_out, 16 * 5)
            ffn(C_FFI2, T_FFI2, UP2, UP2_LOOPS, S_HID2, 3 * KT, 2 * KT)
            root(M_NORM4)

        @block.vector
        def _(dve):
            V = nc.vector
            own = [0]

            def link(ins):
                own[0] += 1
                ins.then_inc(dch, 1)
                dve.wait_ge(dch, own[0])

            def split(c, c_expr, width=KT * P, urgent=None):
                from_ = 0
                if urgent is not None:
                    from_ = width // 2
                    dve.wait_ge(first_half, urgent)
                    V.tensor_tensor(w_l[c % RING][:, 0:from_], raw[:, c % RING, 0:from_],
                                    w_h[c % RING][:, 0:from_], ALU.subtract)
                dve.wait_ge(w_hi_ready, c_expr + 1)
                V.tensor_tensor(w_l[c % RING][:, from_:width], raw[:, c % RING, from_:width],
                                w_h[c % RING][:, from_:width], ALU.subtract).then_inc(w_lo_ready, 1)

            def low(s, out, src, hi):
                dve.wait_ge(hi_ready, s + 1)
                V.tensor_tensor(out, src, hi, ALU.subtract).then_inc(lo_ready, 1)

            def add_squares(n, first):
                dve.wait_ge(sq_ready, n + 1)
                if first:
                    V.tensor_copy(ssq[:, :], tb[2][:, :]).then_inc(ssq_ready, 1)
                else:
                    dve.wait_ge(ssq_ready, n)
                    V.tensor_tensor(ssq[:, :], ssq[:, :], tb[2][:, :], ALU.add).then_inc(ssq_ready, 1)

            def mod_tiles(m, done, index, tile, n):
                dve.wait_ge(job_done, done)
                out = mod[:, bass.ds(tile, n), :]
                src = bank[m % BANKS][:, 0:n * 2 * (NB + 1)].rearrange("p (t a n) -> p t a n", t=n, a=2)
                V.tensor_tensor(out, src[:, :, 0, :],
                                badat[:, bass.ds(tile, n)].unsqueeze(2).broadcast_to([P, n, NB + 1]),
                                ALU.add).then_inc(mod_high, 1)
                dve.wait_ge(mod_high, index + 1)
                V.tensor_tensor(out, out, src[:, :, 1, :], ALU.add).then_inc(taken[m % BANKS], 1)

            def set_gain(index, scale, g, last_job):
                if last_job is not None:
                    for m in range(last_job - BANKS, last_job):
                        wait_taken(dve, m)
                V.scalar_tensor_tensor(gain[:, :, :], mod[:, scale * KT:(scale + 1) * KT, :], 1.0,
                                       vec[:, g, :].unsqueeze(2).broadcast_to([P, KT, NB + 1]),
                                       ALU.add, ALU.mult).then_inc(gain_ready, 1)
                dve.wait_ge(gain_ready, index + 1)

            def inverse_root(m):
                wait_taken(dve, m)
                V.reciprocal(rroot[:, :], rroot[:, :]).then_inc(root_ready, 1)
                return bank[(m + 1) % BANKS][:, 0:NP_], bank[(m + 2) % BANKS][:, 0:NB]

            def norm(index, m, shift, s_base):
                rstd_p, rstd_s = inverse_root(m)
                dve.wait_ge(job_done, computed(m + 1))

                def prompt(kt):
                    if kt >= 4:
                        dve.wait_ge(lo_ready, s_base + kt - 2)
                    ins = V.scalar_tensor_tensor(tb[kt % 4][:, 0:NP_], x[:, kt, 0:NP_], gain[:, kt, 0:1], rstd_p,
                                                 ALU.mult, ALU.mult)
                    if kt < KT - 1:
                        ins.then_inc(nrm_ready, 1)
                    else:
                        ins.then_inc(taken[(m + 1) % BANKS], 1)

                prompt(0)
                dve.wait_ge(job_done, computed(m + 2))
                V.tensor_tensor(ys[:, :, :], x[:, :, NP_:T], rstd_s.unsqueeze(1).broadcast_to([P, KT, NB]),
                                ALU.mult).then_inc(taken[(m + 2) % BANKS], 1)
                wait_taken(dve, m + 2)
                link(V.tensor_tensor(ys[:, :, :], ys[:, :, :], gain[:, :, 1:], ALU.mult))
                V.tensor_tensor(ys[:, :, :], ys[:, :, :], mod[:, shift * KT:(shift + 1) * KT, 1:],
                                ALU.add).then_inc(src_ready, 1)
                prompt(1)
                low(s_base, xn_l[:, :, NP_:T], ys[:, :, :], xn_h[:, :, NP_:T])
                for kt in range(KT):
                    dve.wait_ge(hi_ready, s_base + 1 + kt + 1)
                    V.scalar_tensor_tensor(xn_l[:, kt, 0:NP_], tb[kt % 4][:, 0:NP_],
                                           mod[:, shift * KT + kt, 0:1], xn_h[:, kt, 0:NP_],
                                           ALU.add, ALU.subtract).then_inc(lo_ready, 1)
                    if kt + 2 < KT:
                        prompt(kt + 2)

            def add_gated(t, kt, gate, ready_count):
                big_t = big[t % 2]
                V.scalar_tensor_tensor(x[:, kt, 0:HALF], big_t[:, 0, 0:HALF], mod[:, gate, 0:1],
                                       x[:, kt, 0:HALF], ALU.mult, ALU.add)
                V.scalar_tensor_tensor(x[:, kt, HALF:NP_], big_t[:, 1, 0:NP_ - HALF], mod[:, gate, 0:1],
                                       x[:, kt, HALF:NP_], ALU.mult, ALU.add)
                V.tensor_tensor(tmp8[:, :], big_t[:, 1, NP_ - HALF:HALF], mod[:, gate, 1:],
                                ALU.mult).then_inc(evac[t % 2], 1)
                dve.wait_ge(evac[t % 2], ready_count)
                V.tensor_tensor(x[:, kt, NP_:T], x[:, kt, NP_:T], tmp8[:, :], ALU.add).then_inc(x_ready, 1)

            def ffn(cb, tbase, pattern, loops, s_hid, gate, sq_base):
                n_p = pattern.count("P")

                late = []

                def step(k, c, t, i, kind, defer):
                    after, third = i * len(pattern), i * (n_p // 2)
                    split(c + LEAD, after + (c + LEAD), urgent=i + 1 if k == URGENT and "M" in pattern else None)
                    while late:
                        low_hidden(*late.pop())
                    if kind == "P" and t % 2 != tbase % 2:
                        j = (t - tbase) // 2
                        dve.wait_ge(chunk_done, after + (c + 1))
                        dve.wait_ge(evac[(t - 1) % 2], third + ((t - 1) // 2 + 1))
                        dve.wait_ge(lo_ready, third + (s_hid + j))
                        V.tensor_tensor(two(tb[1][:, :]), two(tb[0][:, :]), slot_view(t),
                                        ALU.mult).then_inc(evac[t % 2], 1)
                        late.append((j, third))
                        if not defer:
                            low_hidden(*late.pop())

                def mods(i):
                    per = len(MOD_GROUPS)
                    for g, (t0, n) in enumerate(MOD_GROUPS):
                        mod_tiles(M_ADA1 + per + g, i * per + (computed(M_ADA1 - 1) - per + g + 1),
                                  i * per + (len(ADA_GROUPS) - per + g),
                                  i * pattern.count("M") + (ADA_FIRST - pattern.count("M") + t0), n)

                def low_hidden(j, third):
                    low(third + (s_hid + j), hid_l[:, third + j, :], tb[1][:, :], hid_h[:, third + j, :])

                def turn(i):
                    for k, kind in enumerate(pattern):
                        step(k, cb + k, tbase + pattern[:k].count("P"), i, kind, k + 1 < len(pattern))
                        if k == TURN_BACK + 1 and "M" in pattern and not (isinstance(i, int) and i == 0):
                            mods(i)

                first = 1 if tbase == 0 else 0
                if first:
                    turn(0)
                with dve.Fori(first, loops) as i:
                    turn(i)
                if "M" in pattern:
                    mods(loops)
                cb += loops * len(pattern)
                for n in range(loops * n_p, 2 * FT):
                    step(None, cb, tbase + n, 0, "P", False)
                    cb += 1
                co = cb
                to = tbase + 2 * FT
                if tbase == T_FFI1:
                    for m in range(M_NORM2 - BANKS, M_NORM2):
                        wait_taken(dve, m)
                link(V.tensor_scalar(mod[:, gate:gate + KT, :], mod[:, gate:gate + KT, :], 0.5, None, ALU.mult))
                link(V.memset(ssq[:, :], 0.0))

                def turn(i):
                    for jj in range(2):
                        for k in range(3):
                            c = co + 3 * jj + k + LEAD
                            if isinstance(i, int) and i * 6 + c >= C_END:
                                continue
                            split(c, i * 6 + c, FFO_CHUNKS[(k + LEAD) % 3][1] * P)
                        dve.wait_ge(chunk_done, i * 6 + (co + 3 * jj + 3))
                        add_gated(to + jj, i * 2 + jj, i * 2 + (jj + gate), i + ((to + jj) // 2 + 1))
                        add_squares(i * 2 + (sq_base + jj), False)

                with dve.Fori(0, KT // 2 - 1) as i:
                    turn(i)
                turn(KT // 2 - 1)

            def log1p_times2z(z, z2, p):
                link(V.tensor_tensor(z2, z, z, ALU.mult))
                link(V.tensor_scalar(p, z2, 1.0 / 19, None, ALU.mult))
                for n in range(17, 1, -2):
                    link(V.scalar_tensor_tensor(p, p, 1.0 / n, z2, ALU.add, ALU.mult))
                link(V.scalar_tensor_tensor(p, p, 1.0, z, ALU.add, ALU.mult))
                link(V.tensor_scalar(p, p, 2.0, None, ALU.mult))

            def first_mods(g):
                if g == 0:
                    dve.wait_ge(small_in, 16 * 2)
                mod_tiles(M_ADA0 + ADA_JOBS.index(("back", g)), g + 1, g, *ADA_GROUPS[g])

            dve.wait_ge(cs_ready, 2)
            V.tensor_tensor(cs_hl[:, :, NB + 1:], cs[:, :, :], cs_hl[:, :, 0:NB + 1],
                            ALU.subtract).then_inc(cs_ready, 1)
            for c in range(ADA_FIRST + LEAD):
                split(c, c)
                if c >= SQ_FROM and c < SQ_FROM + KT:
                    add_squares(c - SQ_FROM, c == SQ_FROM)
                for g, (first, n) in enumerate(ADA_GROUPS):
                    if g + 1 < len(ADA_GROUPS) and sum(ADA_GROUPS[g + 1]) == c - LEAD + 1:
                        first_mods(g)
            first_mods(len(ADA_GROUPS) - 1)
            set_gain(0, SC1, V_G1, M_NORM1)
            norm(0, M_NORM1, SH1, S_XN1)
            ffn(C_FFI1, T_FFI1, UP1, UP1_LOOPS, S_HID1, GA1 * KT, KT)
            set_gain(1, SC2, V_G2, None)
            norm(1, M_NORM2, SH2, S_XN2)

            lam = vec[:, V_LAM, :]
            V.scalar_tensor_tensor(sp[:, 0, :], lam, -1.0, lam, ALU.mult, ALU.max).then_inc(sp_abs, 1)
            for xr in rg_x:
                V.memset(xr[:, 0:CONV_W - 1], 0.0)
            dve.wait_ge(exp_sp, 1)
            link(V.tensor_scalar(sp[:, 2, :], sp[:, 1, :], 2.0, None, ALU.add))
            link(V.reciprocal(sp[:, 2, :], sp[:, 2, :]))
            link(V.tensor_tensor(sp[:, 2, :], sp[:, 2, :], sp[:, 1, :], ALU.mult))
            log1p_times2z(sp[:, 2, :], sp[:, 3, :], sp[:, 1, :])
            link(V.tensor_scalar(sp[:, 0, :], lam, -1.0, 0.0, ALU.mult, ALU.max))
            link(V.tensor_tensor(sp[:, 0, :], sp[:, 0, :], sp[:, 1, :], ALU.add))
            link(V.tensor_scalar(c8[:, 0, :], sp[:, 0, :], -8.0, None, ALU.mult))
            link(V.tensor_scalar(c8[:, 1, :], sp[:, 0, :], 8.0, None, ALU.mult))

            def conv(j):
                xr, u = rg_x[j % RG_BUFS], rg_u[j % RG_BUFS]
                wait_evac(dve, T_OF["xrg", j])
                if j == 0:
                    dve.wait_ge(rg_in, 16 * 7)
                if j >= RG_BUFS:
                    dve.wait_ge(lo_ready, S_HA + j - RG_BUFS + 1)
                NC = CONV_W - 1
                for w in range(CONV_W):
                    tap = cw[:, j, w:w + 1]
                    new = xr[:, NC + NP_:NC + T] if w == NC else stc[:, j, w, :]
                    if w == 0:
                        V.tensor_scalar(u[:, 0:NP_], xr[:, 0:NP_], tap, vec[:, V_CB, j:j + 1], ALU.mult, ALU.add)
                        link(V.tensor_scalar(u[:, NP_:T], new, tap, vec[:, V_CB, j:j + 1], ALU.mult, ALU.add))
                    else:
                        V.scalar_tensor_tensor(u[:, 0:NP_], xr[:, w:w + NP_], tap, u[:, 0:NP_], ALU.mult, ALU.add)
                        link(V.scalar_tensor_tensor(u[:, NP_:T], new, tap, u[:, NP_:T], ALU.mult, ALU.add))
                V.tensor_copy(convp[:, j, :], xr[:, NP_:NP_ + NC])
                V.tensor_copy(convs[:, j, 0:NC - 1, :], stc[:, j, 1:NC, :])
                V.tensor_copy(convs[:, j, NC - 1, :], xr[:, NC + NP_:NC + T]).then_inc(conv_done, 1)

            def rg_weight(j):
                p = j % 2
                a, v, th = rg_a[p], rg_v[p], rg_r[p]
                for hf in range(2):
                    wait_taken(dve, JOB["rgi", j, hf])
                link(V.tensor_tensor(rg_i[p][:, :], rg_i[p][:, :], rg_u[j % RG_BUFS], ALU.mult))
                dve.wait_ge(rg_ra, 2 * j + 2)
                link(V.tensor_tensor(v[:, :], a[:, :], a[:, :], ALU.mult))
                V.scalar_tensor_tensor(v[:, :], v[:, :], 1.0, th[:, :], ALU.add, ALU.mult).then_inc(rg_w, 1)

            def rg_scan(j):
                p = j % 2
                a, v, u, ig = rg_a[p], rg_v[p], rg_u[j % RG_BUFS], rg_i[p]
                dve.wait_ge(rg_sq, j + 1)
                link(V.tensor_tensor(ig[:, :], ig[:, :], v[:, :], ALU.mult))
                V.tensor_tensor_scan(u[:, 0:NP_], a[:, 0:NP_], ig[:, 0:NP_], 0.0, ALU.mult, ALU.add)
                link(V.tensor_tensor(u[:, NP_:T], a[:, NP_:T], sth[:, j, :], ALU.mult))
                link(V.tensor_tensor(u[:, NP_:T], u[:, NP_:T], ig[:, NP_:T], ALU.add))
                V.tensor_copy(hout[:, j, :], u[:, NP_ - 1:T]).then_inc(src_ready, 1)

            def rg_low(j):
                low(S_HA + j, hb_l[:, j, :], rg_u[j % RG_BUFS], hb_h[:, j, :])

            def gate_rows(stage):
                f, ig, m = row_f[:, :], row_i[:, :], row_m[:, :]
                t1, t2, t3 = (t[0:HEADS, :] for t in tb[1:])
                s = slice(NP_, T)
                if stage == 0:
                    wait_evac(dve, T_OF["gates", 0])
                    V.scalar_tensor_tensor(t3, f, -1.0, f, ALU.mult, ALU.max).then_inc(f_abs, 1)
                elif stage == 1:
                    dve.wait_ge(f_exp, 1)
                    link(V.tensor_scalar(t1, t3, 2.0, None, ALU.add))
                    link(V.reciprocal(t1, t1))
                    link(V.tensor_tensor(t1, t1, t3, ALU.mult))
                elif stage == 2:
                    log1p_times2z(t1, t2, t3)
                elif stage == 3:
                    link(V.scalar_tensor_tensor(f, f, 0.0, t3, ALU.min, ALU.subtract))
                    link(V.tensor_tensor_scan(m[:, 0:NP_], f[:, 0:NP_], ig[:, 0:NP_], 0.0, ALU.add, ALU.max))
                    link(V.memset(t2[:, 0:NP_], 0.0))
                    link(V.tensor_tensor_scan(t1[:, 0:NP_], f[:, 0:NP_], t2[:, 0:NP_], 0.0, ALU.add, ALU.add))
                    link(V.tensor_tensor(t1[:, s], f[:, s], stm[:, :], ALU.add))
                    link(V.tensor_tensor(m[:, s], t1[:, s], ig[:, s], ALU.max))
                    link(V.tensor_tensor(rs[:, 0, :], ig[:, s], m[:, s], ALU.subtract))
                    link(V.tensor_tensor(rs[:, 1, :], t1[:, s], m[:, s], ALU.subtract))
                    V.tensor_scalar(rs[:, 2, :], m[:, s], -1.0, None, ALU.mult).then_inc(row_arg, 1)
                else:
                    link(V.tensor_tensor(f[:, 0:NP_], t1[:, 0:NP_], m[:, 0:NP_], ALU.subtract))
                    V.tensor_tensor(ig[:, 0:NP_], ig[:, 0:NP_], t1[:, 0:NP_], ALU.subtract).then_inc(rows_ready, 1)

            def sample_products(h):
                p = h % 2
                if h:
                    wait_taken(dve, JOB["V", h - 1, 3])
                for n, src, w in ((0, q_t[p], "q"), (1, k_t[p], "k"), (2, v_t, "v")):
                    for dt in range(DT):
                        wait_evac(dve, T_OF[w, DT * h + dt])
                    link(V.tensor_copy(sm[:, n, :, :], src[:, :, NP_:T]))
                V.tensor_tensor(prod[:, 0, :, :], sm[:, 0, :, :], sm[:, 1, :, :], ALU.mult).then_inc(prod_ready, 1)
                V.tensor_tensor(prod[:, 1, :, :], sm[:, 0, :, :], stn[:, h, :, :], ALU.mult).then_inc(prod_ready, 1)
                dve.wait_ge(prod_ready, 2 * (h + 1))
                link(V.tensor_tensor(kd[:, :, :], sm[:, 1, :, :],
                                     rsb[:, h, 0, :].unsqueeze(1).broadcast_to([P, DT, NB]), ALU.mult))
                link(V.tensor_tensor(stn[:, h, :, :], stn[:, h, :, :],
                                     rsb[:, h, 1, :].unsqueeze(1).broadcast_to([P, DT, NB]), ALU.mult))
                V.tensor_tensor(stn[:, h, :, :], stn[:, h, :, :], kd[:, :, :], ALU.add).then_inc(states_ready, 1)

            def sample_outputs(h):
                wi, wp, em = (rsb[:, h, n, :] for n in range(3))
                s, den = s8[:, 0, :], s8[:, 1, :]
                link(V.scalar_tensor_tensor(s, sres[:, 0, :], QSCALE, wi, ALU.mult, ALU.mult))
                link(V.scalar_tensor_tensor(den, sres[:, 1, :], QSCALE, wp, ALU.mult, ALU.mult))
                link(V.tensor_tensor(den, den, s, ALU.add))
                link(V.scalar_tensor_tensor(s8[:, 2, :], den, -1.0, em, ALU.mult, ALU.max))
                link(V.tensor_tensor(den, den, s8[:, 2, :], ALU.max))
                link(V.reciprocal(den, den))
                for et in range(DT):
                    num, sv = sres[:, 2 + et, :], s8[:, 2 + et, :]
                    link(V.scalar_tensor_tensor(num, num, QSCALE, wp, ALU.mult, ALU.mult))
                    link(V.tensor_tensor(sv, s, sm[:, 2, et, :], ALU.mult))
                    link(V.tensor_tensor(num, num, sv, ALU.add))
                    link(V.tensor_tensor(hm[:, et, NP_:T], num, den, ALU.mult))

            def small_job(key):
                kind, h, b = key
                m = JOB[key]
                src = bank[m % BANKS]

                def done():
                    dve.wait_ge(job_done, computed(m))

                free = taken[m % BANKS]
                if kind == "aT":
                    done()
                    V.tensor_copy(aT[:, :, :], src[:, 0:CH * HEADS].rearrange("p (c h) -> p c h", c=CH)
                                  ).then_inc(free, 1)
                elif kind == "srow":
                    done()
                    V.tensor_copy(rsb[:, :, :, :], src[:, 0:HEADS * 3 * NB].rearrange("p (h a b) -> p h a b", h=HEADS, a=3)
                                  ).then_inc(free, 1)
                elif kind == "Bt":
                    if h:
                        dve.wait_ge(d_ready, (2 * CH - 1) * h)
                        wait_taken(dve, JOB["num", h - 1, 1])
                    done()
                    V.tensor_copy(tb[0][:, 0:NP_], src[:, 0:NP_]).then_inc(free, 1)
                    wait_taken(dve, m)
                    for c in range(CH):
                        cc = slice(c * P, (c + 1) * P)
                        V.scalar_tensor_tensor(tb[3][:, cc], tb[0][:, cc], aT[:, c, h:h + 1], maskneg[:, :],
                                               ALU.add, ALU.add).then_inc(diag_ready, 1)
                elif kind == "vT" and b == 1:
                    sample_products(h)
                elif kind == "S":
                    if b == 0:
                        dve.wait_ge(d_ready, (2 * CH - 1) * (h + 1))
                        if h:
                            dve.wait_ge(vw_ready, 5 * h)
                        link(V.tensor_copy(wcol[:, :], dmat[:, :, NP_ - 1]))
                    done()
                    V.scalar_tensor_tensor(dmat[:, b, b * P:NP_], src[:, b * P:NP_], QSCALE, dmat[:, b, b * P:NP_],
                                           ALU.mult, ALU.mult).then_inc(free, 1)
                elif kind == "den":
                    done()
                    wait_taken(dve, JOB["em", h, 0])
                    link(V.scalar_tensor_tensor(tb[3][:, 0:NP_], src[:, 0:NP_], -1.0, tb[1][:, 0:NP_], ALU.mult, ALU.max))
                    V.tensor_tensor(tb[3][:, 0:NP_], src[:, 0:NP_], tb[3][:, 0:NP_], ALU.max).then_inc(free, 1)
                    wait_taken(dve, m)
                    link(V.reciprocal(tb[3][:, 0:NP_], tb[3][:, 0:NP_]))
                elif kind == "num":
                    if h:
                        dve.wait_ge(lo_ready, S_HB + DT * h)
                    done()
                    V.tensor_tensor(hm[:, b, 0:NP_], src[:, 0:NP_], tb[3][:, 0:NP_], ALU.mult).then_inc(free, 1)
                    wait_taken(dve, m)
                    if b == 1:
                        for c in range(CH):
                            V.tensor_scalar(vtok[:, c, 0:HD], vtok[:, c, 0:HD], wcol[:, c:c + 1], None,
                                            ALU.mult).then_inc(vw_ready, 1)
                        V.tensor_copy(vtok[:, :, HD], wcol[:, :]).then_inc(vw_ready, 1)
                elif kind == "sm":
                    done()
                    if b == 0:
                        V.tensor_copy(sres[:, 0:2, :], src[:, 0:2 * NB].rearrange("p (g b) -> p g b", g=2))
                    V.tensor_copy(sres[:, 2:4, 4 * b:4 * b + 4],
                                  src[:, 2 * NB:2 * NB + 2 * 4].rearrange("p (e b) -> p e b", e=DT)).then_inc(free, 1)
                    wait_taken(dve, m)
                    if b == 1:
                        sample_outputs(h)
                elif kind == "V":
                    done()
                    for bb in range(2):
                        n = h * NB + 2 * b + bb
                        dve.wait_ge(c_scaled, n + 1)
                        for dt in range(DT):
                            ins = V.scalar_tensor_tensor(cst_c[:, n % 4, dt, :], src[:, bb * HD:(bb + 1) * HD],
                                                         kd[:, dt, 2 * b + bb:2 * b + bb + 1],
                                                         cst_c[:, n % 4, dt, :], ALU.mult, ALU.add)
                    ins.then_inc(free, 1)

            for i, (what, j) in enumerate(MIX):
                c = C_MIX + i + LEAD
                if c == POOL_CHUNKS[-1] + 1:
                    dve.wait_ge(w_lo_ready, c)
                if c not in POOL_CHUNKS:
                    split(c, c)
                t = T_MIX + i
                for jj in RG_SCAN.get(i, ()):
                    rg_scan(jj)
                    rg_low(jj)
                if what == "xrg":
                    conv(j)
                elif what == "bra":
                    dve.wait_ge(chunk_done, C_MIX + i + 1)
                    wait_evac(dve, T_OF["ga", j])
                    V.tensor_tensor(two(ma[:, j, :]), two(ma[:, j, :]), slot_view(t), ALU.mult).then_inc(evac[t % 2], 1)
                elif what == "brb":
                    dve.wait_ge(chunk_done, C_MIX + i + 1)
                    wait_evac(dve, T_OF["gb", j])
                    if j:
                        dve.wait_ge(lo_ready, S_MG + j)
                    else:
                        dve.wait_ge(cp_out, 16 * DT * HEADS)
                    gate = sgb[j] if j < EARLY else tb[0][:, :]
                    V.tensor_tensor(two(tb[1][:, :]), two(gate), slot_view(t), ALU.mult).then_inc(evac[t % 2], 1)
                    wait_evac(dve, t)
                    V.tensor_tensor(tb[1][:, :], tb[1][:, :], ma[:, j, :], ALU.add).then_inc(src_ready, 1)
                    low(S_MG + j, mg_l[:, j, :], tb[1][:, :], mg_h[:, j, :])
                elif what == "o":
                    wait_evac(dve, t)
                    V.tensor_tensor(hm[:, j % DT, :], hm[:, j % DT, :], tb[2][:, :], ALU.mult).then_inc(src_ready, 1)
                    low(S_HB + j, hb_l[:, j, :], hm[:, j % DT, :], hb_h[:, j, :])
                elif what == "out":
                    dve.wait_ge(chunk_done, C_MIX + i + 1)
                    add_gated(t, j, GA2 * KT + j, t // 2 + 1)
                    add_squares(2 * KT + j, j == 0)
                if i in ROWS_AT:
                    gate_rows(ROWS_AT[i])
                for key in AFTER[i]:
                    small_job(key)
                for jj in RG_AT.get(i, ()):
                    rg_weight(jj)

            set_gain(2, SC3, V_G3, None)
            norm(2, M_NORM3, SH3, S_XN3)
            dve.wait_ge(state_out, 16 * 5)
            ffn(C_FFI2, T_FFI2, UP2, UP2_LOOPS, S_HID2, GA3 * KT, 3 * KT)
            rstd_p, rstd_s = inverse_root(M_NORM4)
            dve.wait_ge(job_done, computed(M_NORM4 + 2))
            for kt in range(KT):
                if kt >= 4:
                    dve.wait_ge(y_out[kt % 4], 16 * (kt // 4))
                for cols, rstd in ((slice(0, NP_), rstd_p), (slice(NP_, T), rstd_s)):
                    V.scalar_tensor_tensor(tb[kt % 4][:, cols], x[:, kt, cols], vec[:, V_GF, kt:kt + 1], rstd,
                                           ALU.mult, ALU.mult).then_inc(y_ready, 1)


RG_SCAN = {at + 1 + n: (pair[n],) for at, pair in RG_AT.items() for n in range(2)}


def _tiles(w):
    w = np.asarray(w)
    k, n = w.shape
    return np.ascontiguousarray(w.reshape(k // P, P, n // P, P).transpose(2, 1, 0, 3)).reshape(n // P, P, k)


def _features(a):
    a = np.asarray(a)
    lead = a.shape[:-1]
    a = a.reshape(lead + (KT, P))
    return np.ascontiguousarray(np.moveaxis(np.moveaxis(a, -1, 0), -1, 1))


def kernel(**inputs):
    import concourse.bacc as bacc
    from concourse.bass_utils import run_bass_kernel_spmd

    g = {k: np.asarray(v) for k, v in inputs.items()}
    f32 = np.float32
    x_all = np.concatenate([g["x_prompt"][0], g["x_sample"][:, 0]], 0)
    c_all = np.concatenate([g["c_prompt"], g["c_sample"]], 0)
    w_in = g["w_in"][0]
    q0, k0, v0, o0 = (D * n for n in (1, 2, 3, 4))
    i0 = 5 * D
    f0 = i0 + HEADS
    a0 = f0 + HEADS
    b0 = a0 + D
    gates = np.zeros((D, P), f32)
    gates[:, 0:HEADS] = w_in[:, i0:i0 + HEADS]
    gates[:, 32:32 + HEADS] = w_in[:, f0:f0 + HEADS]
    sources = {
        "gates": gates, "xrg": w_in[:, 0:D], "q": w_in[:, q0:q0 + D], "k": w_in[:, k0:k0 + D],
        "v": w_in[:, v0:v0 + D], "o": w_in[:, o0:o0 + D], "ga": w_in[:, a0:a0 + D], "gb": w_in[:, b0:b0 + D],
        "bra": g["w_br_a"][0], "brb": g["w_br_b"][0], "out": g["w_out"][0],
    }
    tiled = {k: _tiles(w) for k, w in sources.items()}
    w_mix = np.stack([tiled[what][j] for what, j in MIX])

    def up(w):
        t = _tiles(w)
        return np.ascontiguousarray(np.stack([t[:FT], t[FT:]], 1)).reshape(2 * FT, P, D)

    gate_b = np.zeros((P, 1), f32)
    gate_b[0:HEADS, 0] = g["b_ig"][0]
    gate_b[32:32 + HEADS, 0] = g["b_fg"][0]
    vecs = np.stack([g["g_norm1"][0], g["g_norm2"][0], g["g_norm3"][0], g["g_final"], g["conv_b"][0],
                     g["b_rg_a"][0], g["b_rg_i"][0], g["rg_lambda"][0]])
    arrays = {
        "xT": _features(x_all),
        "cT": _features(c_all),
        "w_ada": _tiles(g["w_ada"][0]),
        "b_ada": np.ascontiguousarray(g["b_ada"][0].reshape(NMOD * KT, P).T),
        "ff1_in": up(g["w_ff1_in"][0]),
        "ff1_out": _tiles(g["w_ff1_out"][0]),
        "w_mix": w_mix,
        "ff2_in": up(g["w_ff2_in"][0]),
        "ff2_out": _tiles(g["w_ff2_out"][0]),
        "vecs": np.ascontiguousarray(_features(vecs).transpose(0, 2, 1)),
        "conv_w": _features(g["conv_w"][0]),
        "w_rg": np.ascontiguousarray(np.stack([g["w_rg_a"][0], g["w_rg_i"][0]]).transpose(2, 0, 1, 3)),
        "gate_b": gate_b,
        "st_conv": np.ascontiguousarray(_features(g["state_conv"][0]).transpose(0, 1, 3, 2)),
        "st_h": _features(g["state_rg_h"][0]),
        "st_C": np.ascontiguousarray(
            g["state_C"][0].reshape(NB, HEADS, DT, P, HD).transpose(1, 0, 3, 2, 4)).reshape(HEADS * NB, P, DT * HD),
        "st_n": np.ascontiguousarray(g["state_n"][0].reshape(NB, HEADS, DT, P).transpose(3, 1, 2, 0)),
        "st_m": np.ascontiguousarray(g["state_m"][0].T),
    }
    outs = {
        "yT": (P, KT, T), "o_convp": (P, KT, CONV_W - 1), "o_convs": (P, KT, CONV_W - 1, NB),
        "o_h": (P, KT, NB + 1), "o_Cp": (HEADS, DT, P, HD + 1), "o_Cs": (HEADS * NB, P, DT * HD),
        "o_ns": (P, HEADS, DT, NB), "o_m": (HEADS, NB + 1),
    }
    nc = bacc.Bacc("TRN2", target_bir_lowering=False, num_devices=1)
    args = [nc.dram_tensor(n, a.shape, F32, kind="ExternalInput").ap() for n, a in arrays.items()]
    args += [nc.dram_tensor(n, s, F32, kind="ExternalOutput").ap() for n, s in outs.items()]
    build(nc, *args)
    r = run_bass_kernel_spmd(nc, [arrays], core_ids=[0]).results[0]

    def tokens(a):
        return np.ascontiguousarray(a.transpose(2, 1, 0)).reshape(a.shape[2], D)

    y = tokens(r["yT"])
    y_p, y_s = y[None, :NP_], y[NP_:, None]
    conv_p = tokens(r["o_convp"])[None, None]
    conv_s = np.ascontiguousarray(r["o_convs"].transpose(3, 2, 1, 0)).reshape(1, NB, CONV_W - 1, D)
    hh = tokens(r["o_h"])
    h_p, h_s = hh[None, 0:1], hh[None, 1:]
    cp = r["o_Cp"].reshape(HEADS, HD, HD + 1)
    C_p = np.ascontiguousarray(cp[None, None, :, :, :HD])
    n_p = np.ascontiguousarray(cp[None, None, :, :, HD])
    C_s = np.ascontiguousarray(
        r["o_Cs"].reshape(HEADS, NB, P, DT, HD).transpose(1, 0, 3, 2, 4)).reshape(1, NB, HEADS, HD, HD)
    n_s = np.ascontiguousarray(r["o_ns"].transpose(3, 1, 2, 0)).reshape(1, NB, HEADS, HD)
    m_p = np.ascontiguousarray(r["o_m"][:, 0])[None, None]
    m_s = np.ascontiguousarray(r["o_m"][:, 1:].T)[None]
    return tuple(np.ascontiguousarray(a) for a in
                 (y_p, y_s, conv_p, h_p, C_p, n_p, m_p, conv_s, h_s, C_s, n_s, m_s))
```
